# Optimizing a Trainium2 kernel written in Bass

```python
import math
import jax, jax.numpy as jnp
from jax import lax
import numpy as np

D_MODEL = 1024
BATCH = 1
SEQ = 256
DEPTH = 1
DEC_BATCH = 8
DEC_SEQ = 1
PAST_LEN = 2048
PAGE_SIZE = 128

POOL_WIDTH = D_MODEL // 2
POOL_GROUPS = 4
POOL_GROUP_DIM = POOL_WIDTH // POOL_GROUPS
POOL_WINDOWS = (2, 4, 8, 16)
POOL_HIST = max(POOL_WINDOWS) - 1
MLSTM_WIDTH = D_MODEL - POOL_WIDTH
MLSTM_HEADS = 4
HEAD_DIM = MLSTM_WIDTH // MLSTM_HEADS
CHUNK = 128
MIX_WIDTH = POOL_WIDTH + MLSTM_WIDTH
IN_COLS = POOL_WIDTH + 4 * MLSTM_WIDTH + 2 * MLSTM_HEADS
N_EXPERTS = 32
TOP_K = 4
D_FF = D_MODEL
SWIGLU_ALPHA = 1.702
SWIGLU_LIMIT = 7.0
MOE_BLOCK = 128
PLE_DIM = 256
DN_ALPHA = (2 * DEPTH) ** 0.25
DN_BETA = (8 * DEPTH) ** -0.25
LN_EPS = 1e-5
F32 = jnp.float32

kernel_name = 'hybrid_pool_mlstm_moe_deepnorm_step'

def layer_norm(x, g, b):
    xf = x.astype(F32)
    mu = jnp.mean(xf, -1, keepdims=True)
    var = jnp.mean(jnp.square(xf - mu), -1, keepdims=True)
    return ((xf - mu) * lax.rsqrt(var + LN_EPS) * g.astype(F32) + b.astype(F32)).astype(x.dtype)

def head_norm(h, g):
    mu = jnp.mean(h, -1, keepdims=True)
    var = jnp.mean(jnp.square(h - mu), -1, keepdims=True)
    return (h - mu) * lax.rsqrt(var + LN_EPS) * g.reshape(MLSTM_HEADS, HEAD_DIM).astype(F32)

def pool_mix(u, hist, pos0, w_pool, pool_scale):
    B, T, _ = u.shape
    ext = jnp.concatenate([hist.astype(u.dtype), u], axis=1)
    cs = jnp.cumsum(ext.astype(F32), axis=1)
    cs = jnp.pad(cs, ((0, 0), (1, 0), (0, 0)))
    cs = cs.reshape(B, POOL_HIST + 1 + T, POOL_GROUPS, POOL_GROUP_DIM)
    pos = pos0 + jnp.arange(T, dtype=jnp.int32)
    base = POOL_HIST + 1
    means = []
    for g, w in enumerate(POOL_WINDOWS):
        s = cs[:, base:, g] - cs[:, base - w:base - w + T, g]
        cnt = jnp.minimum(pos + 1, w).astype(F32)
        means.append(s / cnt[None, :, None])
    mean = jnp.stack(means, axis=2)
    z = mean - u.reshape(B, T, POOL_GROUPS, POOL_GROUP_DIM).astype(F32)
    out = jnp.einsum('btgc,gcd->btgd', z, w_pool.astype(F32)).reshape(B, T, POOL_WIDTH)
    out = out * pool_scale.astype(F32)
    return out.astype(u.dtype), ext[:, -POOL_HIST:]

def mlstm_chunk(carry, inp):
    C, n, m = carry
    q, k, v, ig, lf = inp
    L = q.shape[2]
    F = jnp.cumsum(lf, axis=-1)
    causal = jnp.tril(jnp.ones((L, L), dtype=bool))
    logD = F[..., :, None] - F[..., None, :] + ig[..., None, :]
    logD = jnp.where(causal, logD, -jnp.inf)
    inter = m[..., None] + F
    m_t = jnp.maximum(inter, jnp.max(logD, axis=-1))
    Dw = jnp.exp(logD - m_t[..., None])
    sc = jnp.exp(inter - m_t)
    qk = jnp.einsum('bhtk,bhsk->bhts', q, k) * Dw
    num = jnp.einsum('bhts,bhsv->bhtv', qk, v) + sc[..., None] * jnp.einsum('bhvk,bhtk->bhtv', C, q)
    den = jnp.sum(qk, axis=-1) + sc * jnp.einsum('bhk,bhtk->bht', n, q)
    h = num / jnp.maximum(jnp.abs(den), jnp.exp(-m_t))[..., None]
    m_new = m_t[..., -1]
    wk = jnp.exp(ig + F[..., -1:] - F - m_new[..., None])
    decay = jnp.exp(m + F[..., -1] - m_new)
    C_new = decay[..., None, None] * C + jnp.einsum('bhsv,bhsk->bhvk', v * wk[..., None], k)
    n_new = decay[..., None] * n + jnp.einsum('bhs,bhsk->bhk', wk, k)
    return (C_new, n_new, m_new), h

def mlstm(q, k, v, ig, lf, C0, n0, m0):
    B, T, H, dh = q.shape
    L = min(CHUNK, T)
    nc = T // L
    k = k * (dh ** -0.5)

    def to_chunks(a):
        a = a.astype(F32).reshape((B, nc, L) + a.shape[2:])
        return jnp.swapaxes(jnp.moveaxis(a, 1, 0), 2, 3)

    xs = (to_chunks(q), to_chunks(k), to_chunks(v), to_chunks(ig), to_chunks(lf))
    carry0 = (C0.astype(F32), n0.astype(F32), m0.astype(F32))
    (C, n, m), hs = lax.scan(mlstm_chunk, carry0, xs)
    h = jnp.transpose(hs, (1, 0, 3, 2, 4)).reshape(B, T, H, dh)
    return h, C, n, m

def moe(xf, w_router, b_router, w1, b1, w2, b2):
    N, D = xf.shape
    logits = xf.astype(F32) @ w_router.astype(F32) + b_router.astype(F32)
    top_v, top_e = lax.top_k(logits, TOP_K)
    gates = jax.nn.softmax(top_v, axis=-1)
    A = N * TOP_K
    e_flat = top_e.reshape(A).astype(jnp.int32)
    g_flat = gates.reshape(A)
    tok = jnp.arange(A, dtype=jnp.int32) // TOP_K
    order = jnp.argsort(e_flat)
    e_sorted = e_flat[order]
    counts = jnp.bincount(e_flat, length=N_EXPERTS)
    padded = (counts + MOE_BLOCK - 1) // MOE_BLOCK * MOE_BLOCK
    start = jnp.cumsum(counts) - counts
    ends_p = jnp.cumsum(padded)
    pstart = ends_p - padded
    dest = pstart[e_sorted] + jnp.arange(A, dtype=jnp.int32) - start[e_sorted]
    n_blocks = (A + MOE_BLOCK - 1) // MOE_BLOCK + N_EXPERTS
    P = n_blocks * MOE_BLOCK
    slot_tok = jnp.zeros((P,), jnp.int32).at[dest].set(tok[order])
    slot_gate = jnp.zeros((P,), F32).at[dest].set(g_flat[order])
    block_start = jnp.arange(n_blocks, dtype=jnp.int32) * MOE_BLOCK
    block_exp = jnp.minimum(jnp.searchsorted(ends_p, block_start, side='right'), N_EXPERTS - 1)

    def run_block(args):
        e, toks, g = args
        xb = xf[toks]
        h = xb @ w1[e] + b1[e]
        glu = jnp.minimum(h[:, ::2], SWIGLU_LIMIT)
        lin = jnp.clip(h[:, 1::2], -SWIGLU_LIMIT, SWIGLU_LIMIT)
        a = glu * jax.nn.sigmoid(SWIGLU_ALPHA * glu) * (lin + 1)
        out = a @ w2[e] + b2[e]
        return out * g[:, None].astype(out.dtype)

    outs = lax.map(run_block, (block_exp, slot_tok.reshape(n_blocks, MOE_BLOCK),
                               slot_gate.reshape(n_blocks, MOE_BLOCK)))
    return jnp.zeros_like(xf).at[slot_tok].add(outs.reshape(P, D).astype(xf.dtype))

def decoder_layer(x, p, hist, C0, n0, m0, pos0, w_in, b_i, b_f, w_pool, pool_scale, mh_g, w_out,
                  ln1_g, ln1_b, w_router, b_router, w_mlp1, b_mlp1, w_mlp2, b_mlp2,
                  ln2_g, ln2_b, w_ple, w_ple_gate):
    B, T, D = x.shape
    proj = x @ w_in
    M = MLSTM_WIDTH
    cuts = [POOL_WIDTH, POOL_WIDTH + M, POOL_WIDTH + 2 * M, POOL_WIDTH + 3 * M,
            POOL_WIDTH + 4 * M, POOL_WIDTH + 4 * M + MLSTM_HEADS]
    u, q, k, v, o, gi, gf = jnp.split(proj, cuts, axis=-1)
    pool_out, hist_new = pool_mix(u, hist, pos0, w_pool, pool_scale)
    hs = (B, T, MLSTM_HEADS, HEAD_DIM)
    ig = gi.astype(F32) + b_i.astype(F32)
    lf = jax.nn.log_sigmoid(gf.astype(F32) + b_f.astype(F32))
    h, C, n, m = mlstm(q.reshape(hs), k.reshape(hs), v.reshape(hs), ig, lf, C0, n0, m0)
    h = jax.nn.sigmoid(o.astype(F32)) * head_norm(h, mh_g).reshape(B, T, M)
    mix = jnp.concatenate([pool_out, h.astype(x.dtype)], axis=-1) @ w_out
    x1 = layer_norm(DN_ALPHA * x + mix, ln1_g, ln1_b)
    ff = moe(x1.reshape(B * T, D), w_router, b_router, w_mlp1, b_mlp1, w_mlp2, b_mlp2).reshape(B, T, D)
    x2 = layer_norm(DN_ALPHA * x1 + ff, ln2_g, ln2_b)
    y = x2 + jax.nn.sigmoid(x2 @ w_ple_gate) * (p.astype(x2.dtype) @ w_ple)
    return y, hist_new, C, n, m

def setup_inputs(seed: int = 0) -> dict:
    key = jax.random.key(seed)
    ks = jax.random.split(key, 27)

    def nrm(k, shape, s):
        return s * jax.random.normal(k, shape, F32)

    H, dh = MLSTM_HEADS, HEAD_DIM
    return {
        'x_prompt': nrm(ks[0], (BATCH, SEQ, D_MODEL), 1.0),
        'x_sample': nrm(ks[1], (DEC_BATCH, DEC_SEQ, D_MODEL), 1.0),
        'state_pool': nrm(ks[2], (DEPTH, DEC_BATCH, POOL_HIST, POOL_WIDTH), 1.0),
        'state_mlstm_C': nrm(ks[3], (DEPTH, DEC_BATCH, H, dh, dh), 0.1),
        'state_mlstm_n': nrm(ks[4], (DEPTH, DEC_BATCH, H, dh), 0.1),
        'state_mlstm_m': nrm(ks[5], (DEPTH, DEC_BATCH, H), 0.5),
        'p_prompt': nrm(ks[6], (DEPTH, BATCH, SEQ, PLE_DIM), 1.0),
        'p_sample': nrm(ks[7], (DEPTH, DEC_BATCH, DEC_SEQ, PLE_DIM), 1.0),
        'w_in': nrm(ks[8], (DEPTH, D_MODEL, IN_COLS), D_MODEL ** -0.5),
        'b_i': nrm(ks[9], (DEPTH, H), 0.1),
        'b_f': jax.random.uniform(ks[10], (DEPTH, H), F32, 3.0, 6.0),
        'w_pool': nrm(ks[11], (DEPTH, POOL_GROUPS, POOL_GROUP_DIM, POOL_GROUP_DIM), POOL_GROUP_DIM ** -0.5),
        'pool_scale': 1.0 + nrm(ks[12], (DEPTH, POOL_WIDTH), 0.1),
        'mh_g': 1.0 + nrm(ks[13], (DEPTH, MLSTM_WIDTH), 0.1),
        'w_out': nrm(ks[14], (DEPTH, MIX_WIDTH, D_MODEL), DN_BETA * MIX_WIDTH ** -0.5),
        'ln1_g': 1.0 + nrm(ks[15], (DEPTH, D_MODEL), 0.1),
        'ln1_b': nrm(ks[16], (DEPTH, D_MODEL), 0.02),
        'w_router': nrm(ks[17], (DEPTH, D_MODEL, N_EXPERTS), D_MODEL ** -0.5),
        'b_router': nrm(ks[18], (DEPTH, N_EXPERTS), 0.01),
        'w_mlp1': nrm(ks[19], (DEPTH, N_EXPERTS, D_MODEL, 2 * D_FF), D_MODEL ** -0.5),
        'b_mlp1': nrm(ks[20], (DEPTH, N_EXPERTS, 2 * D_FF), 0.02),
        'w_mlp2': nrm(ks[21], (DEPTH, N_EXPERTS, D_FF, D_MODEL), DN_BETA * D_FF ** -0.5),
        'b_mlp2': nrm(ks[22], (DEPTH, N_EXPERTS, D_MODEL), 0.02),
        'ln2_g': 1.0 + nrm(ks[23], (DEPTH, D_MODEL), 0.1),
        'ln2_b': nrm(ks[24], (DEPTH, D_MODEL), 0.02),
        'w_ple': nrm(ks[25], (DEPTH, PLE_DIM, D_MODEL), DN_BETA * PLE_DIM ** -0.5),
        'w_ple_gate': nrm(ks[26], (DEPTH, D_MODEL, D_MODEL), D_MODEL ** -0.5),
    }

def reference(x_prompt, x_sample, state_pool, state_mlstm_C, state_mlstm_n, state_mlstm_m,
              p_prompt, p_sample, w_in, b_i, b_f, w_pool, pool_scale, mh_g, w_out,
              ln1_g, ln1_b, w_router, b_router, w_mlp1, b_mlp1, w_mlp2, b_mlp2,
              ln2_g, ln2_b, w_ple, w_ple_gate):
    yp, ys = x_prompt, x_sample
    pool_p, C_p, n_p, m_p = [], [], [], []
    pool_s, C_s, n_s, m_s = [], [], [], []
    for i in range(DEPTH):
        wts = (w_in[i], b_i[i], b_f[i], w_pool[i], pool_scale[i], mh_g[i], w_out[i],
               ln1_g[i], ln1_b[i], w_router[i], b_router[i], w_mlp1[i], b_mlp1[i],
               w_mlp2[i], b_mlp2[i], ln2_g[i], ln2_b[i], w_ple[i], w_ple_gate[i])
        hist0 = jnp.zeros((BATCH, POOL_HIST, POOL_WIDTH), yp.dtype)
        C0 = jnp.zeros((BATCH, MLSTM_HEADS, HEAD_DIM, HEAD_DIM), F32)
        n0 = jnp.zeros((BATCH, MLSTM_HEADS, HEAD_DIM), F32)
        m0 = jnp.zeros((BATCH, MLSTM_HEADS), F32)
        yp, hp, Cp, np_, mp = decoder_layer(yp, p_prompt[i], hist0, C0, n0, m0, 0, *wts)
        ys, hs, Cs, ns, ms = decoder_layer(ys, p_sample[i], state_pool[i], state_mlstm_C[i],
                                           state_mlstm_n[i], state_mlstm_m[i], PAST_LEN, *wts)
        pool_p.append(hp); C_p.append(Cp); n_p.append(np_); m_p.append(mp)
        pool_s.append(hs); C_s.append(Cs); n_s.append(ns); m_s.append(ms)
    new_pool_prompt = jnp.stack(pool_p)
    new_C_prompt = jnp.stack(C_p)
    new_n_prompt = jnp.stack(n_p)
    new_m_prompt = jnp.stack(m_p)
    new_pool_sample = jnp.stack(pool_s)
    new_C_sample = jnp.stack(C_s)
    new_n_sample = jnp.stack(n_s)
    new_m_sample = jnp.stack(m_s)
    return (yp, ys, new_pool_prompt, new_C_prompt, new_n_prompt, new_m_prompt,
            new_pool_sample, new_C_sample, new_n_sample, new_m_sample)


_drawn_inputs = setup_inputs


def setup_inputs(seed=0):
    import zlib

    import numpy as np

    out = dict(_drawn_inputs(seed))
    spreads = {}
    factors = {'b_router': 3.347, 'b_mlp1': 8.0, 'b_mlp2': 6.29, 'ln2_b': 2.974}
    for name, (base, spread) in spreads.items():
        noise = np.random.default_rng([zlib.crc32(name.encode()), seed]).standard_normal(out[name].shape)
        drawn = base * np.exp(spread * noise) if base else spread * noise
        out[name] = __import__('jax').numpy.asarray(drawn.astype(out[name].dtype))
    for name, factor in factors.items():
        out[name] = (out[name] * factor).astype(out[name].dtype)
    return out
```

```python
from contextlib import ExitStack

import numpy as np
import concourse.bass as bass
from concourse import mybir

F32 = mybir.dt.float32
BF16 = mybir.dt.bfloat16
I32 = mybir.dt.int32
U32 = mybir.dt.uint32
ALU = mybir.AluOpType
ACT = mybir.ActivationFunctionType
AX = mybir.AxisListType

P = 128
D = 1024
KD = D // P
SEQ = 256
SAMPLES = 8
TOK = SEQ + SAMPLES
CHUNKS = [(0, P), (P, P), (SEQ, SAMPLES)]
HEADS = 4
HD = 128
HIST = 15
WINDOWS = (2, 4, 8, 16)
STATES = SAMPLES * HEADS
EXPERTS = 32
TOPK = 4
FF = 1024
PLE = 256
BLOCK = 64
PASSES = -(-TOK // BLOCK)
STEP = 4
TABLE = PASSES * EXPERTS + 2 * STEP
FAR = 16384.0
ALPHA = 2.0 ** 0.25
EPS = 1e-5
LIMIT = 7.0
SIG = 1.702
SLOTS = 16
SLOT = 2048
UNITS = 12
FIRST = 4
BLOCKS_IN = ((512, "q"), (1024, "k"), (1536, "v"), (0, "u"), (2048, "o"))
TILES = 20

C_ID, C_CAUSAL, C_BEFORE, C_ONES, C_SLOT = 0, 128, 256, 384, 512
C_EXP = 640
C_HIST = C_EXP + EXPERTS
C_CNT = C_HIST + 4 * SAMPLES
C_RANK = C_CNT + 4 * 16
C_HALF = C_RANK + 3 * TOPK
C_LIM = C_HALF + 1
C_BLK = C_LIM + 4
C_EPS = C_BLK + PASSES
C_SEL = C_EPS + 1
C_END = C_SEL + TABLE


def constants():
    t = np.zeros((P, C_END), np.float32)
    p = np.arange(P)
    t[:, C_ID:C_ID + P] = np.eye(P)
    t[:, C_CAUSAL:C_CAUSAL + P] = p[:, None] <= p[None, :]
    t[:, C_BEFORE:C_BEFORE + P] = p[:, None] < p[None, :]
    t[:, C_ONES:C_ONES + P] = 1.0
    t[:, C_SLOT:C_SLOT + P] = (p % BLOCK)[None, :]
    t[:, C_EXP:C_EXP + EXPERTS] = np.arange(EXPERTS)
    for g, w in enumerate(WINDOWS):
        for b in range(SAMPLES):
            t[b * HIST + HIST + 1 - w:(b + 1) * HIST, C_HIST + g * SAMPLES + b] = 1.0
        t[:, C_CNT + 16 * g:C_CNT + 16 * g + 16] = w / np.minimum(np.arange(16) + 1, w)
    for c, (t0, _) in enumerate(CHUNKS):
        for k in range(TOPK):
            t[:, C_RANK + TOPK * c + k] = TOPK * (t0 + p) + k - FAR
    t[:, C_HALF] = 2 * FAR + p // BLOCK
    t[:, C_LIM:C_LIM + 4] = BLOCK * np.arange(1, 5)
    t[:, C_BLK:C_BLK + PASSES] = FAR - BLOCK * np.arange(PASSES)
    t[:, C_EPS] = EPS
    t[:, C_SEL:C_SEL + TABLE] = p[:, None] % EXPERTS == np.arange(TABLE)[None, :] % EXPERTS
    t[3 * EXPERTS:, C_SEL:C_SEL + TABLE] = 0.0
    return t


def build(nc, consts, x_prompt, x_sample, state_pool, state_C, state_n, state_m, p_prompt, p_sample,
          w_in, b_i, b_f, w_pool, pool_scale, mh_g, w_out, ln1_g, ln1_b, w_router, b_router,
          w_mlp1, b_mlp1, w_mlp2, b_mlp2, ln2_g, ln2_b, w_ple, w_ple_gate,
          y_prompt, y_sample, pool_prompt, C_prompt, n_prompt, m_prompt,
          pool_sample, C_sample, n_sample, m_sample):
    with ExitStack() as ctx:
        def sb(name, shape, dt=F32):
            return ctx.enter_context(nc.sbuf_tensor(name, shape, dt))

        sems = {}

        def sem(name):
            if name not in sems:
                sems[name] = ctx.enter_context(nc.semaphore(name))
            return sems[name]

        ctx.enter_context(nc.allow_non_contiguous_dma(reason="gate columns and small states"))

        ring = sb("ring", [P, SLOTS, SLOT])
        cst = sb("cst", [P, C_END])
        xreg = sb("xreg", [P, 3 * D])
        lnreg = sb("lnreg", [P, 2 * D])
        proj = sb("proj", [P, TILES, TOK])
        xT = sb("xT", [P, KD, TOK])
        mixT = sb("mixT", [P, KD, TOK])
        wgate = sb("wgate", [P, KD, 2 * HEADS])
        wpool = sb("wpool", [P, 4, P])
        hist = sb("hist", [P, 4 * P])
        bias_parts = sb("bias_parts", [3 * EXPERTS, 3 * FF], BF16)
        window = sb("window", [P, 2, 16 + SEQ])
        small = sb("small", [P, 160])
        srow = sb("srow", [STATES, 7, HD])
        scol = sb("scol", [P, 4, STATES])
        stat = sb("stat", [P, 64])
        bank = [ctx.enter_context(nc.psum_tensor(f"bank{b}", [P, 512], F32)) for b in range(8)]

        ident = cst[:, C_ID:C_ID + P]
        ones = cst[:, C_ONES:C_ONES + P]
        eps = cst[:, C_EPS:C_EPS + 1]

        xtok = xreg[:, :].rearrange("p (c d) -> p c d", c=3)
        ktok = xreg[:, 0:1024].rearrange("p (c h d) -> p c h d", c=2, h=HEADS)
        vtok = xreg[:, 1024:2048].rearrange("p (c h d) -> p c h d", c=2, h=HEADS)
        decayed = xreg[:, 2048:3072].rearrange("p (c h t) -> p c h t", c=2, h=HEADS)
        hout = lnreg[:, 0:1024].rearrange("p (c h t) -> p c h t", c=2, h=HEADS)
        vweighted = lnreg[:, 1024:1536].rearrange("p (h d) -> p h d", h=HEADS)
        CT = lnreg[:, 1536:2048].rearrange("p (h d) -> p h d", h=HEADS)
        softp = lnreg[0:HEADS, 0:256]
        logf = lnreg[0:HEADS, 256:512]
        cumf = lnreg[0:HEADS, 512:768]
        runmax = lnreg[0:HEADS, 768:1024]
        rows = lnreg[0:HEADS, 1024:1024 + 7 * P].rearrange("h (q t) -> h q t", q=7)
        ROW_G, ROW_EMT, ROW_WK, ROW_SC = 0, 2, 4, 6
        maxdiag = [xreg[0:HEADS, 2048 + 512 * c:2560 + 512 * c].rearrange("p (h t) -> p h t", h=HEADS)
                   for c in range(2)]
        gates = sb("gates", [2 * HEADS, TOK])
        fgate = sb("fgate", [HEADS, SEQ])
        gcol = small[:, 0:28]
        dec_b = small[:, 28:32]
        nstate = small[:, 32:36]
        nout = small[0:HEADS, 36:37]
        m1 = small[0:HEADS, 37:38]
        m2 = small[0:HEADS, 38:39]
        nlast = small[0:HEADS, 39:41]
        ddiag = small[0:HEADS, 41:45]
        mhg = small[:, 45:49]
        pscale = small[:, 49:53]
        gbias = small[0:2 * HEADS, 53:54]
        histsum = small[:, 54:86]
        den = small[:, 86:90]
        den2 = small[:, 90:94]
        brout = sb("brout", [1, EXPERTS])
        ncol_out = sb("ncol_out", [HEADS, HD])
        s_gate = stat[0:STATES, 0:2]
        s_col = [stat[0:STATES, 2 + i:3 + i] for i in range(14)]
        (S_M0, S_LF, S_INTER, S_M, S_NM, S_DW, S_SC, S_EMT, S_QK, S_NQ, S_DEN, S_R, S_T, S_RSTD) = range(14)
        s_bn = stat[0:STATES, 16:22]
        s_mv = stat[0:STATES, 22:24]
        h_bn = stat[:, 24:30]
        h_mv = stat[:, 30:38].rearrange("p (h m) -> p h m", h=HEADS)
        h_rstd = stat[:, 38:42]
        ln_bn = stat[:, 42:54]
        ln_mv = stat[:, 54:56]
        ln_rstd = stat[:, 56:57]
        sdiag = scol[0:STATES, 3, :]
        ukeep = sb("ukeep", [P, 4, HIST + SAMPLES])
        urow = sb("urow", [HIST + SAMPLES, 4 * P])
        SMALL_OUTS = 8
        SQ, SK, SV, SN, SCQ, SY, SPROD = range(7)

        def slots(s, n, width):
            return ring[:, s:s + n, :].rearrange("p s f -> p (s f)")[:, 0:width]

        Cst = slots(10, 2, STATES * HD).rearrange("p (s k) -> p s k", s=STATES)
        qb = slots(12, 2, STATES * HD).rearrange("p (s k) -> p s k", s=STATES)
        kb = slots(14, 2, STATES * HD).rearrange("p (s k) -> p s k", s=STATES)
        bsrc = ring[0:3 * EXPERTS, 14:16, :].rearrange("p s f -> p (s f)")[:, 0:3 * FF]

        moe = proj[:, :, :].rearrange("p t n -> p (t n)")
        off = [0]

        def part(n):
            off[0] += n
            return moe[:, off[0] - n:off[0]]

        onehot = part(3 * P).rearrange("p (c s) -> p c s", c=3)
        xgT = part(512).rearrange("p (k s) -> p k s", k=KD)
        glu = part(512).rearrange("p (q f) -> p q f", q=2)
        lin = part(512).rearrange("p (q f) -> p q f", q=2)
        sig = part(512).rearrange("p (q f) -> p q f", q=2)
        act_out = part(512)
        aT = part(512).rearrange("p (m s) -> p m s", m=4)
        eout = part(1024).rearrange("p (b d) -> p b d", b=2)
        info = part(6).rearrange("p (c v) -> p c v", c=3)
        logits = part(EXPERTS)
        top = part(8)
        gate4 = part(4)
        idx4 = part(4)
        gsum = part(4)
        oh4 = part(TOPK * EXPERTS).rearrange("p (k e) -> p k e", k=TOPK)
        oh4v = part(TOPK * EXPERTS).rearrange("p (k e) -> p k e", k=TOPK)
        vrow = part(2 * EXPERTS).rearrange("p (v e) -> p v e", v=2)
        posm = part(EXPERTS)
        assert off[0] <= TILES * TOK
        mix_flat = mixT[:, :, :].rearrange("p k n -> p (k n)")
        pos_table = mix_flat[:, 0:3 * TABLE].rearrange("p (c n) -> p c n", c=3)
        val_table = mix_flat[:, 3 * TABLE:9 * TABLE].rearrange("p (c n v) -> p c n v", c=3, v=2)
        mask = mix_flat[:, 9 * TABLE:9 * TABLE + 3 * EXPERTS].rearrange("p (c e) -> p c e", c=3)
        assert 9 * TABLE + 3 * EXPERTS <= KD * TOK
        sel = sb("sel", [3 * EXPERTS, 2, BLOCK], BF16)
        egate = sb("egate", [P, 2])
        erow = sb("erow", [P, 2], U32)
        idx8 = sb("idx8", [P, 8], U32)
        extra = sb("extra", [P, 1], I32)
        wrout = sb("wrout", [P, KD, EXPERTS])
        x1T = xT

        q_row = nc.dram_tensor("q_row", (STATES, HD), F32).ap()
        k_row = nc.dram_tensor("k_row", (STATES, HD), F32).ap()
        g_row = nc.dram_tensor("g_row", (SAMPLES, HEADS, 2), F32).ap()
        ff_rows = nc.dram_tensor("ff_rows", (TOK * TOPK * 2, 512), F32).ap()

        block = ctx.enter_context(nc.Block())
        K_SCALE = HD ** -0.5

        def tile_done(t):
            if t >= 16 or t % 2:
                return "tile_act", (t + 1) // 2 if t < 16 else 8 + t - 15
            return "tile_dve", t // 2 + 1

        def unit_weights(e, u):
            if u < 8:
                return w_mlp1[0, bass.ds(e, 1), u * P:(u + 1) * P, :].rearrange("o p f -> p (o f)")
            r = u - 8
            return w_mlp2[0, bass.ds(e, 1), r * 2 * P:(r + 1) * 2 * P, :].rearrange("o (a p) f -> p (o a) f", a=2)

        def unit_place(slot, u):
            if u < 8:
                return ring[:, slot, :]
            return ring[:, slot, :].rearrange("p (a f) -> p a f", a=2)

        def slot_of(body_unit):
            return (FIRST + body_unit) % SLOTS

        def landings(body_unit):
            s = slot_of(body_unit)
            return sum(slot_of(v) == s for v in range(body_unit + 1))

        before = [2 if s < 4 else 1 if s < 10 else 0 for s in range(SLOTS)]

        @block.sync
        def _(sp):
            for c, (t0, n) in enumerate(CHUNKS):
                src = x_prompt[0, t0:t0 + n, :] if c < 2 else x_sample[:, 0, :]
                sp.dma_start(xtok[0:n, c, :], src).then_inc(sem(f"x_in{c}"), 16)
            for b, (col, _) in enumerate(BLOCKS_IN):
                for half in range(2):
                    s = 2 * b + half
                    sp.dma_start(ring[:, s, :].rearrange("p (k n) -> p k n", k=4),
                                 w_in[0, 512 * half:512 * half + 512, col:col + 512]
                                 .rearrange("(k p) n -> p k n", p=P)).then_inc(sem(f"slot{s}"), 16)
                if b == 0:
                    for g in range(3):
                        rows_ = slice(g * EXPERTS, (g + 1) * EXPERTS)
                        sp.dma_start(bsrc[rows_, 0:2 * FF], b_mlp1[0]).then_inc(sem("bias_in"), 16)
                        sp.dma_start(bsrc[rows_, 2 * FF:3 * FF], b_mlp2[0]).then_inc(sem("bias_in"), 16)
                if b == 1:
                    sp.dma_start(Cst, state_C[0].rearrange("b h v k -> v (b h) k")).then_inc(sem("C_in"), 16)
            sp.wait_ge(sem("gates_done"), 1)
            sp.dma_start(fgate[:, :], gates[HEADS:2 * HEADS, 0:SEQ]).then_inc(sem("fgate_in"), 16)
            sp.dma_start(g_row.rearrange("b h g -> g h b")[0], gates[0:HEADS, SEQ:TOK]).then_inc(sem("g_row"), 16)
            sp.dma_start(g_row.rearrange("b h g -> g h b")[1], gates[HEADS:2 * HEADS, SEQ:TOK])\
              .then_inc(sem("g_row"), 16)
            sp.wait_ge(sem("g_row"), 32)
            sp.dma_start(s_gate, g_row.rearrange("b h g -> (b h) g")).then_inc(sem("s_gate_in"), 16)
            for s in range(4):
                sp.wait_ge(sem("tile_ps"), 4 * (s // 2) + 4)
                sp.dma_start(ring[:, s, :].rearrange("p (k n) -> p k n", k=2),
                             w_out[0, 256 * s:256 * s + 256, :].rearrange("(k p) n -> p k n", p=P))\
                  .then_inc(sem(f"slot{s}"), 16)
            sp.wait_ge(sem("srow_ready"), 1)
            sp.dma_start(q_row, srow[:, SQ, :]).then_inc(sem("qk_row"), 16)
            sp.dma_start(k_row, srow[:, SK, :]).then_inc(sem("qk_row"), 16)
            sp.wait_ge(sem("qk_row"), 32)
            sp.dma_start(qb, q_row.partition_broadcast(P)).then_inc(sem("qb_in"), 16)
            sp.wait_ge(sem("bias_split"), 1)
            sp.dma_start(kb, k_row.partition_broadcast(P)).then_inc(sem("kb_in"), 16)

            def load_unit(e, j, u):
                s = slot_of(UNITS * j + u)
                sp.dma_start(unit_place(s, u), unit_weights(e, u)).then_inc(sem(f"slot{s}"), 16)

            for n in range(UNITS * STEP):
                s = slot_of(n)
                if n < UNITS:
                    if s < 10:
                        sp.wait_ge(sem("tile_ps"), 4 * (s // 2) + 4)
                    elif s == 10:
                        sp.wait_ge(sem("C_out"), 16)
                    elif s == 12:
                        sp.wait_ge(sem("Cnew_done"), 1)
                elif n < SLOTS:
                    sp.wait_ge(sem("mix_ps"), 6)
                else:
                    sp.wait_ge(sem("units_used"), n - SLOTS + 1)
                load_unit(n // UNITS, n // UNITS, n % UNITS)

            def load_body(e, done):
                for n in range(UNITS * STEP):
                    sp.wait_ge(sem("units_used"), done + (n - SLOTS + 1))
                    load_unit(e + n // UNITS, n // UNITS, n % UNITS)

            bodies = EXPERTS // STEP
            with sp.Fori(1, bodies) as i:
                load_body(i * STEP, i * (STEP * UNITS))
            sp.wait_ge(sem("passes_ready"), 1)
            npass = sp.value_load(extra[0:1, 0:1], min_val=0, max_val=PASSES - 1) + 1
            with sp.If(npass > 1):
                with sp.Fori(1, npass) as b:
                    with sp.Fori(0, bodies) as i:
                        load_body(i * STEP, b * (EXPERTS * UNITS) + i * (STEP * UNITS))
            sp.nop()

            used = npass * (EXPERTS * UNITS)

            def wait_slot(s):
                sp.wait_ge(sem("units_used"), used + ((s - FIRST) % SLOTS + 1 - SLOTS))

            for i in range(4):
                wait_slot(4 + i)
                sp.dma_start(ring[:, 4 + i, :].rearrange("p (k n) -> p k n", k=2),
                             w_ple_gate[0, 256 * i:256 * i + 256, :].rearrange("(k p) n -> p k n", p=P))\
                  .then_inc(sem("wpg_in"), 16)
            wait_slot(9)
            sp.dma_start(ring[:, 8, :].rearrange("p (k n) -> p k n", k=2),
                         w_ple[0].rearrange("(k p) n -> p k n", p=P)).then_inc(sem("wple_in"), 16)
            for c, (t0, n) in enumerate(CHUNKS):
                src = p_prompt[0, 0, t0:t0 + n, :] if c < 2 else p_sample[0, :, 0, :]
                sp.dma_start(ring[0:n, 9, c * PLE:(c + 1) * PLE], src).then_inc(sem("p_in"), 16)
            sp.wait_ge(sem("rows_out"), npass * (16 * EXPERTS))
            for c, (t0, n) in enumerate(CHUNKS):
                sp.dma_start(slots(10 + 2 * c, 2, 4096)[0:n, :],
                             ff_rows.rearrange("(t r) f -> t (r f)", r=2 * TOPK)[t0:t0 + n, :])\
                  .then_inc(sem(f"ff_in{c}"), 16)
            for c, (t0, n) in enumerate(CHUNKS):
                sp.wait_ge(sem("y_done"), c + 1)
                dst = y_prompt[0, t0:t0 + n, :] if c < 2 else y_sample[:, 0, :]
                sp.dma_start(dst, xtok[0:n, c, :]).then_inc(sem("y_out"), 16)
            sp.wait_ge(sem("y_out"), 48)
            sp.wait_ge(sem("C_out"), 16)
            sp.wait_ge(sem("small_out"), 16 * SMALL_OUTS)

        @block.tensor
        def _(pe):
            pe.wait_ge(sem("cst_in"), 16)
            for g in range(6):
                c, half = g // 2, g % 2
                n = CHUNKS[c][1]
                if half == 0:
                    pe.wait_ge(sem(f"x_in{c}"), 16)
                for k in range(4):
                    last = pe.transpose(bank[g][:, k * P:k * P + n],
                                        xtok[0:n, c, (4 * half + k) * P:(4 * half + k + 1) * P], ident[0:n, 0:n])
                last.then_inc(sem("xT_ps"), 1)
            pe.wait_ge(sem("xT_dve"), 3)
            pe.wait_ge(sem("xT_act"), 3)
            pe.wait_ge(sem("wgate_in"), 16)
            for k in range(KD):
                last = pe.matmul(bank[6][0:2 * HEADS, 0:TOK], wgate[:, k, :], xT[:, k, :],
                                 start=(k == 0), stop=(k == KD - 1))
            last.then_inc(sem("gates_ps"), 1)
            pe.wait_ge(sem("hist_in"), 16)
            for g in range(4):
                last = pe.matmul(bank[7][:, g * SAMPLES:(g + 1) * SAMPLES], hist[0:SAMPLES * HIST, g * P:(g + 1) * P],
                                 cst[0:SAMPLES * HIST, C_HIST + g * SAMPLES:C_HIST + (g + 1) * SAMPLES],
                                 start=True, stop=True)
            last.then_inc(sem("hist_ps"), 1)

            def project(t):
                b, j = t // 4, t % 4
                if t >= 2:
                    name, count = tile_done(t - 2)
                    pe.wait_ge(sem(name), count)
                for k in range(KD):
                    s = 2 * b + k // 4
                    if j == 0 and k % 4 == 0:
                        pe.wait_ge(sem(f"slot{s}"), 16)
                    w = ring[:, s, :].rearrange("p (k n) -> p k n", k=4)
                    last = pe.matmul(bank[t % 2][:, 0:TOK], w[:, k % 4, j * P:(j + 1) * P], xT[:, k, :],
                                     start=(k == 0), stop=(k == KD - 1))
                last.then_inc(sem("tile_ps"), 1)

            def turn_tokens(dst, first_tile, c):
                for h in range(HEADS):
                    last = pe.transpose(dst[:, h * P:(h + 1) * P], proj[:, first_tile + h, c * P:(c + 1) * P], ident)
                return last

            for t in range(8):
                project(t)
            pe.wait_ge(sem("tile_dve"), 4)
            pe.wait_ge(sem("tile_act"), 4)
            turn_tokens(bank[4], 4, 0).then_inc(sem("ktok_ps"), 1)
            turn_tokens(bank[5], 4, 1).then_inc(sem("ktok_ps"), 1)
            for t in range(8, 12):
                project(t)
            pe.wait_ge(sem("tile_dve"), 6)
            pe.wait_ge(sem("tile_act"), 6)
            turn_tokens(bank[2], 8, 0).then_inc(sem("vtok_ps"), 1)
            turn_tokens(bank[3], 8, 1).then_inc(sem("vtok_ps"), 1)
            pe.wait_ge(sem("scol_ready"), 1)
            pe.wait_ge(sem("gates_done"), 1)
            for i in range(3):
                last = pe.transpose(bank[6][0:STATES, i * HD:(i + 1) * HD], scol[:, i, :], ident)
            last.then_inc(sem("srow_ps"), 1)
            pe.wait_ge(sem("hist_done"), 1)
            pe.wait_ge(sem("rows_ready"), 1)
            for q in range(7):
                pe.transpose(bank[7][:, 4 * q:4 * q + 4], rows[:, q, :], ident[0:HEADS, 0:HEADS])
            pe.matmul(bank[7][:, 28:32], ones[0:HEADS, :], ddiag, start=True, stop=True).then_inc(sem("gcol_ps"), 1)
            project(12)
            pe.wait_ge(sem("vtok_done"), 2)
            for c in range(2):
                pe.matmul(bank[2 + c][:, :], ones[0:HEADS, :], maxdiag[c].rearrange("p h t -> p (h t)"),
                          start=True, stop=True).then_inc(sem("max_ps"), 1)
            pe.wait_ge(sem("ktok_done"), 2)
            for c in range(2):
                for h in range(HEADS):
                    last = pe.matmul(bank[4 + c][:, h * P:(h + 1) * P], proj[:, 4 + h, c * P:(c + 1) * P],
                                     proj[:, h, c * P:(c + 1) * P], start=True, stop=True)
                last.then_inc(sem("score_ps"), 1)
            project(13)
            project(14)
            project(15)
            pe.wait_ge(sem("sdiag_ready"), 1)
            pe.matmul(bank[6][:, 0:STATES], ones[0:STATES, :], sdiag, start=True, stop=True)
            pe.transpose(bank[6][:, STATES:2 * STATES], srow[:, SV, :], ident[0:STATES, 0:STATES])\
              .then_inc(sem("sbc_ps"), 1)

            def values(c, dst, dden):
                for h in range(HEADS):
                    pe.matmul(dst[:, h * P:(h + 1) * P], decayed[:, c, h, :], vtok[:, c, h, :], start=True, stop=True)
                for h in range(HEADS):
                    last = pe.matmul(dden[:, h:h + 1], decayed[:, c, h, :], ones[:, 0:1], start=True, stop=True)
                return last

            def memory(c, dst, dn):
                for h in range(HEADS):
                    pe.matmul(dst[:, h * P:(h + 1) * P], ktok[:, c, h, :], vweighted[:, h, :], start=True, stop=True)
                for h in range(HEADS):
                    w0 = 4 * (ROW_WK + c) + h
                    last = pe.matmul(dn[:, h:h + 1], ktok[:, c, h, :], gcol[:, w0:w0 + 1], start=True, stop=True)
                return last

            pe.wait_ge(sem("decayed_ready"), 1)
            pe.wait_ge(sem("gcol_done"), 1)
            values(0, bank[2], bank[3][:, 0:4]).then_inc(sem("num_ps"), 1)
            pe.wait_ge(sem("vw_ready"), 1)
            memory(0, bank[4], bank[3][:, 4:8]).then_inc(sem("mem_ps"), 1)
            for g in range(4):
                pe.wait_ge(sem("z_ready"), g + 1)
                if g == 0:
                    pe.wait_ge(sem("wpool_in"), 16)
                    pe.wait_ge(sem("gcol_done"), 1)
                else:
                    pe.wait_ge(sem("pool_done"), g)
                pe.matmul(bank[7][:, 0:TOK], wpool[:, g, :], proj[:, 12 + g, :], start=True, stop=True)\
                  .then_inc(sem("pool_ps"), 1)
                project(16 + g)
                if g == 1:
                    pe.wait_ge(sem("decayed_ready"), 2)
                    pe.wait_ge(sem("ct_ready"), 1)
                    pe.wait_ge(sem("num_done"), 1)
                    values(1, bank[5], bank[3][:, 8:12])
                    for h in range(HEADS):
                        pe.matmul(bank[2][:, h * P:(h + 1) * P], proj[:, h, P:2 * P], CT[:, h, :], start=True, stop=True)
                    for h in range(HEADS):
                        last = pe.matmul(bank[3][:, 12 + h:13 + h], proj[:, h, P:2 * P], nstate[:, h:h + 1],
                                         start=True, stop=True)
                    last.then_inc(sem("num_ps"), 1)
                    pe.wait_ge(sem("vw_ready"), 2)
                    memory(1, bank[4], bank[3][:, 16:20]).then_inc(sem("mem_ps"), 1)
            pe.wait_ge(sem("sbc_done"), 1)
            pe.wait_ge(sem("hn_ready"), 1)
            for h in range(HEADS):
                last = pe.transpose(bank[6][:, h * P:(h + 1) * P], hout[:, 0, h, :], ident)
            last.then_inc(sem("hT_ps"), 1)
            pe.wait_ge(sem("scq_ready"), 1)
            pe.wait_ge(sem("pool_done"), 4)
            pe.transpose(bank[7][0:STATES, 0:P], scol[:, 2, :], ident).then_inc(sem("scq_ps"), 1)
            pe.wait_ge(sem("hn_ready"), 2)
            pe.wait_ge(sem("hT_done"), 1)
            for h in range(HEADS):
                last = pe.transpose(bank[6][:, h * P:(h + 1) * P], hout[:, 1, h, :], ident)
            last.then_inc(sem("hT_ps"), 1)
            pe.wait_ge(sem("ct_ready"), 2)
            for h in range(HEADS):
                pe.transpose(bank[4][:, h * P:(h + 1) * P], CT[:, h, :], ident)
            pe.transpose(bank[5][0:HEADS, 0:P], nstate, ident)
            pe.wait_ge(sem("num_done"), 2)
            for g in range(4):
                last = pe.transpose(bank[2][0:HIST + SAMPLES, g * P:(g + 1) * P], ukeep[:, g, :], ident)
            last.then_inc(sem("cfin_ps"), 1)
            pe.wait_ge(sem("sh_ready"), 1)
            pe.transpose(bank[7][:, P:P + STATES], srow[:, SY, :], ident[0:STATES, 0:STATES]).then_inc(sem("shT_ps"), 1)

            pe.wait_ge(sem("hT_done"), 2)
            pe.wait_ge(sem("pool_done"), 4)
            pe.wait_ge(sem("num_done"), 2)
            pe.wait_ge(sem("tile_act"), 12)
            for c, (t0, n) in enumerate(CHUNKS):
                if c == 1:
                    pe.wait_ge(sem("cfin_done"), 3)
                if c == 2:
                    pe.wait_ge(sem("shT_done"), 1)
                for half in range(2):
                    for k in range(KD):
                        s = k // 2
                        if c == 0 and half == 0 and k % 2 == 0:
                            pe.wait_ge(sem(f"slot{s}"), 32)
                        w = ring[:, s, :].rearrange("p (k n) -> p k n", k=2)
                        last = pe.matmul(bank[2 * c + half][0:n, :], mixT[:, k, t0:t0 + n],
                                         w[:, k % 2, half * 512:half * 512 + 512], start=(k == 0), stop=(k == KD - 1))
                    last.then_inc(sem("mix_ps"), 1)

            pe.wait_ge(sem("wrout_in"), 32)
            for c, (t0, n) in enumerate(CHUNKS):
                pe.wait_ge(sem("x1_ready"), c + 1)
                for half in range(2):
                    g = 2 * c + half
                    if g >= 2:
                        pe.wait_ge(sem("x1T_done"), g - 1)
                    elif g == 1:
                        pe.wait_ge(sem("shT_done"), 1)
                    for k in range(4):
                        kk = 4 * half + k
                        last = pe.transpose(bank[6 + half][:, k * P:k * P + n],
                                            xtok[0:n, c, kk * P:(kk + 1) * P], ident[0:n, 0:n])
                    last.then_inc(sem("x1T_ps"), 1)
                pe.wait_ge(sem("x1T_done"), 2 * c + 2)
                pe.matmul(bank[c][0:n, 0:EXPERTS], ones[0:1, 0:n], brout[:, :], start=True, stop=False)
                for k in range(KD):
                    last = pe.matmul(bank[c][0:n, 0:EXPERTS], x1T[:, k, t0:t0 + n], wrout[:, k, :],
                                     start=False, stop=(k == KD - 1))
                last.then_inc(sem("logits_ps"), 1)
            pe.wait_ge(sem("mask_ready"), 3)
            for c, (_, n) in enumerate(CHUNKS):
                for a in range(c + 1):
                    m = CHUNKS[a][1]
                    left = cst[0:m, C_BEFORE:C_BEFORE + n] if a == c else ones[0:m, 0:n]
                    pe.matmul(bank[3][0:n, c * EXPERTS:(c + 1) * EXPERTS], left, mask[0:m, a, :],
                              start=(a == 0), stop=(a == c))
            for a in range(3):
                m = CHUNKS[a][1]
                last = pe.matmul(bank[4][:, 0:EXPERTS], ones[0:m, :], mask[0:m, a, :], start=(a == 0), stop=(a == 2))
            last.then_inc(sem("pos_ps"), 1)

            def gather():
                for c in range(3):
                    pe.matmul(bank[5][:, 0:2], onehot[:, c, :], info[:, c, :], start=(c == 0), stop=(c == 2))
                for k in range(KD):
                    for c in range(3):
                        last = pe.matmul(bank[2][:, k * BLOCK:(k + 1) * BLOCK], xtok[:, c, k * P:(k + 1) * P],
                                         onehot[:, c, 0:BLOCK], start=(c == 0), stop=(c == 2))
                last.then_inc(sem("gathered"), 1)

            def expert(n, j):
                i4 = n - j
                pe.wait_ge(sem("xg_done"), n * 3 + 3)
                pe.wait_ge(sem("h_read"), n + 1)
                for t in range(2):
                    for q in range(2):
                        col = FF * t + 512 * q
                        pe.matmul(bank[q][BLOCK * t:BLOCK * (t + 1), :], sel[:, j % 2, :],
                                  bias_parts[:, col:col + 512], start=True, stop=False)
                for k in range(KD):
                    u = UNITS * j + k
                    s = slot_of(u)
                    pe.wait_ge(sem(f"slot{s}"), i4 * 12 + 16 * (before[s] + landings(u)))
                    for q in range(2):
                        for t in range(2):
                            col = FF * t + 512 * q
                            last = pe.matmul(bank[q][BLOCK * t:BLOCK * (t + 1), :], xgT[:, k, :],
                                             ring[:, s, col:col + 512], start=False, stop=(k == KD - 1))
                    last.then_inc(sem("units_used"), 1)
                pe.wait_ge(sem("onehot_ready"), n * 3 + 6)
                gather()
                pe.wait_ge(sem("act_ready"), n + 1)
                for m in range(4):
                    last = pe.transpose(bank[3][:, m * P:(m + 1) * P], act_out[:, m * P:(m + 1) * P], ident)
                last.then_inc(sem("aT_ps"), 1)
                pe.wait_ge(sem("aT_done"), n + 1)
                pe.wait_ge(sem("out_done"), n + 1)
                for h in range(2):
                    pe.matmul(bank[4][BLOCK * h:BLOCK * (h + 1), :], sel[:, j % 2, :],
                              bias_parts[:, 2 * FF + 512 * h:2 * FF + 512 * h + 512], start=True, stop=False)
                for k in range(8):
                    u = UNITS * j + 8 + k // 2
                    s = slot_of(u)
                    if k % 2 == 0:
                        pe.wait_ge(sem(f"slot{s}"), i4 * 12 + 16 * (before[s] + landings(u)))
                    w = ring[:, s, :].rearrange("p (a f) -> p a f", a=2)
                    t, m = k // 4, k % 4
                    for h in range(2):
                        last = pe.matmul(bank[4][BLOCK * h:BLOCK * (h + 1), :], aT[:, m, BLOCK * t:BLOCK * (t + 1)],
                                         w[:, k % 2, 512 * h:512 * h + 512], start=False, stop=(k == 7))
                    if k % 2 == 1:
                        last.then_inc(sem("units_used"), 1)

            pe.wait_ge(sem("onehot_ready"), 3)
            gather()
            pe.wait_ge(sem("passes_ready"), 1)
            npass = pe.value_load(extra[0:1, 0:1], min_val=0, max_val=PASSES - 1) + 1
            with pe.Fori(0, npass * EXPERTS, STEP) as n:
                for j in range(STEP):
                    expert(n + j, j)

            pe.wait_ge(sem("out_done"), npass * EXPERTS + 1)
            pe.wait_ge(sem("xg_done"), npass * (3 * EXPERTS) + 3)
            pe.wait_ge(sem("p_in"), 48)
            for c, (t0, n) in enumerate(CHUNKS):
                for k in range(2):
                    last = pe.transpose(bank[c][:, k * P:k * P + n],
                                        ring[0:n, 9, c * PLE + k * P:c * PLE + (k + 1) * P], ident[0:n, 0:n])
                last.then_inc(sem("pT_ps"), 1)
            pe.wait_ge(sem("wple_in"), 16)
            pT = ring[:, 9, 768:768 + 2 * TOK].rearrange("p (k n) -> p k n", k=2)
            wple_sb = ring[:, 8, :].rearrange("p (k n) -> p k n", k=2)
            for c, (t0, n) in enumerate(CHUNKS):
                pe.wait_ge(sem("pT_done"), c + 1)
                for half in range(2):
                    g = 2 * c + half
                    if g >= 2:
                        pe.wait_ge(sem("ple_done"), g - 1)
                    for k in range(2):
                        last = pe.matmul(bank[4 + half][0:n, :], pT[:, k, t0:t0 + n],
                                         wple_sb[:, k, half * 512:half * 512 + 512], start=(k == 0), stop=(k == 1))
                    last.then_inc(sem("ple_ps"), 1)
            pe.wait_ge(sem("wpg_in"), 64)
            for c, (t0, n) in enumerate(CHUNKS):
                pe.wait_ge(sem("x2_ready"), c + 1)
                for half in range(2):
                    g = 2 * c + half
                    if g >= 2:
                        pe.wait_ge(sem("x2T_done"), g - 1)
                    for k in range(4):
                        kk = 4 * half + k
                        last = pe.transpose(bank[6 + half][:, k * P:k * P + n],
                                            xtok[0:n, c, kk * P:(kk + 1) * P], ident[0:n, 0:n])
                    last.then_inc(sem("x2T_ps"), 1)
                pe.wait_ge(sem("x2T_done"), 2 * c + 2)
                for half in range(2):
                    g = 2 * c + half
                    if g >= 4:
                        pe.wait_ge(sem("sig_done"), g - 3)
                    for k in range(KD):
                        w = ring[:, 4 + k // 2, :].rearrange("p (k n) -> p k n", k=2)
                        last = pe.matmul(bank[g % 4][0:n, :], x1T[:, k, t0:t0 + n],
                                         w[:, k % 2, half * 512:half * 512 + 512], start=(k == 0), stop=(k == KD - 1))
                    last.then_inc(sem("gate_ps"), 1)

        @block.vector
        def _(dve):
            counts = {}

            def step(ins, name="dve_chain"):
                counts[name] = counts.get(name, 0) + 1
                ins.then_inc(sem(name), 1)
                dve.wait_ge(sem(name), counts[name])

            TT = dve.tensor_tensor
            TS = dve.tensor_scalar
            STT = dve.scalar_tensor_tensor

            def over(col, shape):
                return col.to_broadcast(shape)

            for g in (0, 2, 4):
                c = g // 2
                t0, n = CHUNKS[c]
                dve.wait_ge(sem("xT_ps"), g + 1)
                dve.tensor_copy(xT[:, 0:4, t0:t0 + n], bank[g][:, :].rearrange("p (k t) -> p k t", k=4)[:, :, 0:n])\
                   .then_inc(sem("xT_dve"), 1)
            dve.wait_ge(sem("hist_ps"), 1)
            dve.tensor_copy(histsum, bank[7][:, 0:32]).then_inc(sem("hist_done"), 1)

            def empty_tile(t):
                dve.wait_ge(sem("tile_ps"), t + 1)
                if 4 <= t < 8:
                    ins = TS(proj[:, t, :], bank[t % 2][:, 0:TOK], K_SCALE, None, ALU.mult)
                else:
                    ins = dve.tensor_copy(proj[:, t, :], bank[t % 2][:, 0:TOK])
                ins.then_inc(sem("tile_dve"), 1)

            empty_tile(0)
            dve.wait_ge(sem("fgate_in"), 16)
            step(STT(softp, fgate[:, :], -1.0, fgate[:, :], ALU.mult, ALU.min), "softp_ready")
            empty_tile(2)
            dve.wait_ge(sem("softp_done"), 1)
            step(STT(logf, fgate[:, :], 0.0, softp, ALU.min, ALU.subtract))
            for c in range(2):
                s = slice(c * P, (c + 1) * P)
                step(dve.tensor_tensor_scan(cumf[:, s], ones[0:HEADS, :], logf[:, s], 0.0, ALU.mult, ALU.add))
                step(TT(rows[:, ROW_G + c, :], gates[0:HEADS, s], cumf[:, s], ALU.subtract))
                step(dve.tensor_tensor_scan(runmax[:, s], rows[:, ROW_G + c, :], rows[:, ROW_G + c, :],
                                            m1 if c else 0.0, ALU.max, ALU.max))
                e = (c + 1) * P - 1
                step(TT(m2 if c else m1, cumf[:, e:e + 1], runmax[:, e:e + 1], ALU.add))
                step(TS(nlast[:, c:c + 1], runmax[:, e:e + 1], -1.0, None, ALU.mult))
                step(TT(rows[:, ROW_EMT + c, :], cumf[:, s], runmax[:, s], ALU.add))
                step(TT(maxdiag[c], runmax[:, s].unsqueeze(1).to_broadcast([HEADS, HEADS, P]),
                        ident[0:HEADS, 0:HEADS].unsqueeze(2).to_broadcast([HEADS, HEADS, P]), ALU.mult),
                     "runmax_ready")
            empty_tile(4)
            dve.wait_ge(sem("rows_act"), 1)
            step(TS(ddiag, ident[0:HEADS, 0:HEADS], rows[:, ROW_SC, P - 1:P], None, ALU.mult), "rows_ready")
            empty_tile(6)
            dve.wait_ge(sem("ktok_ps"), 1)
            dve.tensor_copy(ktok[:, 0], bank[4][:, :].rearrange("p (h d) -> p h d", h=HEADS)).then_inc(sem("ktok_done"), 1)
            empty_tile(8)
            empty_tile(10)
            dve.wait_ge(sem("tile_act"), 6)
            dve.wait_ge(sem("tile_dve"), 6)
            for i in range(3):
                ins = dve.tensor_copy(scol[:, i, :].rearrange("p (b h) -> p b h", h=HEADS),
                                      proj[:, 4 * i:4 * i + 4, SEQ:TOK].rearrange("p h b -> p b h"))
                counts["dve_chain"] = counts.get("dve_chain", 0) + 1
                ins.then_inc(sem("dve_chain"), 1)
            dve.wait_ge(sem("dve_chain"), counts["dve_chain"])
            dve.engine_nop().then_inc(sem("scol_ready"), 1)
            dve.wait_ge(sem("vtok_ps"), 1)
            dve.tensor_copy(vtok[:, 0], bank[2][:, :].rearrange("p (h d) -> p h d", h=HEADS)).then_inc(sem("vtok_done"), 1)
            dve.wait_ge(sem("srow_ps"), 1)
            step(dve.tensor_copy(srow[:, SQ:SV + 1, :], bank[6][0:STATES, 0:3 * HD].rearrange("p (i d) -> p i d", i=3)),
                 "srow_ready")
            dve.wait_ge(sem("gcol_ps"), 1)
            step(dve.tensor_copy(small[:, 0:32], bank[7][:, 0:32]), "gcol_done")
            empty_tile(12)

            dve.wait_ge(sem("s_gate_in"), 16)
            dve.wait_ge(sem("states_in"), 32)
            f_, i_ = s_gate[:, 1:2], s_gate[:, 0:1]
            step(STT(s_col[S_T], f_, -1.0, f_, ALU.mult, ALU.min), "s_soft_ready")
            dve.wait_ge(sem("s_soft_done"), 1)
            step(STT(s_col[S_LF], f_, 0.0, s_col[S_T], ALU.min, ALU.subtract))
            step(TT(s_col[S_INTER], s_col[S_M0], s_col[S_LF], ALU.add))
            step(TT(s_col[S_M], s_col[S_INTER], i_, ALU.max))
            step(TS(s_col[S_NM], s_col[S_M], -1.0, None, ALU.mult), "s_m_ready")
            for c in range(2):
                dve.wait_ge(sem("max_ps"), c + 1)
                for h in range(HEADS):
                    g0 = 4 * (ROW_G + c) + h
                    ins = TS(decayed[:, c, h, :], bank[2 + c][:, h * P:(h + 1) * P], gcol[:, g0:g0 + 1], 0.0,
                             ALU.subtract, ALU.max)
                    ins.then_inc(sem("lag_ready"), 1)
            dve.wait_ge(sem("s_exp_done"), 3)
            step(TS(sdiag, ident[0:STATES, 0:STATES], s_col[S_SC], None, ALU.mult))
            step(dve.tensor_tensor_reduce(srow[:, SPROD, :], srow[:, SQ, :], srow[:, SK, :], 1.0, 0.0, ALU.mult, ALU.add,
                                          s_col[S_QK]))
            step(dve.tensor_tensor_reduce(srow[:, SPROD, :], srow[:, SQ, :], srow[:, SN, :], 1.0, 0.0, ALU.mult, ALU.add,
                                          s_col[S_NQ]))
            step(TS(srow[:, SV, :], srow[:, SV, :], s_col[S_DW], None, ALU.mult))
            step(TT(s_col[S_T], s_col[S_QK], s_col[S_DW], ALU.mult))
            step(STT(s_col[S_DEN], s_col[S_NQ], s_col[S_SC], s_col[S_T], ALU.mult, ALU.add), "sdiag_ready")
            empty_tile(14)
            for c in range(2):
                dve.wait_ge(sem("decay_act"), c + 1)
                step(TT(decayed[:, c], decayed[:, c], cst[:, C_CAUSAL:C_CAUSAL + P].unsqueeze(1)
                        .to_broadcast([P, HEADS, P]), ALU.mult))
                dve.wait_ge(sem("score_ps"), c + 1)
                step(TT(decayed[:, c], decayed[:, c], bank[4 + c][:, :].rearrange("p (h t) -> p h t", h=HEADS),
                        ALU.mult), "decayed_ready")
                if c == 0:
                    dve.wait_ge(sem("rows_ready"), 1)
                    step(TT(vweighted, vtok[:, 0], gcol[:, 4 * ROW_WK:4 * ROW_WK + 4].unsqueeze(2)
                            .to_broadcast([P, HEADS, P]), ALU.mult), "vw_ready")

            def head(c, num, dsum):
                e0 = 4 * (ROW_EMT + c)
                step(STT(den2, dsum, -1.0, dsum, ALU.mult, ALU.max))
                step(TT(den2, den2, gcol[:, e0:e0 + 4], ALU.max))
                step(dve.reciprocal(den2, den2))
                ins = TT(hout[:, c], num, den2.unsqueeze(2).to_broadcast([P, HEADS, P]), ALU.mult)
                step(ins)
                for h in range(HEADS):
                    step(dve.bn_stats(h_bn, hout[:, c, h, :]))
                    step(dve.bn_aggr(h_mv[:, h, :], h_bn), "h_mv_ready" if h == 3 else "dve_chain")
                step(TT(hout[:, c], hout[:, c], h_mv[:, :, 0:1].to_broadcast([P, HEADS, P]), ALU.subtract))
                dve.wait_ge(sem("h_rstd"), c + 1)
                step(dve.reciprocal(h_rstd, h_rstd))
                step(TT(hout[:, c], hout[:, c], h_rstd.unsqueeze(2).to_broadcast([P, HEADS, P]), ALU.mult),
                     "hn_ready")

            dve.wait_ge(sem("num_ps"), 1)
            dve.wait_ge(sem("mem_ps"), 1)
            step(dve.tensor_copy(den, bank[3][:, 0:4]))
            step(dve.tensor_copy(nstate, bank[3][:, 4:8]))
            step(dve.tensor_copy(CT, bank[4][:, :].rearrange("p (h d) -> p h d", h=HEADS)), "ct_ready")
            step(TT(vweighted, vtok[:, 1], gcol[:, 4 * ROW_WK + 4:4 * ROW_WK + 8].unsqueeze(2)
                    .to_broadcast([P, HEADS, P]), ALU.mult), "vw_ready")
            step(dve.tensor_copy(hout[:, 0], bank[2][:, :].rearrange("p (h t) -> p h t", h=HEADS)), "num_done")
            head(0, hout[:, 0], den)
            dve.wait_ge(sem("sbc_ps"), 1)
            step(dve.tensor_copy(scol[:, 0:2, :], bank[6][:, 0:2 * STATES].rearrange("p (i s) -> p i s", i=2)),
                 "sbc_done")
            dve.wait_ge(sem("num_ps"), 2)
            sc1 = gcol[:, 4 * ROW_SC:4 * ROW_SC + 4]
            step(TT(hout[:, 1], bank[2][:, :].rearrange("p (h t) -> p h t", h=HEADS),
                    sc1.unsqueeze(2).to_broadcast([P, HEADS, P]), ALU.mult))
            step(TT(hout[:, 1], hout[:, 1], bank[5][:, :].rearrange("p (h t) -> p h t", h=HEADS), ALU.add))
            step(TT(den, bank[3][:, 12:16], sc1, ALU.mult))
            step(TT(den, den, bank[3][:, 8:12], ALU.add), "num_done")
            head(1, hout[:, 1], den)
            dve.wait_ge(sem("mem_ps"), 2)
            step(TT(CT, CT, dec_b.unsqueeze(2).to_broadcast([P, HEADS, P]), ALU.mult))
            step(TT(CT, CT, bank[4][:, :].rearrange("p (h d) -> p h d", h=HEADS), ALU.add))
            step(TT(nstate, nstate, dec_b, ALU.mult))
            step(TT(nstate, nstate, bank[3][:, 16:20], ALU.add), "ct_ready")
            dve.wait_ge(sem("qb_in"), 16)
            dve.wait_ge(sem("C_in"), 16)
            step(TT(qb, qb, Cst, ALU.mult))
            step(dve.tensor_reduce(scol[:, 2, :], qb, AX.X, ALU.add), "scq_ready")
            def mix_heads(c):
                dve.wait_ge(sem("hT_ps"), c + 1)
                if c == 0:
                    dve.wait_ge(sem("tile_act"), 12)
                for h in range(HEADS):
                    ins = STT(mixT[:, 4 + h, c * P:(c + 1) * P], bank[6][:, h * P:(h + 1) * P], mhg[:, h:h + 1],
                              proj[:, 16 + h, c * P:(c + 1) * P], ALU.mult, ALU.mult)
                ins.then_inc(sem("hT_done"), 1)

            mix_heads(0)
            dve.wait_ge(sem("scq_ps"), 1)
            step(TS(srow[:, SCQ, :], bank[7][0:STATES, 0:P], s_col[S_SC], None, ALU.mult))
            step(STT(srow[:, SY, :], srow[:, SV, :], s_col[S_QK], srow[:, SCQ, :], ALU.mult, ALU.add))
            step(STT(s_col[S_T], s_col[S_DEN], -1.0, s_col[S_DEN], ALU.mult, ALU.max))
            step(TT(s_col[S_T], s_col[S_T], s_col[S_EMT], ALU.max))
            step(dve.reciprocal(s_col[S_R], s_col[S_T]))
            step(TS(srow[:, SY, :], srow[:, SY, :], s_col[S_R], None, ALU.mult))
            step(dve.bn_stats(s_bn, srow[:, SY, :]))
            step(dve.bn_aggr(s_mv, s_bn), "s_mv_ready")
            mix_heads(1)
            dve.wait_ge(sem("s_rstd"), 1)
            step(dve.reciprocal(s_col[S_RSTD], s_col[S_RSTD]))
            step(TS(srow[:, SY, :], srow[:, SY, :], s_mv[:, 0:1], s_col[S_RSTD], ALU.subtract, ALU.mult), "sh_ready")
            step(TS(srow[:, SPROD, :], srow[:, SK, :], s_col[S_DW], None, ALU.mult))
            step(STT(srow[:, SN, :], srow[:, SN, :], s_col[S_SC], srow[:, SPROD, :], ALU.mult, ALU.add), "sn_ready")
            dve.wait_ge(sem("shT_ps"), 1)
            for h in range(HEADS):
                ins = STT(mixT[:, 4 + h, SEQ:TOK],
                          bank[7][:, P:P + STATES].rearrange("p (b h) -> p h b", h=HEADS)[:, h, :], mhg[:, h:h + 1],
                          proj[:, 16 + h, SEQ:TOK], ALU.mult, ALU.mult)
            ins.then_inc(sem("shT_done"), 1)

            def layer_norm(c, n, name, ready):
                x = xtok[0:n, c, :]
                for half in range(2):
                    step(dve.bn_stats(ln_bn[0:n, 6 * half:6 * half + 6], x[:, 512 * half:512 * half + 512]))
                step(dve.bn_aggr(ln_mv[0:n, :], ln_bn[0:n, :]), name + "_mv")
                dve.wait_ge(sem(name + "_rstd"), c + 1)
                step(dve.reciprocal(ln_rstd[0:n, :], ln_rstd[0:n, :]))
                step(TS(x, x, ln_mv[0:n, 0:1], ln_rstd[0:n, :], ALU.subtract, ALU.mult))
                step(TT(x, x, lnreg[0:n, 0:D], ALU.mult))
                step(TT(x, x, lnreg[0:n, D:2 * D], ALU.add), ready)

            dve.wait_ge(sem("ln1_in"), 32)
            for c, (t0, n) in enumerate(CHUNKS):
                dve.wait_ge(sem("x_again"), 48)
                for half in range(2):
                    dve.wait_ge(sem("mix_ps"), 2 * c + half + 1)
                    x = xtok[0:n, c, 512 * half:512 * half + 512]
                    step(STT(x, x, ALPHA, bank[2 * c + half][0:n, :], ALU.mult, ALU.add))
                layer_norm(c, n, "ln1", "x1_ready")

            step(dve.memset(pos_table, FAR))
            step(dve.memset(val_table, 0.0))

            def route(c):
                t0, n = CHUNKS[c]
                dve.wait_ge(sem("logits_ps"), c + 1)
                step(dve.tensor_copy(logits[0:n, :], bank[c][0:n, 0:EXPERTS]))
                step(dve.max(top[0:n, :], logits[0:n, :]))
                step(dve.max_index(idx8[0:n, :], top[0:n, :], logits[0:n, :]))
                step(TS(gsum[0:n, 0:1], top[0:n, 0:1], -1.0, None, ALU.mult), "top_ready")
                step(dve.tensor_copy(idx4[0:n, :], idx8[0:n, 0:TOPK]))
                step(TT(oh4[0:n], cst[0:n, C_EXP:C_EXP + EXPERTS].unsqueeze(1).to_broadcast([n, TOPK, EXPERTS]),
                        idx4[0:n, :].unsqueeze(2).to_broadcast([n, TOPK, EXPERTS]), ALU.is_equal))
                step(dve.tensor_reduce(mask[0:n, c, :], oh4[0:n].rearrange("p k e -> p e k"), AX.X, ALU.add),
                     "mask_ready")
                step(TT(oh4v[0:n], oh4[0:n], cst[0:n, C_RANK + TOPK * c:C_RANK + TOPK * c + TOPK].unsqueeze(2)
                        .to_broadcast([n, TOPK, EXPERTS]), ALU.mult))
                step(dve.tensor_reduce(vrow[0:n, 0, :], oh4v[0:n].rearrange("p k e -> p e k"), AX.X, ALU.add))
                dve.wait_ge(sem("top_exp"), c + 1)
                step(dve.tensor_reduce(gsum[0:n, 1:2], gate4[0:n, :], AX.X, ALU.add))
                step(dve.reciprocal(gsum[0:n, 2:3], gsum[0:n, 1:2]))
                step(TS(gate4[0:n, :], gate4[0:n, :], gsum[0:n, 2:3], None, ALU.mult))
                step(TT(oh4v[0:n], oh4[0:n], gate4[0:n, :].unsqueeze(2).to_broadcast([n, TOPK, EXPERTS]), ALU.mult))
                step(dve.tensor_reduce(vrow[0:n, 1, :], oh4v[0:n].rearrange("p k e -> p e k"), AX.X, ALU.add))
                for v in range(2):
                    table = val_table[0:n, c, 0:PASSES * EXPERTS, v].rearrange("p (b e) -> p b e", b=PASSES)
                    step(dve.tensor_copy(table, vrow[0:n, v, :].unsqueeze(1).to_broadcast([n, PASSES, EXPERTS])))

            for c, (t0, n) in enumerate(CHUNKS):
                for half in range(2):
                    dve.wait_ge(sem("x1T_ps"), 2 * c + half + 1)
                    dve.tensor_copy(x1T[:, 4 * half:4 * half + 4, t0:t0 + n],
                                    bank[6 + half][:, :].rearrange("p (k t) -> p k t", k=4)[:, :, 0:n])\
                       .then_inc(sem("x1T_done"), 1)
                route(c)
            dve.wait_ge(sem("pos_ps"), 1)
            step(dve.tensor_reduce(gsum[:, 0:1], bank[4][:, 0:EXPERTS], AX.X, ALU.max))
            step(TS(gate4, cst[:, C_LIM:C_LIM + 4], gsum[:, 0:1], None, ALU.is_lt))
            step(dve.tensor_reduce(gsum[:, 1:2], gate4, AX.X, ALU.add))
            step(dve.tensor_copy(extra[:, :], gsum[:, 1:2]), "passes_ready")
            for c, (t0, n) in enumerate(CHUNKS):
                step(STT(posm[0:n, :], mask[0:n, c, :], -FAR, bank[3][0:n, c * EXPERTS:(c + 1) * EXPERTS],
                         ALU.mult, ALU.add))
                table = pos_table[0:n, c, 0:PASSES * EXPERTS].rearrange("p (b e) -> p b e", b=PASSES)
                step(TT(table, posm[0:n, :].unsqueeze(1).to_broadcast([n, PASSES, EXPERTS]),
                        cst[0:n, C_BLK:C_BLK + PASSES].unsqueeze(2).to_broadcast([n, PASSES, EXPERTS]), ALU.add))

            def one_hot(n, parity):
                TT(onehot, cst[:, C_SLOT:C_SLOT + P].unsqueeze(1).to_broadcast([P, 3, P]),
                   pos_table[:, :, bass.ds(n, 1)].to_broadcast([P, 3, P]), ALU.is_equal).then_inc(sem("onehot_ready"), 1)
                dve.tensor_copy(info, val_table[:, :, bass.ds(n, 1), :].rearrange("p c o v -> p c (o v)"))\
                   .then_inc(sem("onehot_ready"), 1)
                dve.tensor_copy(sel[:, parity, :], cst[0:3 * EXPERTS, bass.ds(n + C_SEL, 1)]
                                .to_broadcast([3 * EXPERTS, BLOCK])).then_inc(sem("onehot_ready"), 1)

            def gathered(n, parity):
                dve.wait_ge(sem("gathered"), n + 1)
                TS(erow[:, parity:parity + 1], bank[5][:, 0:1], 2.0, cst[:, C_HALF:C_HALF + 1], ALU.mult, ALU.add)\
                    .then_inc(sem("xg_done"), 1)
                dve.tensor_copy(egate[:, parity:parity + 1], bank[5][:, 1:2]).then_inc(sem("xg_done"), 1)
                dve.tensor_copy(xgT, bank[2][:, :].rearrange("p (k s) -> p k s", k=KD)).then_inc(sem("xg_done"), 1)

            def expert(n, j):
                dve.wait_ge(sem("gathered"), n + 1)
                dve.wait_ge(sem("out_done"), n + 1)
                one_hot(n + 1, (j + 1) % 2)
                dve.wait_ge(sem("units_used"), n * UNITS + 8)
                hb = [bank[q][:, :].rearrange("p (f two) -> p two f", two=2) for q in range(2)]
                for q in range(2):
                    TS(glu[:, q, :], hb[q][:, 0, :], LIMIT, None, ALU.min).then_inc(sem("glu_ready"), 1)
                for q in range(2):
                    TS(lin[:, q, :], hb[q][:, 1, :], LIMIT, -LIMIT, ALU.min, ALU.max).then_inc(sem("lin_ready"), 1)
                dve.wait_ge(sem("lin_ready"), (n + 1) * 2)
                dve.wait_ge(sem("glu_ready"), (n + 1) * 2)
                STT(lin, lin, 1.0, glu, ALU.add, ALU.mult).then_inc(sem("h_read"), 1)
                dve.wait_ge(sem("h_read"), n + 2)
                dve.wait_ge(sem("sig_ready"), n + 1)
                TT(act_out.rearrange("p (q f) -> p q f", q=2), lin, sig, ALU.mult).then_inc(sem("act_ready"), 1)
                dve.wait_ge(sem("rows_left"), n + 1)
                gathered(n + 1, (j + 1) % 2)

            dve.wait_ge(sem("dve_chain"), counts["dve_chain"])
            dve.engine_nop().then_inc(sem("h_read"), 1)
            one_hot(0, 0)
            gathered(0, 0)
            dve.wait_ge(sem("passes_ready"), 1)
            npass = dve.value_load(extra[0:1, 0:1], min_val=0, max_val=PASSES - 1) + 1
            with dve.Fori(0, npass * EXPERTS, STEP) as n:
                for j in range(STEP):
                    expert(n + j, j)

            pT = ring[:, 9, 768:768 + 2 * TOK].rearrange("p (k n) -> p k n", k=2)
            for c, (t0, n) in enumerate(CHUNKS):
                dve.wait_ge(sem("pT_ps"), c + 1)
                dve.tensor_copy(pT[:, :, t0:t0 + n], bank[c][:, 0:2 * P].rearrange("p (k t) -> p k t", k=2)[:, :, 0:n])\
                   .then_inc(sem("pT_done"), 1)
            dve.wait_ge(sem("ln2_in"), 32)
            for c, (t0, n) in enumerate(CHUNKS):
                f = slots(10 + 2 * c, 2, 4096)[0:n, :].rearrange("p (k d) -> p k d", k=TOPK)
                dve.wait_ge(sem(f"ff_in{c}"), 16)
                step(TT(f[:, 0:2, :], f[:, 0:2, :], f[:, 2:4, :], ALU.add))
                step(STT(xtok[0:n, c, :], xtok[0:n, c, :], ALPHA, f[:, 0, :], ALU.mult, ALU.add))
                step(TT(xtok[0:n, c, :], xtok[0:n, c, :], f[:, 1, :], ALU.add))
                layer_norm(c, n, "ln2", "x2_ready")
                for half in range(2):
                    dve.wait_ge(sem("x2T_ps"), 2 * c + half + 1)
                    dve.tensor_copy(x1T[:, 4 * half:4 * half + 4, t0:t0 + n],
                                    bank[6 + half][:, :].rearrange("p (k t) -> p k t", k=4)[:, :, 0:n])\
                       .then_inc(sem("x2T_done"), 1)
            for c, (t0, n) in enumerate(CHUNKS):
                f = slots(10 + 2 * c, 2, 4096)[0:n, :].rearrange("p (k d) -> p k d", k=TOPK)
                dve.wait_ge(sem("sig_done"), 2 * c + 2)
                dve.wait_ge(sem("ple_done"), 2 * c + 2)
                ple = ring[0:n, c, 0:D]
                step(TT(f[:, 0, :], f[:, 0, :], ple, ALU.mult))
                step(TT(xtok[0:n, c, :], xtok[0:n, c, :], f[:, 0, :], ALU.add), "y_done")

        @block.scalar
        def _(act):
            act.dma_start(cst[:, :], consts).then_inc(sem("cst_in"), 16)
            act.dma_start(wgate[:, :, :], w_in[0, :, 2560:2568].rearrange("(k p) n -> p k n", p=P))\
               .then_inc(sem("wgate_in"), 16)
            act.dma_start(hist[0:SAMPLES * HIST, :], state_pool[0].rearrange("b r d -> (b r) d"))\
               .then_inc(sem("hist_in"), 16)
            act.dma_start(gbias[0:HEADS, :], b_i.rearrange("o h -> h o")).then_inc(sem("gbias_in"), 16)
            act.dma_start(gbias[HEADS:2 * HEADS, :], b_f.rearrange("o h -> h o")).then_inc(sem("gbias_in"), 16)

            for g in (1, 3, 5):
                c = g // 2
                t0, n = CHUNKS[c]
                act.wait_ge(sem("xT_ps"), g + 1)
                act.copy(xT[:, 4:8, t0:t0 + n], bank[g][:, :].rearrange("p (k t) -> p k t", k=4)[:, :, 0:n])\
                   .then_inc(sem("xT_act"), 1)
            act.wait_ge(sem("gates_ps"), 1)
            act.wait_ge(sem("gbias_in"), 32)
            act.activation(gates[:, :], bank[6][0:2 * HEADS, 0:TOK], ACT.Identity, bias=gbias).then_inc(sem("gates_done"), 1)
            act.dma_start(srow[:, SN, :], state_n[0].rearrange("b h k -> (b h) k")).then_inc(sem("states_in"), 16)
            act.dma_start(s_col[S_M0], state_m.rearrange("o b h -> (b h) o")).then_inc(sem("states_in"), 16)
            act.dma_start(wpool[:, :, :], w_pool[0].rearrange("g c d -> c g d")).then_inc(sem("wpool_in"), 16)
            act.dma_start(pscale, pool_scale[0].rearrange("(g d) -> d g", d=P)).then_inc(sem("cols_in"), 16)
            act.dma_start(mhg, mh_g[0].rearrange("(g d) -> d g", d=P)).then_inc(sem("cols_in"), 16)
            act.dma_start(wrout[:, :, :], w_router[0].rearrange("(k p) e -> p k e", p=P)).then_inc(sem("wrout_in"), 16)
            act.dma_start(brout[:, :], b_router).then_inc(sem("wrout_in"), 16)

            def empty_tile(t):
                act.wait_ge(sem("tile_ps"), t + 1)
                if t >= 16:
                    ins = act.activation(proj[:, t, :], bank[t % 2][:, 0:TOK], ACT.Sigmoid)
                elif 4 <= t < 8:
                    ins = act.activation(proj[:, t, :], bank[t % 2][:, 0:TOK], ACT.Copy, scale=K_SCALE)
                else:
                    ins = act.copy(proj[:, t, :], bank[t % 2][:, 0:TOK])
                ins.then_inc(sem("tile_act"), 1)

            one = ones[0:HEADS, 0:1]
            act.wait_ge(sem("softp_ready"), 1)
            act.activation(softp, softp, ACT.Exp).then_inc(sem("softp_exp"), 1)
            empty_tile(1)
            act.wait_ge(sem("softp_exp"), 1)
            act.activation(softp, softp, ACT.Ln, bias=one).then_inc(sem("softp_done"), 1)
            empty_tile(3)
            act.wait_ge(sem("runmax_ready"), 2)
            act.activation(rows[:, ROW_EMT:ROW_EMT + 2, :], rows[:, ROW_EMT:ROW_EMT + 2, :], ACT.Exp, scale=-1.0)\
               .then_inc(sem("rows_parts"), 1)
            for c in range(2):
                act.activation(rows[:, ROW_WK + c, :], rows[:, ROW_G + c, :], ACT.Exp, bias=nlast[:, c:c + 1])\
                   .then_inc(sem("rows_parts"), 1)
            act.activation(rows[:, ROW_SC, :], runmax[:, P:2 * P], ACT.Exp, bias=m1, scale=-1.0).then_inc(sem("rows_parts"), 1)
            act.wait_ge(sem("rows_parts"), 4)
            act.nop().then_inc(sem("rows_act"), 1)
            empty_tile(5)
            empty_tile(7)
            act.wait_ge(sem("ktok_ps"), 2)
            act.copy(ktok[:, 1], bank[5][:, :].rearrange("p (h d) -> p h d", h=HEADS)).then_inc(sem("ktok_done"), 1)
            empty_tile(9)
            empty_tile(11)
            act.wait_ge(sem("vtok_ps"), 2)
            act.copy(vtok[:, 1], bank[3][:, :].rearrange("p (h d) -> p h d", h=HEADS)).then_inc(sem("vtok_done"), 1)
            act.wait_ge(sem("s_soft_ready"), 1)
            act.activation(s_col[S_T], s_col[S_T], ACT.Exp).then_inc(sem("s_soft_exp"), 1)
            act.wait_ge(sem("s_soft_exp"), 1)
            act.activation(s_col[S_T], s_col[S_T], ACT.Ln, bias=ones[0:STATES, 0:1]).then_inc(sem("s_soft_done"), 1)
            empty_tile(13)
            act.wait_ge(sem("s_m_ready"), 1)
            for src, dst in ((s_gate[:, 0:1], S_DW), (s_col[S_INTER], S_SC)):
                act.activation(s_col[dst], src, ACT.Exp, bias=s_col[S_NM]).then_inc(sem("s_exp_done"), 1)
            act.activation(s_col[S_EMT], s_col[S_M], ACT.Exp, scale=-1.0).then_inc(sem("s_exp_done"), 1)
            for c in range(2):
                act.wait_ge(sem("lag_ready"), 4 * (c + 1))
                act.activation(decayed[:, c], decayed[:, c], ACT.Exp, scale=-1.0).then_inc(sem("decay_act"), 1)
            empty_tile(15)

            def pool_group(g):
                act.wait_ge(sem("pool_ps"), g + 1)
                if g == 0:
                    act.wait_ge(sem("cols_in"), 32)
                act.activation(mixT[:, g, :], bank[7][:, 0:TOK], ACT.Copy, scale=pscale[:, g:g + 1])\
                   .then_inc(sem("pool_done"), 1)

            def root(out_, in_, name):
                act.activation(out_, in_, ACT.Sqrt, bias=eps[0:in_.shape[0], :]).then_inc(sem(name), 1)

            for g in range(4):
                pool_group(g)
                empty_tile(16 + g)
            act.wait_ge(sem("h_mv_ready"), 1)
            root(h_rstd, h_mv[:, :, 1], "h_rstd")
            act.wait_ge(sem("h_mv_ready"), 2)
            act.wait_ge(sem("hn_ready"), 1)
            root(h_rstd, h_mv[:, :, 1], "h_rstd")
            act.wait_ge(sem("s_mv_ready"), 1)
            root(s_col[S_RSTD], s_mv[:, 1:2], "s_rstd")
            act.wait_ge(sem("cfin_ps"), 1)
            act.copy(CT, bank[4][:, :].rearrange("p (h d) -> p h d", h=HEADS)).then_inc(sem("cfin_done"), 1)
            act.copy(ncol_out[:, :], bank[5][0:HEADS, 0:P]).then_inc(sem("cfin_done"), 1)
            act.copy(urow[:, :], bank[2][0:HIST + SAMPLES, :]).then_inc(sem("cfin_done"), 1)
            for c, (t0, n) in enumerate(CHUNKS):
                act.wait_ge(sem("ln1_mv"), c + 1)
                if c:
                    act.wait_ge(sem("x1_ready"), c)
                root(ln_rstd[0:n, :], ln_mv[0:n, 1:2], "ln1_rstd")
            for c, (t0, n) in enumerate(CHUNKS):
                act.wait_ge(sem("top_ready"), c + 1)
                act.activation(gate4[0:n, :], top[0:n, 0:TOPK], ACT.Exp, bias=gsum[0:n, 0:1]).then_inc(sem("top_exp"), 1)

            def expert(n, j):
                act.wait_ge(sem("glu_ready"), n * 2 + 2)
                act.activation(sig, glu, ACT.Sigmoid, scale=SIG).then_inc(sem("sig_ready"), 1)
                act.wait_ge(sem("aT_ps"), n + 1)
                act.copy(aT, bank[3][:, :].rearrange("p (m s) -> p m s", m=4)).then_inc(sem("aT_done"), 1)
                act.wait_ge(sem("units_used"), n * UNITS + UNITS)
                act.wait_ge(sem("rows_left"), n + 1)
                act.activation(eout[:, j % 2, :], bank[4][:, :], ACT.Copy, scale=egate[:, j % 2:j % 2 + 1])\
                   .then_inc(sem("out_done"), 1)

            act.nop().then_inc(sem("out_done"), 1)
            act.wait_ge(sem("passes_ready"), 1)
            npass = act.value_load(extra[0:1, 0:1], min_val=0, max_val=PASSES - 1) + 1
            with act.Fori(0, npass * EXPERTS, STEP) as n:
                for j in range(STEP):
                    expert(n + j, j)

            for c, (t0, n) in enumerate(CHUNKS):
                for half in range(2):
                    act.wait_ge(sem("ple_ps"), 2 * c + half + 1)
                    act.copy(ring[0:n, c, 512 * half:512 * half + 512], bank[4 + half][0:n, :])\
                       .then_inc(sem("ple_done"), 1)
            for c, (t0, n) in enumerate(CHUNKS):
                act.wait_ge(sem("ln2_mv"), c + 1)
                if c:
                    act.wait_ge(sem("x2_ready"), c)
                root(ln_rstd[0:n, :], ln_mv[0:n, 1:2], "ln2_rstd")
            for c, (t0, n) in enumerate(CHUNKS):
                f = slots(10 + 2 * c, 2, 4096)[0:n, :]
                for half in range(2):
                    act.wait_ge(sem("gate_ps"), 2 * c + half + 1)
                    act.activation(f[:, 512 * half:512 * half + 512], bank[(2 * c + half) % 4][0:n, :], ACT.Sigmoid)\
                       .then_inc(sem("sig_done"), 1)

        @block.gpsimd
        def _(pool):
            chain = [0]

            def step(ins):
                chain[0] += 1
                ins.then_inc(sem("pool_chain"), 1)
                pool.wait_ge(sem("pool_chain"), chain[0])

            step(pool.memset(window[:, :, 0:16], 0.0))
            pool.wait_ge(sem("bias_in"), 96)
            for part_ in range(3):
                for g in range(part_, 3):
                    r = slice(g * EXPERTS, (g + 1) * EXPERTS)
                    step(pool.tensor_copy(bias_parts[r, :], bsrc[r, :]))
                for g in range(part_ + 1, 3):
                    r = slice(g * EXPERTS, (g + 1) * EXPERTS)
                    step(pool.tensor_tensor(bsrc[r, :], bsrc[r, :], bias_parts[r, :], ALU.subtract))
            pool.engine_nop().then_inc(sem("bias_split"), 1)

            for g, w in enumerate(WINDOWS):
                u = proj[:, 12 + g, :]
                name, count = tile_done(12 + g)
                pool.wait_ge(sem(name), count)
                step(pool.tensor_copy(window[:, 0, 16:], u[:, 0:SEQ]))
                src, shift = 0, 1
                while shift < w:
                    step(pool.tensor_tensor(window[:, 1 - src, 16:], window[:, src, 16:],
                                            window[:, src, 16 - shift:16 + SEQ - shift], ALU.add))
                    src, shift = 1 - src, 2 * shift
                first = window[:, src, 16:32]
                step(pool.tensor_tensor(first, first, cst[:, C_CNT + 16 * g:C_CNT + 16 * g + 16], ALU.mult))
                if g == 0:
                    pool.wait_ge(sem("hist_done"), 1)
                hs = histsum[:, g * SAMPLES:(g + 1) * SAMPLES]
                step(pool.tensor_tensor(hs, hs, u[:, SEQ:TOK], ALU.add))
                step(pool.tensor_scalar(hs, hs, 1.0 / w, None, ALU.mult))
                step(pool.tensor_scalar(window[:, src, 16:], window[:, src, 16:], 1.0 / w, None, ALU.mult))
                step(pool.tensor_copy(ukeep[:, g, 0:HIST], u[:, SEQ - HIST:SEQ]))
                step(pool.tensor_copy(ukeep[:, g, HIST:HIST + SAMPLES], u[:, SEQ:TOK]))
                step(pool.tensor_tensor(u[:, SEQ:TOK], hs, u[:, SEQ:TOK], ALU.subtract))
                step(pool.tensor_tensor(u[:, 0:SEQ], window[:, src, 16:], u[:, 0:SEQ], ALU.subtract))
                pool.engine_nop().then_inc(sem("z_ready"), 1)

            pool.wait_ge(sem("sbc_done"), 1)
            pool.wait_ge(sem("kb_in"), 16)
            step(pool.tensor_tensor(kb, kb, scol[:, 1, :].unsqueeze(2).to_broadcast([P, STATES, HD]), ALU.mult))
            pool.wait_ge(sem("scq_ready"), 1)
            step(pool.tensor_tensor(Cst, Cst, scol[:, 0, :].unsqueeze(2).to_broadcast([P, STATES, HD]), ALU.mult))
            step(pool.tensor_tensor(Cst, Cst, kb, ALU.add))
            pool.engine_nop().then_inc(sem("Cnew_done"), 1)
            pool.dma_start(C_sample[0].rearrange("b h v k -> v (b h) k"), Cst).then_inc(sem("C_out"), 16)
            pool.wait_ge(sem("cfin_done"), 3)
            pool.dma_start(pool_prompt[0, 0], urow[0:HIST, :]).then_inc(sem("small_out"), 16)
            pool.dma_start(pool_sample[0, :, HIST - 1, :], urow[HIST:HIST + SAMPLES, :]).then_inc(sem("small_out"), 16)
            pool.dma_start(C_prompt[0, 0].rearrange("h v k -> v h k"), CT).then_inc(sem("small_out"), 16)
            pool.dma_start(n_prompt[0, 0], ncol_out[:, :]).then_inc(sem("small_out"), 16)
            pool.dma_start(m_prompt[0].rearrange("b h -> h b"), m2).then_inc(sem("small_out"), 16)
            pool.wait_ge(sem("sn_ready"), 1)
            pool.dma_start(n_sample[0].rearrange("b h k -> (b h) k"), srow[:, SN, :]).then_inc(sem("small_out"), 16)
            pool.dma_start(m_sample.rearrange("o b h -> (b h) o"), s_col[S_M]).then_inc(sem("small_out"), 16)
            pool.dma_start(pool_sample[0, :, 0:HIST - 1, :], state_pool[0, :, 1:HIST, :]).then_inc(sem("small_out"), 16)
            pool.wait_ge(sem("hT_ps"), 2)
            step(pool.memset(xtok[:, 2, :], 0.0))
            for c, (t0, n) in enumerate(CHUNKS):
                src = x_prompt[0, t0:t0 + n, :] if c < 2 else x_sample[:, 0, :]
                pool.dma_start(xtok[0:n, c, :], src).then_inc(sem("x_again"), 16)
            pool.wait_ge(sem("small_out"), 16 * SMALL_OUTS)
            pool.dma_start(lnreg[:, 0:D], ln1_g.partition_broadcast(P).rearrange("p o d -> p (o d)"))\
                .then_inc(sem("ln1_in"), 16)
            pool.dma_start(lnreg[:, D:2 * D], ln1_b.partition_broadcast(P).rearrange("p o d -> p (o d)"))\
                .then_inc(sem("ln1_in"), 16)
            pool.wait_ge(sem("ln1_in"), 32)
            pool.wait_ge(sem("x1_ready"), 3)
            pool.dma_start(lnreg[:, 0:D], ln2_g.partition_broadcast(P).rearrange("p o d -> p (o d)"))\
                .then_inc(sem("ln2_in"), 16)
            pool.dma_start(lnreg[:, D:2 * D], ln2_b.partition_broadcast(P).rearrange("p o d -> p (o d)"))\
                .then_inc(sem("ln2_in"), 16)

            def expert(n, j):
                pool.wait_ge(sem("out_done"), n + 2)
                pool.wait_ge(sem("xg_done"), n * 3 + 3)
                pool.sem_inc(sem("scatters"), 1)
                pool.indirect_dma_start(out=ff_rows, out_offset=bass.IndirectOffsetOnAxis(
                    ap=erow[:, j % 2:j % 2 + 1], axis=0), in_=eout[:, j % 2, :], in_offset=None,
                    bounds_check=last_row, oob_is_err=False).then_inc(sem("rows_out"), 16)
                pool.wait_ge(sem("rows_out"), n * 16 + 16)
                pool.sem_inc(sem("rows_left"), 1)

            pool.engine_nop().then_inc(sem("rows_left"), 1)
            pool.wait_ge(sem("passes_ready"), 1)
            last_row = pool.alloc_register("last_row")
            pool.reg_mov(last_row, TOK * TOPK * 2 - 1)
            npass = pool.value_load(extra[0:1, 0:1], min_val=0, max_val=PASSES - 1) + 1
            with pool.Fori(0, npass * EXPERTS, STEP) as n:
                for j in range(STEP):
                    expert(n + j, j)


INPUTS = ["x_prompt", "x_sample", "state_pool", "state_mlstm_C", "state_mlstm_n", "state_mlstm_m", "p_prompt",
          "p_sample", "w_in", "b_i", "b_f", "w_pool", "pool_scale", "mh_g", "w_out", "ln1_g", "ln1_b", "w_router",
          "b_router", "w_mlp1", "b_mlp1", "w_mlp2", "b_mlp2", "ln2_g", "ln2_b", "w_ple", "w_ple_gate"]
OUTPUTS = [(1, SEQ, D), (SAMPLES, 1, D), (1, 1, HIST, 4 * P), (1, 1, HEADS, HD, HD), (1, 1, HEADS, HD), (1, 1, HEADS),
           (1, SAMPLES, HIST, 4 * P), (1, SAMPLES, HEADS, HD, HD), (1, SAMPLES, HEADS, HD), (1, SAMPLES, HEADS)]


def kernel(**inputs):
    import concourse.bacc as bacc
    from concourse.bass_utils import run_bass_kernel_spmd

    nc = bacc.Bacc("TRN2", target_bir_lowering=False, num_devices=1, dynamic_dma_scratch_size=8192)
    arrays = {"in_consts": constants()}
    for name in INPUTS:
        arrays[f"in_{name}"] = np.ascontiguousarray(inputs[name])
    args = [nc.dram_tensor(name, a.shape, mybir.dt.from_np(a.dtype), kind="ExternalInput").ap()
            for name, a in arrays.items()]
    args += [nc.dram_tensor(f"out_{i}", shape, F32, kind="ExternalOutput").ap() for i, shape in enumerate(OUTPUTS)]
    build(nc, *args)
    r = run_bass_kernel_spmd(nc, [arrays], core_ids=[0])
    return tuple(r.results[0][f"out_{i}"] for i in range(len(OUTPUTS)))
```

```python
from contextlib import ExitStack

import numpy as np
import concourse.bass as bass
from concourse import mybir

F32 = mybir.dt.float32
BF16 = mybir.dt.bfloat16
I32 = mybir.dt.int32
U32 = mybir.dt.uint32
ALU = mybir.AluOpType
ACT = mybir.ActivationFunctionType
AX = mybir.AxisListType

P = 128
D = 1024
KD = D // P
SEQ = 256
SAMPLES = 8
TOK = SEQ + SAMPLES
CHUNKS = [(0, P), (P, P), (SEQ, SAMPLES)]
HEADS = 4
HD = 128
HIST = 15
WINDOWS = (2, 4, 8, 16)
STATES = SAMPLES * HEADS
EXPERTS = 32
TOPK = 4
FF = 1024
PLE = 256
BLOCK = 64
PASSES = -(-TOK // BLOCK)
STEP = 4
TABLE = PASSES * EXPERTS + 2 * STEP
FAR = 16384.0
ALPHA = 2.0 ** 0.25
EPS = 1e-5
LIMIT = 7.0
SIG = 1.702
SLOTS = 16
SLOT = 2048
UNITS = 12
FIRST = 4
COLUMNS_IN = (0, 512, 1024, 1536, 2048)
T_U, T_Q, T_K, T_V, T_O = range(0, 20, 4)
TILES = 20
ORDER = (0, 2, 1)

C_ID, C_CAUSAL, C_BEFORE, C_ONES, C_SLOT = 0, 128, 256, 384, 512
C_EXP = 640
C_HIST = C_EXP + EXPERTS
C_CNT = C_HIST + 4 * SAMPLES
C_RANK = C_CNT + 4 * 16
C_HALF = C_RANK + 3 * TOPK
C_LIM = C_HALF + 1
C_BLK = C_LIM + 4
C_EPS = C_BLK + PASSES
C_SEL = C_EPS + 1
C_HEAD = C_SEL + TABLE
C_KIND = C_HEAD + STATES
C_END = C_KIND + 2


def constants():
    t = np.zeros((P, C_END), np.float32)
    p = np.arange(P)
    t[:, C_ID:C_ID + P] = np.eye(P)
    t[:, C_CAUSAL:C_CAUSAL + P] = p[:, None] <= p[None, :]
    t[:, C_BEFORE:C_BEFORE + P] = p[:, None] < p[None, :]
    t[:, C_ONES:C_ONES + P] = 1.0
    t[:, C_SLOT:C_SLOT + P] = (p % BLOCK)[None, :]
    t[:, C_EXP:C_EXP + EXPERTS] = np.arange(EXPERTS)
    for g, w in enumerate(WINDOWS):
        for b in range(SAMPLES):
            t[b * HIST + HIST + 1 - w:(b + 1) * HIST, C_HIST + g * SAMPLES + b] = 1.0
        t[:, C_CNT + 16 * g:C_CNT + 16 * g + 16] = w / np.minimum(np.arange(16) + 1, w)
    for c, (t0, _) in enumerate(CHUNKS):
        for k in range(TOPK):
            t[:, C_RANK + TOPK * c + k] = TOPK * (t0 + p) + k - FAR
    t[:, C_HALF] = 2 * FAR + p // BLOCK
    t[:, C_LIM:C_LIM + 4] = BLOCK * np.arange(1, 5)
    t[:, C_BLK:C_BLK + PASSES] = FAR - BLOCK * np.arange(PASSES)
    t[:, C_EPS] = EPS
    t[:, C_SEL:C_SEL + TABLE] = p[:, None] % EXPERTS == np.arange(TABLE)[None, :] % EXPERTS
    t[3 * EXPERTS:, C_SEL:C_SEL + TABLE] = 0.0
    t[:, C_HEAD:C_HEAD + STATES] = p[:, None] % HEADS == np.arange(STATES)[None, :] % HEADS
    t[:, C_KIND:C_KIND + 2] = p[:, None] // HEADS == np.arange(2)[None, :]
    return t


def build(nc, consts, x_prompt, x_sample, state_pool, state_C, state_n, state_m, p_prompt, p_sample,
          w_in, b_i, b_f, w_pool, pool_scale, mh_g, w_out, ln1_g, ln1_b, w_router, b_router,
          w_mlp1, b_mlp1, w_mlp2, b_mlp2, ln2_g, ln2_b, w_ple, w_ple_gate,
          y_prompt, y_sample, pool_prompt, C_prompt, n_prompt, m_prompt,
          pool_sample, C_sample, n_sample, m_sample):
    with ExitStack() as ctx:
        def sb(name, shape, dt=F32):
            return ctx.enter_context(nc.sbuf_tensor(name, shape, dt))

        sems = {}

        def sem(name):
            if name not in sems:
                sems[name] = ctx.enter_context(nc.semaphore(name))
            return sems[name]

        ctx.enter_context(nc.allow_non_contiguous_dma(reason="gate columns and small states"))

        ring = sb("ring", [P, SLOTS, SLOT])
        cst = sb("cst", [P, C_END])
        xreg = sb("xreg", [P, 3 * D])
        lnreg = sb("lnreg", [P, 2 * D])
        proj = sb("proj", [P, TILES, TOK])
        xT = sb("xT", [P, KD, TOK])
        mixT = sb("mixT", [P, KD, TOK])
        wgate = sb("wgate", [P, KD, 2 * HEADS])
        wpool = sb("wpool", [P, 4, P])
        hist_mix = sb("hist_mix", [P, D])
        hist = hist_mix[:, 0:4 * P]
        bias_parts = sb("bias_parts", [3 * EXPERTS, 3 * FF], BF16)
        window = sb("window", [P, 2, 16 + SEQ])
        small = sb("small", [P, 160])
        srow = sb("srow", [STATES, 7, HD])
        scol = sb("scol", [P, 4, STATES])
        stat = sb("stat", [P, 64])
        bank = [ctx.enter_context(nc.psum_tensor(f"bank{b}", [P, 512], F32)) for b in range(8)]

        ident = cst[:, C_ID:C_ID + P]
        ones = cst[:, C_ONES:C_ONES + P]
        eps = cst[:, C_EPS:C_EPS + 1]

        xtok = xreg[:, :].rearrange("p (c d) -> p c d", c=3)
        ktok = xreg[:, 0:1024].rearrange("p (c h d) -> p c h d", c=2, h=HEADS)
        vtok = xreg[:, 1024:2048].rearrange("p (c h d) -> p c h d", c=2, h=HEADS)
        decayed = xreg[:, 2048:3072].rearrange("p (c h t) -> p c h t", c=2, h=HEADS)
        hout = lnreg[:, 0:1024].rearrange("p (c h t) -> p c h t", c=2, h=HEADS)
        vweighted = lnreg[:, 1024:1536].rearrange("p (h d) -> p h d", h=HEADS)
        CT = lnreg[:, 1536:2048].rearrange("p (h d) -> p h d", h=HEADS)
        softp = lnreg[0:HEADS, 0:256]
        logf = lnreg[0:HEADS, 256:512]
        cumf = lnreg[0:HEADS, 512:768]
        runmax = lnreg[0:HEADS, 768:1024]
        rows = lnreg[0:HEADS, 1024:1024 + 7 * P].rearrange("h (q t) -> h q t", q=7)
        ROW_G, ROW_EMT, ROW_WK, ROW_SC = 0, 2, 4, 6
        maxdiag = [xreg[0:HEADS, 2048 + 512 * c:2560 + 512 * c].rearrange("p (h t) -> p h t", h=HEADS)
                   for c in range(2)]
        gates = sb("gates", [2 * HEADS, TOK])
        fgate = sb("fgate", [HEADS, SEQ])
        gcol = small[:, 0:28]
        dec_b = small[:, 28:32]
        nstate = small[:, 32:36]
        nout = small[0:HEADS, 36:37]
        m1 = small[0:HEADS, 37:38]
        m2 = small[0:HEADS, 38:39]
        nlast = small[0:HEADS, 39:41]
        ddiag = small[0:HEADS, 41:45]
        mhg = small[:, 45:49]
        pscale = small[:, 49:53]
        gbias = small[0:2 * HEADS, 53:54]
        histsum = small[:, 94:126]
        den = small[:, 86:90]
        den2 = small[:, 90:94]
        brout = sb("brout", [1, EXPERTS])
        ncol_out = sb("ncol_out", [HEADS, HD])
        s_gate = stat[0:STATES, 0:2]
        s_col = [stat[0:STATES, 2 + i:3 + i] for i in range(14)]
        (S_M0, S_LF, S_INTER, S_M, S_NM, S_DW, S_SC, S_EMT, S_QK, S_NQ, S_DEN, S_R, S_T, S_RSTD) = range(14)
        s_bn = stat[0:STATES, 16:22]
        s_mv = stat[0:STATES, 22:24]
        h_bn = sb("h_bn", [P, HEADS, 6])
        h_mv = stat[:, 30:38].rearrange("p (h m) -> p h m", h=HEADS)
        h_rstd = stat[:, 38:42]
        ln_bn = stat[:, 42:54]
        ln_mv = stat[:, 54:56]
        ln_rstd = stat[:, 56:57]
        sdiag = scol[0:STATES, 3, :]
        scq = sb("scq", [P, STATES])[:, :]
        s_spread = small[0:2 * HEADS, 54:86]
        ukeep = sb("ukeep", [P, 4, HIST + SAMPLES])
        urow = sb("urow", [HIST + SAMPLES, 4 * P])
        SMALL_OUTS = 8
        Cfin = window[:, :, :].rearrange("p a t -> p (a t)")[:, 0:512].rearrange("p (h d) -> p h d", h=HEADS)
        mix2 = hist_mix[0:SAMPLES, :]
        SQ, SK, SV, SN, SCQ, SY, SPROD = range(7)

        def slots(s, n, width):
            return ring[:, s:s + n, :].rearrange("p s f -> p (s f)")[:, 0:width]

        Cst = slots(10, 2, STATES * HD).rearrange("p (s k) -> p s k", s=STATES)
        qb = slots(12, 2, STATES * HD).rearrange("p (s k) -> p s k", s=STATES)
        kb = slots(14, 2, STATES * HD).rearrange("p (s k) -> p s k", s=STATES)
        bsrc = ring[0:3 * EXPERTS, 14:16, :].rearrange("p s f -> p (s f)")[:, 0:3 * FF]

        moe = proj[:, :, :].rearrange("p t n -> p (t n)")
        off = [0]

        def part(n):
            off[0] += n
            return moe[:, off[0] - n:off[0]]

        info = part(6).rearrange("p (c v) -> p c v", c=3)
        logits = part(EXPERTS)
        top = part(8)
        gate4 = part(4)
        idx4 = part(4)
        gsum = part(4)
        oh4 = part(TOPK * EXPERTS).rearrange("p (k e) -> p k e", k=TOPK)
        oh4v = part(TOPK * EXPERTS).rearrange("p (k e) -> p k e", k=TOPK)
        vrow = part(2 * EXPERTS).rearrange("p (v e) -> p v e", v=2)
        posm = part(EXPERTS)
        pos_table = part(3 * TABLE).rearrange("p (c n) -> p c n", c=3)
        val_table = part(6 * TABLE).rearrange("p (c n v) -> p c n v", c=3, v=2)
        mask = part(3 * EXPERTS).rearrange("p (c e) -> p c e", c=3)
        assert off[0] <= T_O * TOK
        onehot = part(3 * P).rearrange("p (c s) -> p c s", c=3)
        xgT = part(512).rearrange("p (k s) -> p k s", k=KD)
        glu = part(512).rearrange("p (q f) -> p q f", q=2)
        lin = part(512).rearrange("p (q f) -> p q f", q=2)
        sig = part(512).rearrange("p (q f) -> p q f", q=2)
        act_out = part(512)
        assert off[0] <= TILES * TOK
        mix_flat = mixT[:, :, :].rearrange("p k n -> p (k n)")
        aT = mix_flat[:, 0:512].rearrange("p (m s) -> p m s", m=4)
        eout = mix_flat[:, 512:1536].rearrange("p (b d) -> p b d", b=2)
        sel = sb("sel", [3 * EXPERTS, 2, BLOCK], BF16)
        egate = sb("egate", [P, 2])
        erow = sb("erow", [P, 2], U32)
        idx8 = sb("idx8", [P, 8], U32)
        extra = sb("extra", [P, 1], I32)
        wrout = sb("wrout", [P, KD, EXPERTS])
        x1T = xT

        q_row = nc.dram_tensor("q_row", (STATES, HD), F32).ap()
        k_row = nc.dram_tensor("k_row", (STATES, HD), F32).ap()
        ff_rows = nc.dram_tensor("ff_rows", (TOK * TOPK * 2, 512), F32).ap()

        block = ctx.enter_context(nc.Block())
        K_SCALE = HD ** -0.5

        def tile_done(t):
            if t >= 16 or t % 2:
                return "tile_act", (t + 1) // 2 if t < 16 else 8 + t - 15
            return "tile_dve", t // 2 + 1

        def unit_weights(e, u):
            if u < 8:
                return w_mlp1[0, bass.ds(e, 1), u * P:(u + 1) * P, :].rearrange("o p f -> p (o f)")
            r = u - 8
            return w_mlp2[0, bass.ds(e, 1), r * 2 * P:(r + 1) * 2 * P, :].rearrange("o (a p) f -> p (o a) f", a=2)

        def unit_place(slot, u):
            if u < 8:
                return ring[:, slot, :]
            return ring[:, slot, :].rearrange("p (a f) -> p a f", a=2)

        def slot_of(body_unit):
            return (FIRST + body_unit) % SLOTS

        def landings(body_unit):
            s = slot_of(body_unit)
            return sum(slot_of(v) == s for v in range(body_unit + 1))

        before = [2 if s < 4 else 1 if s < 10 else 0 for s in range(SLOTS)]

        @block.sync
        def _(sp):
            for c, (t0, n) in enumerate(CHUNKS):
                src = x_prompt[0, t0:t0 + n, :] if c < 2 else x_sample[:, 0, :]
                sp.dma_start(xtok[0:n, c, :], src).then_inc(sem(f"x_in{c}"), 16)

            def load_block(b):
                col = COLUMNS_IN[b]
                for half in range(2):
                    s = 2 * b + half
                    sp.dma_start(ring[:, s, :].rearrange("p (k n) -> p k n", k=4),
                                 w_in[0, 512 * half:512 * half + 512, col:col + 512]
                                 .rearrange("(k p) n -> p k n", p=P)).then_inc(sem(f"slot{s}"), 16)

            load_block(0)
            load_block(1)
            load_block(2)
            for g in range(3):
                rows_ = slice(g * EXPERTS, (g + 1) * EXPERTS)
                sp.dma_start(bsrc[rows_, 0:2 * FF], b_mlp1[0]).then_inc(sem("bias_in"), 16)
                sp.dma_start(bsrc[rows_, 2 * FF:3 * FF], b_mlp2[0]).then_inc(sem("bias_in"), 16)
            load_block(3)
            load_block(4)
            sp.dma_start(Cst, state_C[0].rearrange("b h v k -> v (b h) k")).then_inc(sem("C_in"), 16)
            def load_w_out(s):
                sp.wait_ge(sem("tile_ps"), 4 * (s // 2) + 4)
                sp.dma_start(ring[:, s, :].rearrange("p (k n) -> p k n", k=2),
                             w_out[0, 256 * s:256 * s + 256, :].rearrange("(k p) n -> p k n", p=P))\
                  .then_inc(sem(f"slot{s}"), 16)

            load_w_out(0)
            load_w_out(1)
            sp.wait_ge(sem("srow_ready"), 1)
            sp.dma_start(q_row, srow[:, SQ, :]).then_inc(sem("qk_row"), 16)
            sp.wait_ge(sem("qk_row"), 16)
            sp.dma_start(qb, q_row.partition_broadcast(P)).then_inc(sem("qb_in"), 16)
            load_w_out(2)
            load_w_out(3)
            sp.wait_ge(sem("srow_ready"), 2)
            sp.dma_start(k_row, srow[:, SK, :]).then_inc(sem("qk_row"), 16)
            sp.wait_ge(sem("qk_row"), 32)
            sp.wait_ge(sem("bias_cast"), 3)
            sp.dma_start(kb, k_row.partition_broadcast(P)).then_inc(sem("kb_in"), 16)

            def load_unit(e, j, u):
                s = slot_of(UNITS * j + u)
                sp.dma_start(unit_place(s, u), unit_weights(e, u)).then_inc(sem(f"slot{s}"), 16)

            for n in range(UNITS * STEP):
                s = slot_of(n)
                if n < UNITS:
                    if s < 10:
                        sp.wait_ge(sem("tile_ps"), 4 * (s // 2) + 4)
                    if s == 8:
                        sp.wait_ge(sem("mem_ps"), 2)
                        for c in range(2):
                            sp.dma_start(xtok[:, c, :], x_prompt[0, c * P:(c + 1) * P, :]).then_inc(sem("x_again"), 16)
                    if s == 10:
                        sp.wait_ge(sem("C_out"), 16)
                    elif s == 12:
                        sp.wait_ge(sem("Cnew_done"), 1)
                        sp.wait_ge(sem("scq_ready"), 1)
                elif n < SLOTS:
                    sp.wait_ge(sem("mix_ps"), 5)
                else:
                    sp.wait_ge(sem("units_used"), n - SLOTS + 1)
                load_unit(n // UNITS, n // UNITS, n % UNITS)

            def load_body(e, done):
                for n in range(UNITS * STEP):
                    sp.wait_ge(sem("units_used"), done + (n - SLOTS + 1))
                    load_unit(e + n // UNITS, n // UNITS, n % UNITS)

            bodies = EXPERTS // STEP
            with sp.Fori(1, bodies) as i:
                load_body(i * STEP, i * (STEP * UNITS))
            sp.wait_ge(sem("passes_ready"), 1)
            npass = sp.value_load(extra[0:1, 0:1], min_val=0, max_val=PASSES - 1) + 1
            with sp.If(npass > 1):
                with sp.Fori(1, npass) as b:
                    with sp.Fori(0, bodies) as i:
                        load_body(i * STEP, b * (EXPERTS * UNITS) + i * (STEP * UNITS))
            sp.nop()

            used = npass * (EXPERTS * UNITS)

            def wait_slot(s):
                sp.wait_ge(sem("units_used"), used + ((s - FIRST) % SLOTS + 1 - SLOTS))

            for i in range(4):
                wait_slot(4 + i)
                sp.dma_start(ring[:, 4 + i, :].rearrange("p (k n) -> p k n", k=2),
                             w_ple_gate[0, 256 * i:256 * i + 256, :].rearrange("(k p) n -> p k n", p=P))\
                  .then_inc(sem("wpg_in"), 16)
            wait_slot(9)
            sp.dma_start(ring[:, 8, :].rearrange("p (k n) -> p k n", k=2),
                         w_ple[0].rearrange("(k p) n -> p k n", p=P)).then_inc(sem("wple_in"), 16)
            for c, (t0, n) in enumerate(CHUNKS):
                src = p_prompt[0, 0, t0:t0 + n, :] if c < 2 else p_sample[0, :, 0, :]
                sp.dma_start(ring[0:n, 9, c * PLE:(c + 1) * PLE], src).then_inc(sem("p_in"), 16)
            sp.wait_ge(sem("rows_out"), npass * (16 * EXPERTS))
            for c, (t0, n) in enumerate(CHUNKS):
                sp.dma_start(slots(10 + 2 * c, 2, 4096)[0:n, :],
                             ff_rows.rearrange("(t r) f -> t (r f)", r=2 * TOPK)[t0:t0 + n, :])\
                  .then_inc(sem(f"ff_in{c}"), 16)
            for c, (t0, n) in enumerate(CHUNKS):
                sp.wait_ge(sem("y_done"), c + 1)
                dst = y_prompt[0, t0:t0 + n, :] if c < 2 else y_sample[:, 0, :]
                sp.dma_start(dst, xtok[0:n, c, :]).then_inc(sem("y_out"), 16)
            sp.wait_ge(sem("y_out"), 48)
            sp.wait_ge(sem("C_out"), 16)
            sp.wait_ge(sem("small_out"), 16 * SMALL_OUTS)

        @block.tensor
        def _(pe):
            pe.wait_ge(sem("cst_in"), 16)
            for g in range(6):
                c, half = g // 2, g % 2
                n = CHUNKS[c][1]
                if half == 0:
                    pe.wait_ge(sem(f"x_in{c}"), 16)
                for k in range(4):
                    last = pe.transpose(bank[g][:, k * P:k * P + n],
                                        xtok[0:n, c, (4 * half + k) * P:(4 * half + k + 1) * P], ident[0:n, 0:n])
                last.then_inc(sem("xT_ps"), 1)
            pe.wait_ge(sem("xT_dve"), 3)
            pe.wait_ge(sem("xT_act"), 3)
            pe.wait_ge(sem("gate_in"), 48)
            for k in range(KD):
                last = pe.matmul(bank[6][0:2 * HEADS, 0:TOK], wgate[:, k, :], xT[:, k, :],
                                 start=(k == 0), stop=(k == KD - 1))
            last.then_inc(sem("gates_ps"), 1)
            pe.wait_ge(sem("hist_in"), 16)
            for g in range(4):
                last = pe.matmul(bank[7][:, g * SAMPLES:(g + 1) * SAMPLES], hist[0:SAMPLES * HIST, g * P:(g + 1) * P],
                                 cst[0:SAMPLES * HIST, C_HIST + g * SAMPLES:C_HIST + (g + 1) * SAMPLES],
                                 start=True, stop=True)
            last.then_inc(sem("hist_ps"), 1)

            def project(t):
                b, j = t // 4, t % 4
                if t >= 2:
                    name, count = tile_done(t - 2)
                    pe.wait_ge(sem(name), count)
                for k in range(KD):
                    s = 2 * b + k // 4
                    if j == 0 and k % 4 == 0:
                        pe.wait_ge(sem(f"slot{s}"), 16)
                    w = ring[:, s, :].rearrange("p (k n) -> p k n", k=4)
                    last = pe.matmul(bank[t % 2][:, 0:TOK], w[:, k % 4, j * P:(j + 1) * P], xT[:, k, :],
                                     start=(k == 0), stop=(k == KD - 1))
                last.then_inc(sem("tile_ps"), 1)

            def turn_tokens(dst, first_tile, c):
                for h in range(HEADS):
                    last = pe.transpose(dst[:, h * P:(h + 1) * P], proj[:, first_tile + h, c * P:(c + 1) * P], ident)
                return last

            def pool_mix(g):
                pe.wait_ge(sem("z_ready"), g + 1)
                if g == 0:
                    pe.wait_ge(sem("pool_in"), 48)
                    pe.wait_ge(sem("gcol_done"), 1)
                else:
                    pe.wait_ge(sem("pool_done"), g)
                pe.matmul(bank[7][:, 0:TOK], wpool[:, g, :], proj[:, T_U + g, :], start=True, stop=True)\
                  .then_inc(sem("pool_ps"), 1)

            def values(c, dst, dden):
                for h in range(HEADS):
                    pe.matmul(dst[:, h * P:(h + 1) * P], decayed[:, c, h, :], vtok[:, c, h, :], start=True, stop=True)
                for h in range(HEADS):
                    last = pe.matmul(dden[:, h:h + 1], decayed[:, c, h, :], ones[:, 0:1], start=True, stop=True)
                return last

            def memory(c, dst, dn):
                for h in range(HEADS):
                    pe.matmul(dst[:, h * P:(h + 1) * P], ktok[:, c, h, :], vweighted[:, h, :], start=True, stop=True)
                for h in range(HEADS):
                    w0 = 4 * (ROW_WK + c) + h
                    last = pe.matmul(dn[:, h:h + 1], ktok[:, c, h, :], gcol[:, w0:w0 + 1], start=True, stop=True)
                return last

            def turn_heads(c):
                pe.wait_ge(sem("hn_ready"), c + 1)
                if c:
                    pe.wait_ge(sem("hT_done"), c)
                for h in range(HEADS):
                    last = pe.transpose(bank[6][:, h * P:(h + 1) * P], hout[:, c, h, :], ident)
                last.then_inc(sem("hT_ps"), 1)

            project(0)
            pe.wait_ge(sem("gates_done"), 1)
            pe.matmul(bank[5][0:HEADS, 0:SEQ], ident[0:2 * HEADS, HEADS:2 * HEADS], gates[:, 0:SEQ],
                      start=True, stop=True)
            pe.wait_ge(sem("spread_ready"), 1)
            pe.matmul(bank[5][0:STATES, SEQ:SEQ + 2], s_spread, cst[0:2 * HEADS, C_KIND:C_KIND + 2],
                      start=True, stop=True).then_inc(sem("gsel_ps"), 1)
            for t in range(1, 6):
                project(t)
            pe.wait_ge(sem("hist_done"), 1)
            pe.wait_ge(sem("rows_ready"), 1)
            for q in range(7):
                pe.transpose(bank[7][:, 4 * q:4 * q + 4], rows[:, q, :], ident[0:HEADS, 0:HEADS])
            pe.matmul(bank[7][:, 28:32], ones[0:HEADS, :], ddiag, start=True, stop=True).then_inc(sem("gcol_ps"), 1)
            for c in range(2):
                pe.matmul(bank[2 + c][:, :], ones[0:HEADS, :], maxdiag[c].rearrange("p h t -> p (h t)"),
                          start=True, stop=True).then_inc(sem("max_ps"), 1)
            def sample_rows(i):
                pe.wait_ge(sem("scol_ready"), i + 1)
                if i == 0:
                    pe.wait_ge(sem("gates_done"), 1)
                else:
                    pe.wait_ge(sem("srow_ready"), i)
                pe.transpose(bank[6][0:STATES, i * HD:(i + 1) * HD], scol[:, i, :], ident).then_inc(sem("srow_ps"), 1)

            for t in range(6, 9):
                project(t)
            sample_rows(0)
            for t in range(9, 13):
                project(t)
            pe.wait_ge(sem("tile_dve"), 6)
            pe.wait_ge(sem("tile_act"), 6)
            turn_tokens(bank[4], T_K, 0).then_inc(sem("ktok_ps"), 1)
            turn_tokens(bank[5], T_K, 1).then_inc(sem("ktok_ps"), 1)
            sample_rows(1)
            project(13)
            pe.wait_ge(sem("ktok_done"), 2)
            for c in range(2):
                for h in range(HEADS):
                    last = pe.matmul(bank[4 + c][:, h * P:(h + 1) * P], proj[:, T_K + h, c * P:(c + 1) * P],
                                     proj[:, T_Q + h, c * P:(c + 1) * P], start=True, stop=True)
                last.then_inc(sem("score_ps"), 1)
            pool_mix(0)
            project(14)
            pe.wait_ge(sem("sdiag_ready"), 1)
            pe.wait_ge(sem("srow_ready"), 2)
            pe.matmul(bank[6][:, 0:STATES], ones[0:STATES, :], sdiag, start=True, stop=True).then_inc(sem("sbc_ps"), 1)
            pool_mix(1)
            project(15)
            pool_mix(2)
            project(16)
            pe.wait_ge(sem("lag_ready"), 8)
            pe.wait_ge(sem("tile_dve"), 8)
            pe.wait_ge(sem("tile_act"), 8)
            turn_tokens(bank[2], T_V, 0).then_inc(sem("vtok_ps"), 1)
            turn_tokens(bank[3], T_V, 1).then_inc(sem("vtok_ps"), 1)
            pe.wait_ge(sem("sbc_done"), 1)
            sample_rows(2)
            pool_mix(3)
            project(17)
            pe.wait_ge(sem("decayed_ready"), 1)
            pe.wait_ge(sem("vtok_done"), 2)
            values(0, bank[2], bank[3][:, 0:4]).then_inc(sem("num_ps"), 1)
            pe.wait_ge(sem("vw_ready"), 1)
            memory(0, bank[4], bank[3][:, 4:8]).then_inc(sem("mem_ps"), 1)
            project(18)
            pe.wait_ge(sem("sdiag_ready"), 2)
            pe.transpose(bank[6][:, STATES:2 * STATES], srow[:, SV, :], ident[0:STATES, 0:STATES])\
              .then_inc(sem("sbc_ps"), 1)
            pe.wait_ge(sem("decayed_ready"), 2)
            pe.wait_ge(sem("num_done"), 1)
            values(1, bank[5], bank[3][:, 8:12])
            for h in range(HEADS):
                pe.matmul(bank[2][:, h * P:(h + 1) * P], proj[:, T_Q + h, P:2 * P], CT[:, h, :], start=True, stop=True)
            for h in range(HEADS):
                last = pe.matmul(bank[3][:, 12 + h:13 + h], proj[:, T_Q + h, P:2 * P], nstate[:, h:h + 1],
                                 start=True, stop=True)
            last.then_inc(sem("num_ps"), 1)
            pe.wait_ge(sem("vw_ready"), 2)
            memory(1, bank[4], bank[3][:, 16:20]).then_inc(sem("mem_ps"), 1)
            project(19)
            pe.wait_ge(sem("pool_done"), 4)
            for g in range(4):
                last = pe.transpose(bank[7][0:HIST + SAMPLES, g * P:(g + 1) * P], ukeep[:, g, :], ident)
            last.then_inc(sem("cfin_ps"), 1)

            def mix(c, banks, ks):
                t0, n = CHUNKS[c]
                for half in range(2):
                    for k in ks:
                        w = ring[:, k // 2, :].rearrange("p (k n) -> p k n", k=2)
                        last = pe.matmul(banks[half][0:n, :], mixT[:, k, t0:t0 + n],
                                         w[:, k % 2, half * 512:half * 512 + 512], start=(k == 0), stop=(k == KD - 1))
                    if ks[-1] == KD - 1:
                        last.then_inc(sem("mix_ps"), 1)

            def router(i):
                c = ORDER[i]
                t0, n = CHUNKS[c]
                for half in range(2):
                    g = 2 * i + half
                    pe.wait_ge(sem("ln1_ready"), g + 1)
                    if g >= 2:
                        pe.wait_ge(sem("x1T_done"), g - 1)
                    for k in range(4):
                        kk = 4 * half + k
                        last = pe.transpose(bank[6 + half][:, k * P:k * P + n],
                                            xtok[0:n, c, kk * P:(kk + 1) * P], ident[0:n, 0:n])
                    last.then_inc(sem("x1T_ps"), 1)
                if i == 0:
                    pe.wait_ge(sem("wrout_in"), 32)
                else:
                    pe.wait_ge(sem("logits_done"), i)
                pe.wait_ge(sem("x1T_done"), 2 * i + 2)
                pe.matmul(bank[4][0:n, 0:EXPERTS], ones[0:1, 0:n], brout[:, :], start=True, stop=False)
                for k in range(KD):
                    last = pe.matmul(bank[4][0:n, 0:EXPERTS], x1T[:, k, t0:t0 + n], wrout[:, k, :],
                                     start=False, stop=(k == KD - 1))
                last.then_inc(sem("logits_ps"), 1)

            for s in range(4):
                pe.wait_ge(sem(f"slot{s}"), 32)
            pe.wait_ge(sem("tile_act"), 12)
            first, second = (bank[0], bank[1]), (bank[2], bank[5])
            mix(0, first, range(4))
            pe.wait_ge(sem("sbc_done"), 2)
            turn_heads(0)
            pe.wait_ge(sem("num_done"), 2)
            mix(1, second, range(4))
            pe.wait_ge(sem("cfin_done"), 1)
            pe.wait_ge(sem("scq_ready"), 1)
            pe.transpose(bank[7][0:STATES, 0:P], scq, ident).then_inc(sem("scq_ps"), 1)
            pe.wait_ge(sem("hT_done"), 1)
            mix(0, first, range(4, KD))
            turn_heads(1)
            pe.wait_ge(sem("ct_ready"), 2)
            for h in range(HEADS):
                pe.transpose(bank[4][:, h * P:(h + 1) * P], CT[:, h, :], ident)
            pe.transpose(bank[3][0:HEADS, 0:P], nstate, ident).then_inc(sem("cfin_ps"), 1)
            pe.wait_ge(sem("sh_ready"), 1)
            pe.transpose(bank[7][:, P:P + STATES], srow[:, SY, :], ident[0:STATES, 0:STATES])\
              .then_inc(sem("shT_ps"), 1)
            pe.wait_ge(sem("shT_done"), 1)
            pe.wait_ge(sem("cfin_done"), 3)
            for k in range(KD):
                w = ring[:, k // 2, :].rearrange("p (k n) -> p k n", k=2)
                for q in range(4):
                    last = pe.matmul(bank[3][32 * q:32 * q + SAMPLES, 0:256], mixT[:, k, SEQ:TOK],
                                     w[:, k % 2, 256 * q:256 * q + 256], start=(k == 0), stop=(k == KD - 1))
            last.then_inc(sem("mix_ps"), 1)
            pe.wait_ge(sem("hT_done"), 2)
            mix(1, second, range(4, KD))
            for i in range(3):
                router(i)
            pe.wait_ge(sem("mask_ready"), 3)
            for c, (_, n) in enumerate(CHUNKS):
                for a in range(c + 1):
                    m = CHUNKS[a][1]
                    left = cst[0:m, C_BEFORE:C_BEFORE + n] if a == c else ones[0:m, 0:n]
                    pe.matmul(bank[3][0:n, c * EXPERTS:(c + 1) * EXPERTS], left, mask[0:m, a, :],
                              start=(a == 0), stop=(a == c))
            for a in range(3):
                m = CHUNKS[a][1]
                last = pe.matmul(bank[4][:, 0:EXPERTS], ones[0:m, :], mask[0:m, a, :], start=(a == 0), stop=(a == 2))
            last.then_inc(sem("pos_ps"), 1)

            def gather():
                for c in range(3):
                    pe.matmul(bank[5][:, 0:2], onehot[:, c, :], info[:, c, :], start=(c == 0), stop=(c == 2))
                for k in range(KD):
                    for c in range(3):
                        last = pe.matmul(bank[2][:, k * BLOCK:(k + 1) * BLOCK], xtok[:, c, k * P:(k + 1) * P],
                                         onehot[:, c, 0:BLOCK], start=(c == 0), stop=(c == 2))
                last.then_inc(sem("gathered"), 1)

            def expert(n, j):
                i4 = n - j
                pe.wait_ge(sem("xg_done"), n * 3 + 3)
                pe.wait_ge(sem("h_read"), n + 1)
                for t in range(2):
                    for q in range(2):
                        col = FF * t + 512 * q
                        pe.matmul(bank[q][BLOCK * t:BLOCK * (t + 1), :], sel[:, j % 2, :],
                                  bias_parts[:, col:col + 512], start=True, stop=False)
                for k in range(KD):
                    u = UNITS * j + k
                    s = slot_of(u)
                    pe.wait_ge(sem(f"slot{s}"), i4 * 12 + 16 * (before[s] + landings(u)))
                    for q in range(2):
                        for t in range(2):
                            col = FF * t + 512 * q
                            last = pe.matmul(bank[q][BLOCK * t:BLOCK * (t + 1), :], xgT[:, k, :],
                                             ring[:, s, col:col + 512], start=False, stop=(k == KD - 1))
                    last.then_inc(sem("units_used"), 1)
                pe.wait_ge(sem("onehot_ready"), n * 3 + 6)
                gather()
                pe.wait_ge(sem("act_ready"), n + 1)
                for m in range(4):
                    last = pe.transpose(bank[3][:, m * P:(m + 1) * P], act_out[:, m * P:(m + 1) * P], ident)
                last.then_inc(sem("aT_ps"), 1)
                pe.wait_ge(sem("aT_done"), n + 1)
                pe.wait_ge(sem("out_done"), n + 1)
                for h in range(2):
                    pe.matmul(bank[4][BLOCK * h:BLOCK * (h + 1), :], sel[:, j % 2, :],
                              bias_parts[:, 2 * FF + 512 * h:2 * FF + 512 * h + 512], start=True, stop=False)
                for k in range(8):
                    u = UNITS * j + 8 + k // 2
                    s = slot_of(u)
                    if k % 2 == 0:
                        pe.wait_ge(sem(f"slot{s}"), i4 * 12 + 16 * (before[s] + landings(u)))
                    w = ring[:, s, :].rearrange("p (a f) -> p a f", a=2)
                    t, m = k // 4, k % 4
                    for h in range(2):
                        last = pe.matmul(bank[4][BLOCK * h:BLOCK * (h + 1), :], aT[:, m, BLOCK * t:BLOCK * (t + 1)],
                                         w[:, k % 2, 512 * h:512 * h + 512], start=False, stop=(k == 7))
                    if k % 2 == 1:
                        last.then_inc(sem("units_used"), 1)

            pe.wait_ge(sem("onehot_ready"), 3)
            gather()
            pe.wait_ge(sem("passes_ready"), 1)
            npass = pe.value_load(extra[0:1, 0:1], min_val=0, max_val=PASSES - 1) + 1
            with pe.Fori(0, npass * EXPERTS, STEP) as n:
                for j in range(STEP):
                    expert(n + j, j)

            pe.wait_ge(sem("out_done"), npass * EXPERTS + 1)
            pe.wait_ge(sem("xg_done"), npass * (3 * EXPERTS) + 3)
            pe.wait_ge(sem("p_in"), 48)
            for c, (t0, n) in enumerate(CHUNKS):
                for k in range(2):
                    last = pe.transpose(bank[c][:, k * P:k * P + n],
                                        ring[0:n, 9, c * PLE + k * P:c * PLE + (k + 1) * P], ident[0:n, 0:n])
                last.then_inc(sem("pT_ps"), 1)
            pe.wait_ge(sem("wple_in"), 16)
            pT = ring[:, 9, 768:768 + 2 * TOK].rearrange("p (k n) -> p k n", k=2)
            wple_sb = ring[:, 8, :].rearrange("p (k n) -> p k n", k=2)
            for c, (t0, n) in enumerate(CHUNKS):
                pe.wait_ge(sem("pT_done"), c + 1)
                for half in range(2):
                    g = 2 * c + half
                    if g >= 2:
                        pe.wait_ge(sem("ple_done"), g - 1)
                    for k in range(2):
                        last = pe.matmul(bank[4 + half][0:n, :], pT[:, k, t0:t0 + n],
                                         wple_sb[:, k, half * 512:half * 512 + 512], start=(k == 0), stop=(k == 1))
                    last.then_inc(sem("ple_ps"), 1)
            pe.wait_ge(sem("wpg_in"), 64)
            for c, (t0, n) in enumerate(CHUNKS):
                for half in range(2):
                    g = 2 * c + half
                    pe.wait_ge(sem("ln2_ready"), g + 1)
                    if g >= 2:
                        pe.wait_ge(sem("x2T_done"), g - 1)
                    for k in range(4):
                        kk = 4 * half + k
                        last = pe.transpose(bank[6 + half][:, k * P:k * P + n],
                                            xtok[0:n, c, kk * P:(kk + 1) * P], ident[0:n, 0:n])
                    last.then_inc(sem("x2T_ps"), 1)
                pe.wait_ge(sem("x2T_done"), 2 * c + 2)
                for half in range(2):
                    g = 2 * c + half
                    if g >= 4:
                        pe.wait_ge(sem("sig_done"), g - 3)
                    for k in range(KD):
                        w = ring[:, 4 + k // 2, :].rearrange("p (k n) -> p k n", k=2)
                        last = pe.matmul(bank[g % 4][0:n, :], x1T[:, k, t0:t0 + n],
                                         w[:, k % 2, half * 512:half * 512 + 512], start=(k == 0), stop=(k == KD - 1))
                    last.then_inc(sem("gate_ps"), 1)

        @block.vector
        def _(dve):
            counts = {}

            def step(ins, name="dve_chain"):
                counts[name] = counts.get(name, 0) + 1
                ins.then_inc(sem(name), 1)
                dve.wait_ge(sem(name), counts[name])

            TT = dve.tensor_tensor
            TS = dve.tensor_scalar
            STT = dve.scalar_tensor_tensor

            def over(col, shape):
                return col.to_broadcast(shape)

            for g in (0, 2, 4):
                c = g // 2
                t0, n = CHUNKS[c]
                dve.wait_ge(sem("xT_ps"), g + 1)
                dve.tensor_copy(xT[:, 0:4, t0:t0 + n], bank[g][:, :].rearrange("p (k t) -> p k t", k=4)[:, :, 0:n])\
                   .then_inc(sem("xT_dve"), 1)
            dve.wait_ge(sem("hist_ps"), 1)
            dve.tensor_copy(histsum, bank[7][:, 0:32]).then_inc(sem("hist_done"), 1)

            def empty_tile(t):
                dve.wait_ge(sem("tile_ps"), t + 1)
                if T_K <= t < T_V:
                    ins = TS(proj[:, t, :], bank[t % 2][:, 0:TOK], K_SCALE, None, ALU.mult)
                else:
                    ins = dve.tensor_copy(proj[:, t, :], bank[t % 2][:, 0:TOK])
                ins.then_inc(sem("tile_dve"), 1)

            def more(ins, name="dve_chain"):
                counts[name] = counts.get(name, 0) + 1
                ins.then_inc(sem(name), 1)

            empty_tile(0)
            dve.wait_ge(sem("gates_done"), 1)
            step(TT(s_spread.rearrange("g (b h) -> g b h", h=HEADS),
                    gates[:, SEQ:TOK].unsqueeze(2).to_broadcast([2 * HEADS, SAMPLES, HEADS]),
                    cst[0:2 * HEADS, C_HEAD:C_HEAD + STATES].rearrange("g (b h) -> g b h", h=HEADS), ALU.mult),
                 "spread_ready")
            dve.wait_ge(sem("gsel_ps"), 1)
            step(dve.tensor_copy(fgate[:, :], bank[5][0:HEADS, 0:SEQ]))
            step(STT(softp, fgate[:, :], -1.0, fgate[:, :], ALU.mult, ALU.min), "soft_ready")
            empty_tile(2)
            dve.wait_ge(sem("soft_done"), 1)
            step(STT(logf, fgate[:, :], 0.0, softp, ALU.min, ALU.subtract))
            for c in range(2):
                s = slice(c * P, (c + 1) * P)
                step(dve.tensor_tensor_scan(cumf[:, s], ones[0:HEADS, :], logf[:, s], 0.0, ALU.mult, ALU.add))
                step(TT(rows[:, ROW_G + c, :], gates[0:HEADS, s], cumf[:, s], ALU.subtract))
                step(dve.tensor_tensor_scan(runmax[:, s], rows[:, ROW_G + c, :], rows[:, ROW_G + c, :],
                                            m1 if c else 0.0, ALU.max, ALU.max))
                e = (c + 1) * P - 1
                step(TT(m2 if c else m1, cumf[:, e:e + 1], runmax[:, e:e + 1], ALU.add))
                step(TS(nlast[:, c:c + 1], runmax[:, e:e + 1], -1.0, None, ALU.mult))
                step(TT(rows[:, ROW_EMT + c, :], cumf[:, s], runmax[:, s], ALU.add))
                step(TT(maxdiag[c], runmax[:, s].unsqueeze(1).to_broadcast([HEADS, HEADS, P]),
                        ident[0:HEADS, 0:HEADS].unsqueeze(2).to_broadcast([HEADS, HEADS, P]), ALU.mult),
                     "runmax_ready")
            empty_tile(4)
            dve.wait_ge(sem("rows_act"), 1)
            step(TS(ddiag, ident[0:HEADS, 0:HEADS], rows[:, ROW_SC, P - 1:P], None, ALU.mult), "rows_ready")
            step(dve.tensor_copy(s_gate, bank[5][0:STATES, SEQ:SEQ + 2]))
            dve.wait_ge(sem("states_in"), 32)
            f_, i_ = s_gate[:, 1:2], s_gate[:, 0:1]
            step(STT(s_col[S_T], f_, -1.0, f_, ALU.mult, ALU.min), "soft_ready")
            dve.wait_ge(sem("gcol_ps"), 1)
            step(dve.tensor_copy(small[:, 0:32], bank[7][:, 0:32]), "gcol_done")
            for c in range(2):
                dve.wait_ge(sem("max_ps"), c + 1)
                for h in range(HEADS):
                    g0 = 4 * (ROW_G + c) + h
                    more(TS(decayed[:, c, h, :], bank[2 + c][:, h * P:(h + 1) * P], gcol[:, g0:g0 + 1], 0.0,
                            ALU.subtract, ALU.max), "lag_ready")
            def sample_columns(i):
                more(dve.tensor_copy(scol[:, i, :].rearrange("p (b h) -> p b h", h=HEADS),
                                     proj[:, T_Q + 4 * i:T_Q + 4 * i + 4, SEQ:TOK].rearrange("p h b -> p b h")),
                     "scol_ready")

            empty_tile(6)
            dve.wait_ge(sem("bias_cast"), 1)
            step(TT(bsrc[0:2 * EXPERTS, :], bsrc[0:2 * EXPERTS, :], bias_parts[0:2 * EXPERTS, :], ALU.subtract),
                 "bias_rest")
            dve.wait_ge(sem("tile_act"), 4)
            dve.wait_ge(sem("tile_dve"), 4)
            sample_columns(0)
            empty_tile(8)
            dve.wait_ge(sem("srow_ps"), 1)
            step(dve.tensor_copy(srow[:, SQ, :], bank[6][0:STATES, 0:HD]), "srow_ready")
            dve.wait_ge(sem("soft_done"), 2)
            step(STT(s_col[S_LF], f_, 0.0, s_col[S_T], ALU.min, ALU.subtract))
            step(TT(s_col[S_INTER], s_col[S_M0], s_col[S_LF], ALU.add))
            step(TT(s_col[S_M], s_col[S_INTER], i_, ALU.max))
            step(TS(s_col[S_NM], s_col[S_M], -1.0, None, ALU.mult), "s_m_ready")
            dve.wait_ge(sem("bias_cast"), 2)
            step(TT(bsrc[0:EXPERTS, :], bsrc[0:EXPERTS, :], bias_parts[0:EXPERTS, :], ALU.subtract), "bias_rest")
            empty_tile(10)

            dve.wait_ge(sem("tile_act"), 6)
            dve.wait_ge(sem("tile_dve"), 6)
            sample_columns(1)
            for c in range(2):
                dve.wait_ge(sem("decay_act"), c + 1)
                more(TT(decayed[:, c], decayed[:, c], cst[:, C_CAUSAL:C_CAUSAL + P].unsqueeze(1)
                        .to_broadcast([P, HEADS, P]), ALU.mult))
            empty_tile(12)
            dve.wait_ge(sem("ktok_ps"), 1)
            dve.tensor_copy(ktok[:, 0], bank[4][:, :].rearrange("p (h d) -> p h d", h=HEADS)).then_inc(sem("ktok_done"), 1)
            dve.wait_ge(sem("srow_ps"), 2)
            step(dve.tensor_copy(srow[:, SK, :], bank[6][0:STATES, HD:2 * HD]), "srow_ready")
            step(dve.tensor_tensor_reduce(srow[:, SPROD, :], srow[:, SQ, :], srow[:, SK, :], 1.0, 0.0, ALU.mult, ALU.add,
                                          s_col[S_QK]))
            step(dve.tensor_tensor_reduce(srow[:, SPROD, :], srow[:, SQ, :], srow[:, SN, :], 1.0, 0.0, ALU.mult, ALU.add,
                                          s_col[S_NQ]))
            dve.wait_ge(sem("s_exp_done"), 3)
            step(TT(s_col[S_T], s_col[S_QK], s_col[S_DW], ALU.mult))
            step(STT(s_col[S_DEN], s_col[S_NQ], s_col[S_SC], s_col[S_T], ALU.mult, ALU.add))
            step(TS(srow[:, SPROD, :], srow[:, SK, :], s_col[S_DW], None, ALU.mult))
            step(STT(srow[:, SN, :], srow[:, SN, :], s_col[S_SC], srow[:, SPROD, :], ALU.mult, ALU.add), "sn_ready")
            step(TS(sdiag, ident[0:STATES, 0:STATES], s_col[S_SC], None, ALU.mult), "sdiag_ready")
            for c in range(2):
                dve.wait_ge(sem("score_ps"), c + 1)
                more(TT(decayed[:, c], decayed[:, c], bank[4 + c][:, :].rearrange("p (h t) -> p h t", h=HEADS),
                        ALU.mult), "decayed_ready")
            empty_tile(14)
            dve.wait_ge(sem("tile_act"), 8)
            dve.wait_ge(sem("tile_dve"), 8)
            sample_columns(2)
            dve.wait_ge(sem("sbc_ps"), 1)
            step(dve.tensor_copy(scol[:, 0, :], bank[6][:, 0:STATES]), "sbc_done")
            dve.wait_ge(sem("scq_parts"), 1)
            step(dve.tensor_reduce(scq, qb, AX.X, ALU.add), "scq_ready")
            dve.wait_ge(sem("vtok_ps"), 1)
            step(dve.tensor_copy(vtok[:, 0], bank[2][:, :].rearrange("p (h d) -> p h d", h=HEADS)))
            dve.engine_nop().then_inc(sem("vtok_done"), 1)
            step(TT(vweighted, vtok[:, 0], gcol[:, 4 * ROW_WK:4 * ROW_WK + 4].unsqueeze(2)
                    .to_broadcast([P, HEADS, P]), ALU.mult), "vw_ready")
            dve.wait_ge(sem("srow_ps"), 3)
            step(TS(srow[:, SV, :], bank[6][0:STATES, 2 * HD:3 * HD], s_col[S_DW], None, ALU.mult), "sdiag_ready")

            dve.wait_ge(sem("mem_ps"), 1)
            step(dve.tensor_copy(nstate, bank[3][:, 4:8]))
            step(dve.tensor_copy(den, bank[3][:, 0:4]))
            step(dve.tensor_copy(CT, bank[4][:, :].rearrange("p (h d) -> p h d", h=HEADS)), "ct_ready")
            step(dve.tensor_copy(hout[:, 0], bank[2][:, :].rearrange("p (h t) -> p h t", h=HEADS)), "num_done")
            dve.wait_ge(sem("vtok_done"), 2)
            step(TT(vweighted, vtok[:, 1], gcol[:, 4 * ROW_WK + 4:4 * ROW_WK + 8].unsqueeze(2)
                    .to_broadcast([P, HEADS, P]), ALU.mult), "vw_ready")

            def head(c, num, dsum):
                e0 = 4 * (ROW_EMT + c)
                step(STT(den2, dsum, -1.0, dsum, ALU.mult, ALU.max))
                step(TT(den2, den2, gcol[:, e0:e0 + 4], ALU.max))
                step(dve.reciprocal(den2, den2))
                step(TT(hout[:, c], num, den2.unsqueeze(2).to_broadcast([P, HEADS, P]), ALU.mult))
                for h in range(HEADS):
                    more(dve.bn_stats(h_bn[:, h, :], hout[:, c, h, :]))
                dve.wait_ge(sem("dve_chain"), counts["dve_chain"])
                for h in range(HEADS):
                    more(dve.bn_aggr(h_mv[:, h, :], h_bn[:, h, :]), "h_mv_ready")
                dve.wait_ge(sem("h_mv_ready"), counts["h_mv_ready"])
                step(TT(hout[:, c], hout[:, c], h_mv[:, :, 0:1].to_broadcast([P, HEADS, P]), ALU.subtract))
                dve.wait_ge(sem("h_rstd"), c + 1)
                step(dve.reciprocal(h_rstd, h_rstd))
                step(TT(hout[:, c], hout[:, c], h_rstd.unsqueeze(2).to_broadcast([P, HEADS, P]), ALU.mult),
                     "hn_ready")

            def mix_heads(c):
                dve.wait_ge(sem("hT_ps"), c + 1)
                dve.wait_ge(sem("tile_act"), 12)
                for h in range(HEADS):
                    ins = STT(mixT[:, 4 + h, c * P:(c + 1) * P], bank[6][:, h * P:(h + 1) * P], mhg[:, h:h + 1],
                              proj[:, T_O + h, c * P:(c + 1) * P], ALU.mult, ALU.mult)
                ins.then_inc(sem("hT_done"), 1)

            head(0, hout[:, 0], den)
            dve.wait_ge(sem("sbc_ps"), 2)
            step(dve.tensor_copy(scol[:, 1, :], bank[6][:, STATES:2 * STATES]), "sbc_done")
            dve.wait_ge(sem("mem_ps"), 2)
            sc1 = gcol[:, 4 * ROW_SC:4 * ROW_SC + 4]
            step(TT(hout[:, 1], bank[2][:, :].rearrange("p (h t) -> p h t", h=HEADS),
                    sc1.unsqueeze(2).to_broadcast([P, HEADS, P]), ALU.mult))
            step(TT(hout[:, 1], hout[:, 1], bank[5][:, :].rearrange("p (h t) -> p h t", h=HEADS), ALU.add))
            step(TT(den, bank[3][:, 12:16], sc1, ALU.mult))
            step(TT(den, den, bank[3][:, 8:12], ALU.add), "num_done")
            head(1, hout[:, 1], den)
            mix_heads(0)
            step(TT(CT, CT, dec_b.unsqueeze(2).to_broadcast([P, HEADS, P]), ALU.mult))
            step(TT(CT, CT, bank[4][:, :].rearrange("p (h d) -> p h d", h=HEADS), ALU.add))
            step(TT(nstate, nstate, dec_b, ALU.mult))
            step(TT(nstate, nstate, bank[3][:, 16:20], ALU.add), "ct_ready")
            mix_heads(1)
            dve.wait_ge(sem("scq_ps"), 1)
            step(TS(srow[:, SCQ, :], bank[7][0:STATES, 0:P], s_col[S_SC], None, ALU.mult))
            step(STT(srow[:, SY, :], srow[:, SV, :], s_col[S_QK], srow[:, SCQ, :], ALU.mult, ALU.add))
            step(STT(s_col[S_T], s_col[S_DEN], -1.0, s_col[S_DEN], ALU.mult, ALU.max))
            step(TT(s_col[S_T], s_col[S_T], s_col[S_EMT], ALU.max))
            step(dve.reciprocal(s_col[S_R], s_col[S_T]))
            step(TS(srow[:, SY, :], srow[:, SY, :], s_col[S_R], None, ALU.mult))
            step(dve.bn_stats(s_bn, srow[:, SY, :]))
            step(dve.bn_aggr(s_mv, s_bn), "s_mv_ready")
            dve.wait_ge(sem("h_rstd"), 3)
            step(dve.reciprocal(s_col[S_RSTD], s_col[S_RSTD]))
            step(TS(srow[:, SY, :], srow[:, SY, :], s_mv[:, 0:1], s_col[S_RSTD], ALU.subtract, ALU.mult), "sh_ready")
            dve.wait_ge(sem("shT_ps"), 1)
            for h in range(HEADS):
                ins = STT(mixT[:, 4 + h, SEQ:TOK],
                          bank[7][:, P:P + STATES].rearrange("p (b h) -> p h b", h=HEADS)[:, h, :], mhg[:, h:h + 1],
                          proj[:, T_O + h, SEQ:TOK], ALU.mult, ALU.mult)
            ins.then_inc(sem("shT_done"), 1)

            def layer_norm(i, c, n, name):
                x = xtok[0:n, c, :]
                halves = [slice(0, 512), slice(512, 1024)]
                dve.wait_ge(sem("dve_chain"), counts["dve_chain"])
                step(dve.bn_aggr(ln_mv[0:n, :], ln_bn[0:n, :]), name + "_mv")
                for s in halves:
                    more(STT(x[:, s], x[:, s], ln_mv[0:n, 0:1], lnreg[0:n, s], ALU.subtract, ALU.mult))
                dve.wait_ge(sem(name + "_rstd"), i + 1)
                step(dve.reciprocal(ln_rstd[0:n, :], ln_rstd[0:n, :]))
                for h, s in enumerate(halves):
                    more(STT(x[:, s], x[:, s], ln_rstd[0:n, :], lnreg[0:n, D + 512 * h:D + 512 * h + 512],
                             ALU.mult, ALU.add), name + "_ready")

            def half_stats(n, half, x):
                more(dve.bn_stats(ln_bn[0:n, 6 * half:6 * half + 6], x))

            def route(i):
                c = ORDER[i]
                t0, n = CHUNKS[c]
                dve.wait_ge(sem("logits_ps"), i + 1)
                step(dve.tensor_copy(logits[0:n, :], bank[4][0:n, 0:EXPERTS]), "logits_done")
                step(dve.max(top[0:n, :], logits[0:n, :]))
                more(TS(gsum[0:n, 0:1], top[0:n, 0:1], -1.0, None, ALU.mult), "top_ready")
                step(dve.max_index(idx8[0:n, :], top[0:n, :], logits[0:n, :]))
                step(dve.tensor_copy(idx4[0:n, :], idx8[0:n, 0:TOPK]))
                step(TT(oh4[0:n], cst[0:n, C_EXP:C_EXP + EXPERTS].unsqueeze(1).to_broadcast([n, TOPK, EXPERTS]),
                        idx4[0:n, :].unsqueeze(2).to_broadcast([n, TOPK, EXPERTS]), ALU.is_equal))
                step(dve.tensor_reduce(mask[0:n, c, :], oh4[0:n].rearrange("p k e -> p e k"), AX.X, ALU.add),
                     "mask_ready")
                step(TT(oh4v[0:n], oh4[0:n], cst[0:n, C_RANK + TOPK * c:C_RANK + TOPK * c + TOPK].unsqueeze(2)
                        .to_broadcast([n, TOPK, EXPERTS]), ALU.mult))
                step(dve.tensor_reduce(vrow[0:n, 0, :], oh4v[0:n].rearrange("p k e -> p e k"), AX.X, ALU.add))
                dve.wait_ge(sem("top_exp"), i + 1)
                step(dve.tensor_reduce(gsum[0:n, 1:2], gate4[0:n, :], AX.X, ALU.add))
                step(dve.reciprocal(gsum[0:n, 2:3], gsum[0:n, 1:2]))
                step(TS(gate4[0:n, :], gate4[0:n, :], gsum[0:n, 2:3], None, ALU.mult))
                step(TT(oh4v[0:n], oh4[0:n], gate4[0:n, :].unsqueeze(2).to_broadcast([n, TOPK, EXPERTS]), ALU.mult))
                step(dve.tensor_reduce(vrow[0:n, 1, :], oh4v[0:n].rearrange("p k e -> p e k"), AX.X, ALU.add))
                for v in range(2):
                    table = val_table[0:n, c, 0:PASSES * EXPERTS, v].rearrange("p (b e) -> p b e", b=PASSES)
                    more(dve.tensor_copy(table, vrow[0:n, v, :].unsqueeze(1).to_broadcast([n, PASSES, EXPERTS])))
                dve.wait_ge(sem("dve_chain"), counts["dve_chain"])

            dve.wait_ge(sem("ln1_in"), 32)
            dve.wait_ge(sem("x_again"), 32)
            dve.wait_ge(sem("x2_again"), 16)
            for i, c in enumerate(ORDER):
                n = CHUNKS[c][1]
                if c == 2:
                    dve.wait_ge(sem("mix2_done"), 4)
                    x = xtok[0:n, c, :]
                    step(STT(x, x, ALPHA, mix2, ALU.mult, ALU.add))
                    for half in range(2):
                        half_stats(n, half, x[:, 512 * half:512 * half + 512])
                else:
                    for half in range(2):
                        dve.wait_ge(sem("mix_ps"), (4 if c else 1) + half)
                        b = ((bank[0], bank[1]), (bank[2], bank[5]))[c][half]
                        x = xtok[0:n, c, 512 * half:512 * half + 512]
                        step(STT(x, x, ALPHA, b[0:n, :], ALU.mult, ALU.add))
                        half_stats(n, half, x)
                layer_norm(i, c, n, "ln1")
                if i == 0:
                    step(dve.memset(pos_table, FAR))
                    step(dve.memset(val_table, 0.0))
            for i in range(3):
                route(i)
            dve.wait_ge(sem("pos_ps"), 1)
            for c, (t0, n) in enumerate(CHUNKS):
                step(STT(posm[0:n, :], mask[0:n, c, :], -FAR, bank[3][0:n, c * EXPERTS:(c + 1) * EXPERTS],
                         ALU.mult, ALU.add))
                table = pos_table[0:n, c, 0:PASSES * EXPERTS].rearrange("p (b e) -> p b e", b=PASSES)
                step(TT(table, posm[0:n, :].unsqueeze(1).to_broadcast([n, PASSES, EXPERTS]),
                        cst[0:n, C_BLK:C_BLK + PASSES].unsqueeze(2).to_broadcast([n, PASSES, EXPERTS]), ALU.add))

            def one_hot(n, parity):
                TT(onehot, cst[:, C_SLOT:C_SLOT + P].unsqueeze(1).to_broadcast([P, 3, P]),
                   pos_table[:, :, bass.ds(n, 1)].to_broadcast([P, 3, P]), ALU.is_equal).then_inc(sem("onehot_ready"), 1)
                dve.tensor_copy(info, val_table[:, :, bass.ds(n, 1), :].rearrange("p c o v -> p c (o v)"))\
                   .then_inc(sem("onehot_ready"), 1)
                dve.tensor_copy(sel[:, parity, :], cst[0:3 * EXPERTS, bass.ds(n + C_SEL, 1)]
                                .to_broadcast([3 * EXPERTS, BLOCK])).then_inc(sem("onehot_ready"), 1)

            def gathered(n, parity):
                dve.wait_ge(sem("gathered"), n + 1)
                TS(erow[:, parity:parity + 1], bank[5][:, 0:1], 2.0, cst[:, C_HALF:C_HALF + 1], ALU.mult, ALU.add)\
                    .then_inc(sem("xg_done"), 1)
                dve.tensor_copy(egate[:, parity:parity + 1], bank[5][:, 1:2]).then_inc(sem("xg_done"), 1)
                dve.tensor_copy(xgT, bank[2][:, :].rearrange("p (k s) -> p k s", k=KD)).then_inc(sem("xg_done"), 1)

            def expert(n, j):
                dve.wait_ge(sem("gathered"), n + 1)
                dve.wait_ge(sem("out_done"), n + 1)
                one_hot(n + 1, (j + 1) % 2)
                dve.wait_ge(sem("units_used"), n * UNITS + 8)
                hb = [bank[q][:, :].rearrange("p (f two) -> p two f", two=2) for q in range(2)]
                for q in range(2):
                    TS(glu[:, q, :], hb[q][:, 0, :], LIMIT, None, ALU.min).then_inc(sem("glu_ready"), 1)
                for q in range(2):
                    TS(lin[:, q, :], hb[q][:, 1, :], LIMIT, -LIMIT, ALU.min, ALU.max).then_inc(sem("lin_ready"), 1)
                dve.wait_ge(sem("lin_ready"), (n + 1) * 2)
                dve.wait_ge(sem("glu_ready"), (n + 1) * 2)
                STT(lin, lin, 1.0, glu, ALU.add, ALU.mult).then_inc(sem("h_read"), 1)
                dve.wait_ge(sem("h_read"), n + 2)
                dve.wait_ge(sem("sig_ready"), n + 1)
                TT(act_out.rearrange("p (q f) -> p q f", q=2), lin, sig, ALU.mult).then_inc(sem("act_ready"), 1)
                dve.wait_ge(sem("rows_left"), n + 1)
                gathered(n + 1, (j + 1) % 2)

            dve.wait_ge(sem("dve_chain"), counts["dve_chain"])
            dve.engine_nop().then_inc(sem("h_read"), 1)
            one_hot(0, 0)
            step(dve.tensor_reduce(gsum[:, 0:1], bank[4][:, 0:EXPERTS], AX.X, ALU.max))
            step(TS(gate4, cst[:, C_LIM:C_LIM + 4], gsum[:, 0:1], None, ALU.is_lt))
            step(dve.tensor_reduce(gsum[:, 1:2], gate4, AX.X, ALU.add))
            step(dve.tensor_copy(extra[:, :], gsum[:, 1:2]), "passes_ready")
            gathered(0, 0)
            dve.wait_ge(sem("passes_ready"), 1)
            npass = dve.value_load(extra[0:1, 0:1], min_val=0, max_val=PASSES - 1) + 1
            with dve.Fori(0, npass * EXPERTS, STEP) as n:
                for j in range(STEP):
                    expert(n + j, j)

            pT = ring[:, 9, 768:768 + 2 * TOK].rearrange("p (k n) -> p k n", k=2)
            for c, (t0, n) in enumerate(CHUNKS):
                dve.wait_ge(sem("pT_ps"), c + 1)
                dve.tensor_copy(pT[:, :, t0:t0 + n], bank[c][:, 0:2 * P].rearrange("p (k t) -> p k t", k=2)[:, :, 0:n])\
                   .then_inc(sem("pT_done"), 1)
            dve.wait_ge(sem("ln2_in"), 32)
            for c, (t0, n) in enumerate(CHUNKS):
                f = slots(10 + 2 * c, 2, 4096)[0:n, :].rearrange("p (k d) -> p k d", k=TOPK)
                dve.wait_ge(sem(f"ff_in{c}"), 16)
                step(TT(f[:, 0:2, :], f[:, 0:2, :], f[:, 2:4, :], ALU.add))
                step(STT(xtok[0:n, c, :], xtok[0:n, c, :], ALPHA, f[:, 0, :], ALU.mult, ALU.add))
                step(TT(xtok[0:n, c, :], xtok[0:n, c, :], f[:, 1, :], ALU.add))
                for half in range(2):
                    half_stats(n, half, xtok[0:n, c, 512 * half:512 * half + 512])
                layer_norm(c, c, n, "ln2")
                for half in range(2):
                    dve.wait_ge(sem("x2T_ps"), 2 * c + half + 1)
                    dve.tensor_copy(x1T[:, 4 * half:4 * half + 4, t0:t0 + n],
                                    bank[6 + half][:, :].rearrange("p (k t) -> p k t", k=4)[:, :, 0:n])\
                       .then_inc(sem("x2T_done"), 1)
            for c, (t0, n) in enumerate(CHUNKS):
                f = slots(10 + 2 * c, 2, 4096)[0:n, :].rearrange("p (k d) -> p k d", k=TOPK)
                dve.wait_ge(sem("sig_done"), 2 * c + 2)
                dve.wait_ge(sem("ple_done"), 2 * c + 2)
                ple = ring[0:n, c, 0:D]
                step(TT(f[:, 0, :], f[:, 0, :], ple, ALU.mult))
                step(TT(xtok[0:n, c, :], xtok[0:n, c, :], f[:, 0, :], ALU.add), "y_done")

        @block.scalar
        def _(act):
            act.dma_start(cst[:, :], consts).then_inc(sem("cst_in"), 16)
            act.dma_start(wgate[:, :, :], w_in[0, :, 2560:2568].rearrange("(k p) n -> p k n", p=P))\
               .then_inc(sem("gate_in"), 16)
            act.dma_start(gbias[0:HEADS, :], b_i.rearrange("o h -> h o")).then_inc(sem("gate_in"), 16)
            act.dma_start(gbias[HEADS:2 * HEADS, :], b_f.rearrange("o h -> h o")).then_inc(sem("gate_in"), 16)

            act.dma_start(hist[0:SAMPLES * HIST, :], state_pool[0].rearrange("b r d -> (b r) d"))\
               .then_inc(sem("hist_in"), 16)

            for g in (1, 3, 5):
                c = g // 2
                t0, n = CHUNKS[c]
                act.wait_ge(sem("xT_ps"), g + 1)
                act.copy(xT[:, 4:8, t0:t0 + n], bank[g][:, :].rearrange("p (k t) -> p k t", k=4)[:, :, 0:n])\
                   .then_inc(sem("xT_act"), 1)
            act.wait_ge(sem("gates_ps"), 1)
            act.wait_ge(sem("gate_in"), 48)
            act.activation(gates[:, :], bank[6][0:2 * HEADS, 0:TOK], ACT.Identity, bias=gbias).then_inc(sem("gates_done"), 1)
            act.dma_start(srow[:, SN, :], state_n[0].rearrange("b h k -> (b h) k")).then_inc(sem("states_in"), 16)
            act.dma_start(s_col[S_M0], state_m.rearrange("o b h -> (b h) o")).then_inc(sem("states_in"), 16)
            act.dma_start(wpool[:, :, :], w_pool[0].rearrange("g c d -> c g d")).then_inc(sem("pool_in"), 16)
            act.dma_start(pscale, pool_scale[0].rearrange("(g d) -> d g", d=P)).then_inc(sem("pool_in"), 16)
            act.dma_start(mhg, mh_g[0].rearrange("(g d) -> d g", d=P)).then_inc(sem("pool_in"), 16)
            act.dma_start(wrout[:, :, :], w_router[0].rearrange("(k p) e -> p k e", p=P)).then_inc(sem("wrout_in"), 16)
            act.dma_start(brout[:, :], b_router).then_inc(sem("wrout_in"), 16)

            def empty_tile(t):
                act.wait_ge(sem("tile_ps"), t + 1)
                if t >= 16:
                    ins = act.activation(proj[:, t, :], bank[t % 2][:, 0:TOK], ACT.Sigmoid)
                elif T_K <= t < T_V:
                    ins = act.activation(proj[:, t, :], bank[t % 2][:, 0:TOK], ACT.Copy, scale=K_SCALE)
                else:
                    ins = act.copy(proj[:, t, :], bank[t % 2][:, 0:TOK])
                ins.then_inc(sem("tile_act"), 1)

            one = ones[0:HEADS, 0:1]
            act.wait_ge(sem("soft_ready"), 1)
            act.activation(softp, softp, ACT.Exp).then_inc(sem("soft_exp"), 1)
            empty_tile(1)
            act.wait_ge(sem("soft_exp"), 1)
            act.activation(softp, softp, ACT.Ln, bias=one).then_inc(sem("soft_done"), 1)
            empty_tile(3)
            act.wait_ge(sem("runmax_ready"), 2)
            act.activation(rows[:, ROW_EMT:ROW_EMT + 2, :], rows[:, ROW_EMT:ROW_EMT + 2, :], ACT.Exp, scale=-1.0)\
               .then_inc(sem("rows_parts"), 1)
            for c in range(2):
                act.activation(rows[:, ROW_WK + c, :], rows[:, ROW_G + c, :], ACT.Exp, bias=nlast[:, c:c + 1])\
                   .then_inc(sem("rows_parts"), 1)
            act.activation(rows[:, ROW_SC, :], runmax[:, P:2 * P], ACT.Exp, bias=m1, scale=-1.0).then_inc(sem("rows_parts"), 1)
            act.wait_ge(sem("rows_parts"), 4)
            act.nop().then_inc(sem("rows_act"), 1)
            empty_tile(5)

            def bias_part(part_):
                r = slice(0, (3 - part_) * EXPERTS)
                act.copy(bias_parts[r, :], bsrc[r, :]).then_inc(sem("bias_cast"), 1)

            act.wait_ge(sem("bias_in"), 96)
            bias_part(0)
            act.wait_ge(sem("soft_ready"), 2)
            act.activation(s_col[S_T], s_col[S_T], ACT.Exp).then_inc(sem("soft_exp"), 1)
            for c in range(2):
                act.wait_ge(sem("lag_ready"), 4 * (c + 1))
                act.activation(decayed[:, c], decayed[:, c], ACT.Exp, scale=-1.0).then_inc(sem("decay_act"), 1)
            empty_tile(7)
            act.wait_ge(sem("soft_exp"), 2)
            act.activation(s_col[S_T], s_col[S_T], ACT.Ln, bias=ones[0:STATES, 0:1]).then_inc(sem("soft_done"), 1)
            act.wait_ge(sem("bias_rest"), 1)
            bias_part(1)
            empty_tile(9)
            act.wait_ge(sem("s_m_ready"), 1)
            for src, dst in ((s_gate[:, 0:1], S_DW), (s_col[S_INTER], S_SC)):
                act.activation(s_col[dst], src, ACT.Exp, bias=s_col[S_NM]).then_inc(sem("s_exp_done"), 1)
            act.activation(s_col[S_EMT], s_col[S_M], ACT.Exp, scale=-1.0).then_inc(sem("s_exp_done"), 1)
            act.wait_ge(sem("bias_rest"), 2)
            bias_part(2)
            empty_tile(11)
            act.wait_ge(sem("ktok_ps"), 2)
            act.copy(ktok[:, 1], bank[5][:, :].rearrange("p (h d) -> p h d", h=HEADS)).then_inc(sem("ktok_done"), 1)

            def pool_group(g):
                act.wait_ge(sem("pool_ps"), g + 1)
                if g == 0:
                    act.wait_ge(sem("pool_in"), 48)
                act.activation(mixT[:, g, :], bank[7][:, 0:TOK], ACT.Copy, scale=pscale[:, g:g + 1])\
                   .then_inc(sem("pool_done"), 1)

            def root(out_, in_, name):
                act.activation(out_, in_, ACT.Sqrt, bias=eps[0:in_.shape[0], :]).then_inc(sem(name), 1)

            empty_tile(13)
            pool_group(0)
            pool_group(1)
            empty_tile(15)
            pool_group(2)
            empty_tile(16)
            act.wait_ge(sem("vtok_ps"), 2)
            act.copy(vtok[:, 1], bank[3][:, :].rearrange("p (h d) -> p h d", h=HEADS)).then_inc(sem("vtok_done"), 1)
            pool_group(3)
            empty_tile(17)
            empty_tile(18)
            act.wait_ge(sem("h_mv_ready"), 4)
            root(h_rstd, h_mv[:, :, 1], "h_rstd")
            empty_tile(19)
            act.wait_ge(sem("cfin_ps"), 1)
            act.copy(urow[:, :], bank[7][0:HIST + SAMPLES, :]).then_inc(sem("cfin_done"), 1)
            act.wait_ge(sem("h_mv_ready"), 8)
            act.wait_ge(sem("hn_ready"), 1)
            root(h_rstd, h_mv[:, :, 1], "h_rstd")
            act.wait_ge(sem("hT_ps"), 2)
            act.dma_start(lnreg[:, 0:D], ln1_g.partition_broadcast(P).rearrange("p o d -> p (o d)"))\
               .then_inc(sem("ln1_in"), 16)
            act.wait_ge(sem("cfin_ps"), 2)
            act.dma_start(lnreg[:, D:2 * D], ln1_b.partition_broadcast(P).rearrange("p o d -> p (o d)"))\
               .then_inc(sem("ln1_in"), 16)
            act.copy(ncol_out[:, :], bank[3][0:HEADS, 0:P]).then_inc(sem("cfin_done"), 1)
            act.copy(Cfin, bank[4][:, :].rearrange("p (h d) -> p h d", h=HEADS)).then_inc(sem("cfin_done"), 1)
            act.wait_ge(sem("s_mv_ready"), 1)
            root(s_col[S_RSTD], s_mv[:, 1:2], "h_rstd")

            def ln_root(i, c, name):
                n = CHUNKS[c][1]
                act.wait_ge(sem(name + "_mv"), i + 1)
                if i:
                    act.wait_ge(sem(name + "_ready"), 2 * i)
                root(ln_rstd[0:n, :], ln_mv[0:n, 1:2], name + "_rstd")

            def turned(i, name):
                t0, n = CHUNKS[ORDER[i]]
                for half in range(2):
                    act.wait_ge(sem(name + "_ps"), 2 * i + half + 1)
                    act.copy(x1T[:, 4 * half:4 * half + 4, t0:t0 + n],
                             bank[6 + half][:, :].rearrange("p (k t) -> p k t", k=4)[:, :, 0:n])\
                       .then_inc(sem(name + "_done"), 1)

            def top_exp(i):
                n = CHUNKS[ORDER[i]][1]
                act.wait_ge(sem("top_ready"), i + 1)
                act.activation(gate4[0:n, :], top[0:n, 0:TOPK], ACT.Exp, bias=gsum[0:n, 0:1]).then_inc(sem("top_exp"), 1)

            ln_root(0, 0, "ln1")
            act.wait_ge(sem("mix_ps"), 3)
            for q in range(4):
                act.copy(mix2[:, 256 * q:256 * q + 256], bank[3][32 * q:32 * q + SAMPLES, 0:256])\
                   .then_inc(sem("mix2_done"), 1)
            ln_root(1, 2, "ln1")
            ln_root(2, 1, "ln1")
            for i in range(3):
                turned(i, "x1T")
                top_exp(i)

            def expert(n, j):
                act.wait_ge(sem("glu_ready"), n * 2 + 2)
                act.activation(sig, glu, ACT.Sigmoid, scale=SIG).then_inc(sem("sig_ready"), 1)
                act.wait_ge(sem("aT_ps"), n + 1)
                act.copy(aT, bank[3][:, :].rearrange("p (m s) -> p m s", m=4)).then_inc(sem("aT_done"), 1)
                act.wait_ge(sem("units_used"), n * UNITS + UNITS)
                act.wait_ge(sem("rows_left"), n + 1)
                act.activation(eout[:, j % 2, :], bank[4][:, :], ACT.Copy, scale=egate[:, j % 2:j % 2 + 1])\
                   .then_inc(sem("out_done"), 1)

            act.nop().then_inc(sem("out_done"), 1)
            act.wait_ge(sem("passes_ready"), 1)
            npass = act.value_load(extra[0:1, 0:1], min_val=0, max_val=PASSES - 1) + 1
            with act.Fori(0, npass * EXPERTS, STEP) as n:
                for j in range(STEP):
                    expert(n + j, j)

            for c, (t0, n) in enumerate(CHUNKS):
                for half in range(2):
                    act.wait_ge(sem("ple_ps"), 2 * c + half + 1)
                    act.copy(ring[0:n, c, 512 * half:512 * half + 512], bank[4 + half][0:n, :])\
                       .then_inc(sem("ple_done"), 1)
            for c, (t0, n) in enumerate(CHUNKS):
                ln_root(c, c, "ln2")
            for c, (t0, n) in enumerate(CHUNKS):
                f = slots(10 + 2 * c, 2, 4096)[0:n, :]
                for half in range(2):
                    act.wait_ge(sem("gate_ps"), 2 * c + half + 1)
                    act.activation(f[:, 512 * half:512 * half + 512], bank[(2 * c + half) % 4][0:n, :], ACT.Sigmoid)\
                       .then_inc(sem("sig_done"), 1)

        @block.gpsimd
        def _(pool):
            chain = [0]

            def step(ins):
                chain[0] += 1
                ins.then_inc(sem("pool_chain"), 1)
                pool.wait_ge(sem("pool_chain"), chain[0])

            step(pool.memset(window[:, :, 0:16], 0.0))
            for g, w in enumerate(WINDOWS):
                u = proj[:, T_U + g, :]
                name, count = tile_done(T_U + g)
                pool.wait_ge(sem(name), count)
                step(pool.tensor_copy(window[:, 0, 16:], u[:, 0:SEQ]))
                src, shift = 0, 1
                while shift < w:
                    step(pool.tensor_tensor(window[:, 1 - src, 16:], window[:, src, 16:],
                                            window[:, src, 16 - shift:16 + SEQ - shift], ALU.add))
                    src, shift = 1 - src, 2 * shift
                first = window[:, src, 16:32]
                step(pool.tensor_tensor(first, first, cst[:, C_CNT + 16 * g:C_CNT + 16 * g + 16], ALU.mult))
                if g == 0:
                    pool.wait_ge(sem("hist_done"), 1)
                hs = histsum[:, g * SAMPLES:(g + 1) * SAMPLES]
                step(pool.tensor_tensor(hs, hs, u[:, SEQ:TOK], ALU.add))
                step(pool.tensor_scalar(hs, hs, 1.0 / w, None, ALU.mult))
                step(pool.tensor_scalar(window[:, src, 16:], window[:, src, 16:], 1.0 / w, None, ALU.mult))
                step(pool.tensor_copy(ukeep[:, g, 0:HIST], u[:, SEQ - HIST:SEQ]))
                step(pool.tensor_copy(ukeep[:, g, HIST:HIST + SAMPLES], u[:, SEQ:TOK]))
                step(pool.tensor_tensor(u[:, SEQ:TOK], hs, u[:, SEQ:TOK], ALU.subtract))
                step(pool.tensor_tensor(u[:, 0:SEQ], window[:, src, 16:], u[:, 0:SEQ], ALU.subtract))
                pool.engine_nop().then_inc(sem("z_ready"), 1)

            pool.wait_ge(sem("C_in"), 16)
            pool.wait_ge(sem("qb_in"), 16)
            step(pool.tensor_tensor(qb, qb, Cst, ALU.mult))
            pool.engine_nop().then_inc(sem("scq_parts"), 1)
            pool.wait_ge(sem("sbc_done"), 1)
            step(pool.tensor_tensor(Cst, Cst, scol[:, 0, :].unsqueeze(2).to_broadcast([P, STATES, HD]), ALU.mult))
            pool.wait_ge(sem("mem_ps"), 2)
            step(pool.memset(xtok[:, 2, :], 0.0))
            pool.dma_start(xtok[0:SAMPLES, 2, :], x_sample[:, 0, :]).then_inc(sem("x2_again"), 16)
            pool.wait_ge(sem("sbc_done"), 2)
            pool.wait_ge(sem("kb_in"), 16)
            step(pool.tensor_tensor(kb, kb, scol[:, 1, :].unsqueeze(2).to_broadcast([P, STATES, HD]), ALU.mult))
            step(pool.tensor_tensor(Cst, Cst, kb, ALU.add))
            pool.engine_nop().then_inc(sem("Cnew_done"), 1)
            pool.dma_start(C_sample[0].rearrange("b h v k -> v (b h) k"), Cst).then_inc(sem("C_out"), 16)
            pool.wait_ge(sem("cfin_done"), 3)
            pool.dma_start(pool_prompt[0, 0], urow[0:HIST, :]).then_inc(sem("small_out"), 16)
            pool.dma_start(pool_sample[0, :, HIST - 1, :], urow[HIST:HIST + SAMPLES, :]).then_inc(sem("small_out"), 16)
            pool.dma_start(C_prompt[0, 0].rearrange("h v k -> v h k"), Cfin).then_inc(sem("small_out"), 16)
            pool.dma_start(n_prompt[0, 0], ncol_out[:, :]).then_inc(sem("small_out"), 16)
            pool.dma_start(m_prompt[0].rearrange("b h -> h b"), m2).then_inc(sem("small_out"), 16)
            pool.wait_ge(sem("sn_ready"), 1)
            pool.dma_start(n_sample[0].rearrange("b h k -> (b h) k"), srow[:, SN, :]).then_inc(sem("small_out"), 16)
            pool.dma_start(m_sample.rearrange("o b h -> (b h) o"), s_col[S_M]).then_inc(sem("small_out"), 16)
            pool.dma_start(pool_sample[0, :, 0:HIST - 1, :], state_pool[0, :, 1:HIST, :]).then_inc(sem("small_out"), 16)
            pool.wait_ge(sem("ln1_ready"), 6)
            pool.dma_start(lnreg[:, 0:D], ln2_g.partition_broadcast(P).rearrange("p o d -> p (o d)"))\
                .then_inc(sem("ln2_in"), 16)
            pool.dma_start(lnreg[:, D:2 * D], ln2_b.partition_broadcast(P).rearrange("p o d -> p (o d)"))\
                .then_inc(sem("ln2_in"), 16)

            def expert(n, j):
                pool.wait_ge(sem("out_done"), n + 2)
                pool.wait_ge(sem("xg_done"), n * 3 + 3)
                pool.sem_inc(sem("scatters"), 1)
                pool.indirect_dma_start(out=ff_rows, out_offset=bass.IndirectOffsetOnAxis(
                    ap=erow[:, j % 2:j % 2 + 1], axis=0), in_=eout[:, j % 2, :], in_offset=None,
                    bounds_check=last_row, oob_is_err=False).then_inc(sem("rows_out"), 16)
                pool.wait_ge(sem("rows_out"), n * 16 + 16)
                pool.sem_inc(sem("rows_left"), 1)

            pool.engine_nop().then_inc(sem("rows_left"), 1)
            pool.wait_ge(sem("passes_ready"), 1)
            last_row = pool.alloc_register("last_row")
            pool.reg_mov(last_row, TOK * TOPK * 2 - 1)
            npass = pool.value_load(extra[0:1, 0:1], min_val=0, max_val=PASSES - 1) + 1
            with pool.Fori(0, npass * EXPERTS, STEP) as n:
                for j in range(STEP):
                    expert(n + j, j)


INPUTS = ["x_prompt", "x_sample", "state_pool", "state_mlstm_C", "state_mlstm_n", "state_mlstm_m", "p_prompt",
          "p_sample", "w_in", "b_i", "b_f", "w_pool", "pool_scale", "mh_g", "w_out", "ln1_g", "ln1_b", "w_router",
          "b_router", "w_mlp1", "b_mlp1", "w_mlp2", "b_mlp2", "ln2_g", "ln2_b", "w_ple", "w_ple_gate"]
OUTPUTS = [(1, SEQ, D), (SAMPLES, 1, D), (1, 1, HIST, 4 * P), (1, 1, HEADS, HD, HD), (1, 1, HEADS, HD), (1, 1, HEADS),
           (1, SAMPLES, HIST, 4 * P), (1, SAMPLES, HEADS, HD, HD), (1, SAMPLES, HEADS, HD), (1, SAMPLES, HEADS)]


def kernel(**inputs):
    import concourse.bacc as bacc
    from concourse.bass_utils import run_bass_kernel_spmd

    nc = bacc.Bacc("TRN2", target_bir_lowering=False, num_devices=1, dynamic_dma_scratch_size=8192)
    arrays = {"in_consts": constants()}
    for name in INPUTS:
        arrays[f"in_{name}"] = np.ascontiguousarray(inputs[name])
    args = [nc.dram_tensor(name, a.shape, mybir.dt.from_np(a.dtype), kind="ExternalInput").ap()
            for name, a in arrays.items()]
    args += [nc.dram_tensor(f"out_{i}", shape, F32, kind="ExternalOutput").ap() for i, shape in enumerate(OUTPUTS)]
    build(nc, *args)
    r = run_bass_kernel_spmd(nc, [arrays], core_ids=[0])
    return tuple(r.results[0][f"out_{i}"] for i in range(len(OUTPUTS)))
```

```python
from contextlib import ExitStack

import numpy as np
import concourse.bass as bass
from concourse import mybir

F32 = mybir.dt.float32
BF16 = mybir.dt.bfloat16
I32 = mybir.dt.int32
U32 = mybir.dt.uint32
ALU = mybir.AluOpType
ACT = mybir.ActivationFunctionType
AX = mybir.AxisListType

P = 128
D = 1024
KD = D // P
SEQ = 256
SAMPLES = 8
TOK = SEQ + SAMPLES
CHUNKS = [(0, P), (P, P), (SEQ, SAMPLES)]
HEADS = 4
HD = 128
HIST = 15
WINDOWS = (2, 4, 8, 16)
STATES = SAMPLES * HEADS
EXPERTS = 32
TOPK = 4
FF = 1024
PLE = 256
BLOCK = 64
PASSES = -(-TOK // BLOCK)
STEP = 4
BUFFERS = STEP
TABLE = PASSES * EXPERTS + 2 * STEP
FAR = 16384.0
ALPHA = 2.0 ** 0.25
EPS = 1e-5
LIMIT = 7.0
SIG = 1.702
SLOTS = 16
SLOT = 2048
UNITS = 12
FIRST = 4
COLUMNS_IN = (0, 512, 1024, 1536, 2048)
T_U, T_Q, T_K, T_V, T_O = range(0, 20, 4)
TILES = 20
LAST_ORDER = (0, 2, 1)
ORDER = (0, 2, 1)

C_ID, C_CAUSAL, C_BEFORE, C_ONES, C_SLOT = 0, 128, 256, 384, 512
C_EXP = 640
C_HIST = C_EXP + EXPERTS
C_CNT = C_HIST + 4 * SAMPLES
C_RANK = C_CNT + 4 * 16
C_HALF = C_RANK + 3 * TOPK
C_LIM = C_HALF + 1
C_BLK = C_LIM + 4
C_EPS = C_BLK + PASSES
C_SEL = C_EPS + 1
C_HEAD = C_SEL + TABLE
C_KIND = C_HEAD + STATES
C_END = C_KIND + 2


def constants():
    t = np.zeros((P, C_END), np.float32)
    p = np.arange(P)
    t[:, C_ID:C_ID + P] = np.eye(P)
    t[:, C_CAUSAL:C_CAUSAL + P] = p[:, None] <= p[None, :]
    t[:, C_BEFORE:C_BEFORE + P] = p[:, None] < p[None, :]
    t[:, C_ONES:C_ONES + P] = 1.0
    t[:, C_SLOT:C_SLOT + P] = (p % BLOCK)[None, :]
    t[:, C_EXP:C_EXP + EXPERTS] = np.arange(EXPERTS)
    for g, w in enumerate(WINDOWS):
        for b in range(SAMPLES):
            t[b * HIST + HIST + 1 - w:(b + 1) * HIST, C_HIST + g * SAMPLES + b] = 1.0
        t[:, C_CNT + 16 * g:C_CNT + 16 * g + 16] = w / np.minimum(np.arange(16) + 1, w)
    for c, (t0, _) in enumerate(CHUNKS):
        for k in range(TOPK):
            t[:, C_RANK + TOPK * c + k] = TOPK * (t0 + p) + k - FAR
    t[:, C_HALF] = 2 * FAR + p // BLOCK
    t[:, C_LIM:C_LIM + 4] = BLOCK * np.arange(1, 5)
    t[:, C_BLK:C_BLK + PASSES] = FAR - BLOCK * np.arange(PASSES)
    t[:, C_EPS] = EPS
    t[:, C_SEL:C_SEL + TABLE] = p[:, None] % EXPERTS == np.arange(TABLE)[None, :] % EXPERTS
    t[3 * EXPERTS:, C_SEL:C_SEL + TABLE] = 0.0
    t[:, C_HEAD:C_HEAD + STATES] = p[:, None] % HEADS == np.arange(STATES)[None, :] % HEADS
    t[:, C_KIND:C_KIND + 2] = p[:, None] // HEADS == np.arange(2)[None, :]
    return t


def build(nc, consts, x_prompt, x_sample, state_pool, state_C, state_n, state_m, p_prompt, p_sample,
          w_in, b_i, b_f, w_pool, pool_scale, mh_g, w_out, ln1_g, ln1_b, w_router, b_router,
          w_mlp1, b_mlp1, w_mlp2, b_mlp2, ln2_g, ln2_b, w_ple, w_ple_gate,
          y_prompt, y_sample, pool_prompt, C_prompt, n_prompt, m_prompt,
          pool_sample, C_sample, n_sample, m_sample):
    with ExitStack() as ctx:
        def sb(name, shape, dt=F32):
            return ctx.enter_context(nc.sbuf_tensor(name, shape, dt))

        sems = {}

        def sem(name):
            if name not in sems:
                sems[name] = ctx.enter_context(nc.semaphore(name))
            return sems[name]

        ctx.enter_context(nc.allow_non_contiguous_dma(reason="gate columns and small states"))

        ring = sb("ring", [P, SLOTS, SLOT])
        cst = sb("cst", [P, C_END])
        xreg = sb("xreg", [P, 3 * D])
        lnreg = sb("lnreg", [P, 2 * D])
        proj = sb("proj", [P, TILES, TOK])
        xT = sb("xT", [P, KD, TOK])
        mixT = sb("mixT", [P, KD, TOK])
        wgate = sb("wgate", [P, KD, 2 * HEADS])
        wpool = sb("wpool", [P, 4, P])
        hist_mix = sb("hist_mix", [P, D])
        hist = hist_mix[:, 0:4 * P]
        bias_parts = sb("bias_parts", [3 * EXPERTS, 3 * FF], BF16)
        window = sb("window", [P, 2, 16 + SEQ])
        small = sb("small", [P, 160])
        srow = sb("srow", [STATES, 7, HD])
        scol = sb("scol", [P, 4, STATES])
        stat = sb("stat", [P, 64])
        bank = [ctx.enter_context(nc.psum_tensor(f"bank{b}", [P, 512], F32)) for b in range(8)]

        logits_bank = [bank[4], bank[0], bank[1]]

        ident = cst[:, C_ID:C_ID + P]
        ones = cst[:, C_ONES:C_ONES + P]
        eps = cst[:, C_EPS:C_EPS + 1]

        xtok = xreg[:, :].rearrange("p (c d) -> p c d", c=3)
        ktok = xreg[:, 0:1024].rearrange("p (c h d) -> p c h d", c=2, h=HEADS)
        vtok = xreg[:, 1024:2048].rearrange("p (c h d) -> p c h d", c=2, h=HEADS)
        decayed = xreg[:, 2048:3072].rearrange("p (c h t) -> p c h t", c=2, h=HEADS)
        hout = lnreg[:, 0:1024].rearrange("p (c h t) -> p c h t", c=2, h=HEADS)
        vweighted = lnreg[:, 1024:1536].rearrange("p (h d) -> p h d", h=HEADS)
        CT = lnreg[:, 1536:2048].rearrange("p (h d) -> p h d", h=HEADS)
        softp = lnreg[0:HEADS, 0:256]
        logf = lnreg[0:HEADS, 256:512]
        cumf = lnreg[0:HEADS, 512:768]
        runmax = lnreg[0:HEADS, 768:1024]
        rows = lnreg[0:HEADS, 1024:1024 + 7 * P].rearrange("h (q t) -> h q t", q=7)
        ROW_G, ROW_EMT, ROW_WK, ROW_SC = 0, 2, 4, 6
        maxdiag = [xreg[0:HEADS, 2048 + 512 * c:2560 + 512 * c].rearrange("p (h t) -> p h t", h=HEADS)
                   for c in range(2)]
        gates = sb("gates", [2 * HEADS, TOK])
        gcol = small[:, 0:28]
        dec_b = small[:, 28:32]
        nstate = small[:, 32:36]
        m1 = small[0:HEADS, 37:38]
        m2 = small[0:HEADS, 38:39]
        nlast = small[0:HEADS, 39:41]
        ddiag = small[0:HEADS, 41:45]
        mhg = small[:, 45:49]
        pscale = small[:, 49:53]
        gbias = small[0:2 * HEADS, 53:54]
        histsum = small[:, 94:126]
        den = small[:, 86:90]
        den2 = small[:, 90:94]
        brout = sb("brout", [1, EXPERTS])
        ncol_out = sb("ncol_out", [HEADS, HD])
        s_gate = stat[0:STATES, 0:2]
        s_col = [stat[0:STATES, 2 + i:3 + i] for i in range(14)]
        (S_M0, S_LF, S_INTER, S_M, S_NM, S_DW, S_SC, S_EMT, S_QK, S_NQ, S_DEN, S_R, S_T, S_RSTD) = range(14)
        s_bn = stat[0:STATES, 16:22]
        s_mv = stat[0:STATES, 22:24]
        h_bn = sb("h_bn", [P, HEADS, 6])
        h_mv = stat[:, 30:38].rearrange("p (h m) -> p h m", h=HEADS)
        h_rstd = stat[:, 38:42]
        ln_bn = stat[:, 42:54]
        ln_mv = stat[:, 54:56]
        ln_rstd = stat[:, 56:57]
        sdiag = scol[0:STATES, 3, :]
        scq = sb("scq", [P, STATES])[:, :]
        s_spread = small[0:2 * HEADS, 54:86]
        ukeep = sb("ukeep", [P, 4, HIST + SAMPLES])
        urow = sb("urow", [HIST + SAMPLES, 4 * P])
        SMALL_OUTS = 4
        Cfin = window[:, :, :].rearrange("p a t -> p (a t)")[:, 0:512].rearrange("p (h d) -> p h d", h=HEADS)
        mix2 = hist_mix[0:SAMPLES, :]
        SQ, SK, SV, SN, SCQ, SY, SPROD = range(7)
        fgate = srow[0:HEADS, SCQ:SCQ + 2, :].rearrange("h i d -> h (i d)")

        def slots(s, n, width):
            return ring[:, s:s + n, :].rearrange("p s f -> p (s f)")[:, 0:width]

        Cst = slots(10, 2, STATES * HD).rearrange("p (s k) -> p s k", s=STATES)
        qb = slots(12, 2, STATES * HD).rearrange("p (s k) -> p s k", s=STATES)
        kb = slots(14, 2, STATES * HD).rearrange("p (s k) -> p s k", s=STATES)
        bsrc = ring[0:3 * EXPERTS, 14:16, :].rearrange("p s f -> p (s f)")[:, 0:3 * FF]

        moe = proj[:, :, :].rearrange("p t n -> p (t n)")
        off = [0]

        def part(n):
            off[0] += n
            return moe[:, off[0] - n:off[0]]

        info = part(6).rearrange("p (c v) -> p c v", c=3)
        logits = part(EXPERTS)
        top = part(8)
        gate4 = part(3 * TOPK).rearrange("p (c k) -> p c k", c=3)
        idx4 = part(4)
        gsum = part(4)
        oh4v = sb("oh4v", [P, TOPK, EXPERTS])
        oh4_last = sb("oh4_last", [P, TOPK, EXPERTS])[:, :, :]
        oh4 = part(3 * TOPK * EXPERTS).rearrange("p (c k e) -> p c k e", c=3, k=TOPK)
        vrow = part(2 * EXPERTS).rearrange("p (v e) -> p v e", v=2)
        posm = part(3 * EXPERTS).rearrange("p (c e) -> p c e", c=3)
        pos_table = part(3 * TABLE).rearrange("p (c n) -> p c n", c=3)
        val_table = part(6 * TABLE).rearrange("p (c n v) -> p c n v", c=3, v=2)
        mask = part(3 * EXPERTS).rearrange("p (c e) -> p c e", c=3)
        assert off[0] <= T_O * TOK
        onehot = part(3 * P).rearrange("p (c s) -> p c s", c=3)
        xgT = part(512).rearrange("p (q h s) -> p q h s", q=4, h=2)
        glu = part(512).rearrange("p (q f) -> p q f", q=2)
        lin = part(512).rearrange("p (q f) -> p q f", q=2)
        sig = part(512).rearrange("p (q f) -> p q f", q=2)
        act_out = part(512)
        assert off[0] <= TILES * TOK
        mix_flat = mixT[:, :, :].rearrange("p k n -> p (k n)")
        eout = mix_flat[:, 0:BUFFERS * 512].rearrange("p (b d) -> p b d", b=BUFFERS)
        aT = wpool[:, :, :]
        xg = hist_mix[:, 0:512].rearrange("p (q d) -> p q d", q=4)
        sel = sb("sel", [3 * EXPERTS, 2, BLOCK], BF16)
        egate = sb("egate", [P, BUFFERS])
        erow = sb("erow", [P, BUFFERS], U32)
        idx8 = sb("idx8", [P, 8], U32)
        extra = sb("extra", [P, 1], I32)
        wrout = sb("wrout", [P, KD, EXPERTS])
        x1T = xT

        q_row = nc.dram_tensor("q_row", (STATES, HD), F32).ap()
        k_row = nc.dram_tensor("k_row", (STATES, HD), F32).ap()
        ff_rows = nc.dram_tensor("ff_rows", (TOK * TOPK * 2, 512), F32).ap()

        block = ctx.enter_context(nc.Block())
        K_SCALE = HD ** -0.5

        def tile_done(t):
            if t >= 16 or t % 2:
                return "tile_act", (t + 1) // 2 if t < 16 else 8 + t - 15
            return "tile_dve", t // 2 + 1

        def unit_weights(e, u):
            if u < 8:
                return w_mlp1[0, bass.ds(e, 1), u * P:(u + 1) * P, :].rearrange("o p f -> p (o f)")
            r = u - 8
            return w_mlp2[0, bass.ds(e, 1), r * 2 * P:(r + 1) * 2 * P, :].rearrange("o (a p) f -> p (o a) f", a=2)

        def unit_place(slot, u):
            if u < 8:
                return ring[:, slot, :]
            return ring[:, slot, :].rearrange("p (a f) -> p a f", a=2)

        def ff_sum(c):
            return slots(10 + 2 * c, 2, 4096).rearrange("p (k d) -> p k d", k=TOPK)

        def slot_of(body_unit):
            return (FIRST + body_unit) % SLOTS

        def landings(body_unit):
            s = slot_of(body_unit)
            return sum(slot_of(v) == s for v in range(body_unit + 1))

        before = [2 if s < 4 else 1 if s < 10 else 0 for s in range(SLOTS)]

        @block.sync
        def _(sp):
            for c, (t0, n) in enumerate(CHUNKS):
                src = x_prompt[0, t0:t0 + n, :] if c < 2 else x_sample[:, 0, :]
                sp.dma_start(xtok[0:n, c, :], src).then_inc(sem(f"x_in{c}"), 16)

            def load_block(b):
                col = COLUMNS_IN[b]
                for half in range(2):
                    s = 2 * b + half
                    sp.dma_start(ring[:, s, :].rearrange("p (k n) -> p k n", k=4),
                                 w_in[0, 512 * half:512 * half + 512, col:col + 512]
                                 .rearrange("(k p) n -> p k n", p=P)).then_inc(sem(f"slot{s}"), 16)

            load_block(0)
            load_block(1)
            load_block(2)
            for g in range(3):
                rows_ = slice(g * EXPERTS, (g + 1) * EXPERTS)
                sp.dma_start(bsrc[rows_, 0:2 * FF], b_mlp1[0]).then_inc(sem("bias_in"), 16)
                sp.dma_start(bsrc[rows_, 2 * FF:3 * FF], b_mlp2[0]).then_inc(sem("bias_in"), 16)
            load_block(3)
            load_block(4)
            sp.dma_start(Cst, state_C[0].rearrange("b h v k -> v (b h) k")).then_inc(sem("cq_in"), 16)
            def load_w_out(s):
                sp.wait_ge(sem("tile_ps"), 4 * (s // 2) + 4)
                sp.dma_start(ring[:, s, :].rearrange("p (k n) -> p k n", k=2),
                             w_out[0, 256 * s:256 * s + 256, :].rearrange("(k p) n -> p k n", p=P))\
                  .then_inc(sem(f"slot{s}"), 16)

            load_w_out(0)
            load_w_out(1)
            sp.wait_ge(sem("srow_ready"), 1)
            sp.dma_start(q_row, srow[:, SQ, :]).then_inc(sem("qk_row"), 16)
            sp.wait_ge(sem("qk_row"), 16)
            sp.dma_start(qb, q_row.partition_broadcast(P)).then_inc(sem("cq_in"), 16)
            load_w_out(2)
            load_w_out(3)
            sp.wait_ge(sem("srow_ready"), 2)
            sp.dma_start(k_row, srow[:, SK, :]).then_inc(sem("qk_row"), 16)
            sp.wait_ge(sem("qk_row"), 32)
            sp.wait_ge(sem("bias_cast"), 3)
            sp.dma_start(kb, k_row.partition_broadcast(P)).then_inc(sem("kb_in"), 16)

            def load_unit(e, j, u):
                s = slot_of(UNITS * j + u)
                sp.dma_start(unit_place(s, u), unit_weights(e, u)).then_inc(sem(f"slot{s}"), 16)

            for n in range(UNITS * STEP):
                s = slot_of(n)
                if n < UNITS:
                    if s < 10:
                        sp.wait_ge(sem("tile_ps"), 4 * (s // 2) + 4)
                    if s == 8:
                        sp.wait_ge(sem("mem_ps"), 2)
                        for c in range(2):
                            sp.dma_start(xtok[:, c, :], x_prompt[0, c * P:(c + 1) * P, :]).then_inc(sem("x_again"), 16)
                        sp.dma_start(xtok[0:SAMPLES, 2, :], x_sample[:, 0, :]).then_inc(sem("x_again"), 16)
                    if s == 10:
                        sp.wait_ge(sem("hT_ps"), 2)
                        sp.dma_start(lnreg[:, 0:D], ln1_g.partition_broadcast(P).rearrange("p o d -> p (o d)"))\
                          .then_inc(sem("ln1_in"), 16)
                        sp.wait_ge(sem("cfin_ps"), 2)
                        sp.dma_start(lnreg[:, D:2 * D], ln1_b.partition_broadcast(P).rearrange("p o d -> p (o d)"))\
                          .then_inc(sem("ln1_in"), 16)
                        sp.wait_ge(sem("C_out"), 16)
                    elif s == 12:
                        sp.wait_ge(sem("Cnew_done"), 1)
                        sp.wait_ge(sem("scq_ready"), 1)
                elif n < SLOTS:
                    sp.wait_ge(sem("mix_ps"), 5)
                else:
                    sp.wait_ge(sem("units_used"), n - SLOTS + 1)
                load_unit(n // UNITS, n // UNITS, n % UNITS)

            def load_body(e, done):
                for n in range(UNITS * STEP):
                    sp.wait_ge(sem("units_used"), done + (n - SLOTS + 1))
                    load_unit(e + n // UNITS, n // UNITS, n % UNITS)

            bodies = EXPERTS // STEP
            with sp.Fori(1, bodies) as i:
                load_body(i * STEP, i * (STEP * UNITS))
            sp.wait_ge(sem("passes_ready"), 1)
            npass = sp.value_load(extra[0:1, 0:1], min_val=0, max_val=PASSES - 1) + 1
            with sp.If(npass > 1):
                with sp.Fori(1, npass) as b:
                    with sp.Fori(0, bodies) as i:
                        load_body(i * STEP, b * (EXPERTS * UNITS) + i * (STEP * UNITS))
            sp.nop()

            used = npass * (EXPERTS * UNITS)

            def wait_slot(s):
                sp.wait_ge(sem("units_used"), used + ((s - FIRST) % SLOTS + 1 - SLOTS))

            def load_gate_weights(i):
                sp.dma_start(ring[:, 4 + i, :].rearrange("p (k n) -> p k n", k=2),
                             w_ple_gate[0, 256 * i:256 * i + 256, :].rearrange("(k p) n -> p k n", p=P))\
                  .then_inc(sem(f"slot{4 + i}"), 16)

            wait_slot(9)
            sp.dma_start(ring[:, 8, :].rearrange("p (k n) -> p k n", k=2),
                         w_ple[0].rearrange("(k p) n -> p k n", p=P)).then_inc(sem("ple_in"), 16)
            for c, (t0, n) in enumerate(CHUNKS):
                src = p_prompt[0, 0, t0:t0 + n, :] if c < 2 else p_sample[0, :, 0, :]
                sp.dma_start(ring[0:n, 9, c * PLE:(c + 1) * PLE], src).then_inc(sem("ple_in"), 16)
            load_gate_weights(0)
            sent = npass * (16 * EXPERTS // STEP) + 16
            for j in range(BUFFERS):
                sp.wait_ge(sem(f"rows_out{j}"), sent)
            for c in LAST_ORDER:
                t0, n = CHUNKS[c]
                for part_ in range(2):
                    sp.dma_start(ff_sum(c)[0:n, 2 * part_:2 * part_ + 2, :].rearrange("p k d -> p (k d)"),
                                 ff_rows.rearrange("(t r) f -> t (r f)", r=2 * TOPK)
                                 [t0:t0 + n, 2048 * part_:2048 * part_ + 2048]).then_inc(sem(f"ff_in{part_}{c}"), 16)
                if c == 2:
                    for i in range(1, 4):
                        load_gate_weights(i)
            for i, c in enumerate(LAST_ORDER):
                t0, n = CHUNKS[c]
                dst = y_prompt[0, t0:t0 + n, :] if c < 2 else y_sample[:, 0, :]
                for half in range(2):
                    sp.wait_ge(sem("y_done"), 2 * i + half + 1)
                    s = slice(512 * half, 512 * half + 512)
                    sp.dma_start(dst[:, s], xtok[0:n, c, s]).then_inc(sem("y_out"), 16)
            sp.wait_ge(sem("y_out"), 96)
            sp.wait_ge(sem("C_out"), 16)
            sp.wait_ge(sem("small_out"), 16 * SMALL_OUTS)

        @block.tensor
        def _(pe):
            pe.wait_ge(sem("cst_in"), 16)
            for g in range(6):
                c, half = g // 2, g % 2
                n = CHUNKS[c][1]
                if half == 0:
                    pe.wait_ge(sem(f"x_in{c}"), 16)
                for k in range(4):
                    last = pe.transpose(bank[g][:, k * P:k * P + n],
                                        xtok[0:n, c, (4 * half + k) * P:(4 * half + k + 1) * P], ident[0:n, 0:n])
                last.then_inc(sem("xT_ps"), 1)
            pe.wait_ge(sem("xT_dve"), 3)
            pe.wait_ge(sem("xT_act"), 3)
            pe.wait_ge(sem("gate_in"), 48)
            for k in range(KD):
                last = pe.matmul(bank[6][0:2 * HEADS, 0:TOK], wgate[:, k, :], xT[:, k, :],
                                 start=(k == 0), stop=(k == KD - 1))
            last.then_inc(sem("gates_ps"), 1)
            pe.wait_ge(sem("hist_in"), 16)
            for g in range(4):
                last = pe.matmul(bank[7][:, g * SAMPLES:(g + 1) * SAMPLES], hist[0:SAMPLES * HIST, g * P:(g + 1) * P],
                                 cst[0:SAMPLES * HIST, C_HIST + g * SAMPLES:C_HIST + (g + 1) * SAMPLES],
                                 start=True, stop=True)
            last.then_inc(sem("hist_ps"), 1)

            def project(t):
                b, j = t // 4, t % 4
                if t >= 2:
                    name, count = tile_done(t - 2)
                    pe.wait_ge(sem(name), count)
                for k in range(KD):
                    s = 2 * b + k // 4
                    if j == 0 and k % 4 == 0:
                        pe.wait_ge(sem(f"slot{s}"), 16)
                    w = ring[:, s, :].rearrange("p (k n) -> p k n", k=4)
                    last = pe.matmul(bank[t % 2][:, 0:TOK], w[:, k % 4, j * P:(j + 1) * P], xT[:, k, :],
                                     start=(k == 0), stop=(k == KD - 1))
                last.then_inc(sem("tile_ps"), 1)

            def turn_tokens(dst, first_tile, c):
                for h in range(HEADS):
                    last = pe.transpose(dst[:, h * P:(h + 1) * P], proj[:, first_tile + h, c * P:(c + 1) * P], ident)
                return last

            def pool_mix(g):
                pe.wait_ge(sem("z_ready"), g + 1)
                if g == 0:
                    pe.wait_ge(sem("pool_in"), 48)
                    pe.wait_ge(sem("gcol_done"), 1)
                else:
                    pe.wait_ge(sem("pool_done"), g)
                pe.matmul(bank[7][:, 0:TOK], wpool[:, g, :], proj[:, T_U + g, :], start=True, stop=True)\
                  .then_inc(sem("pool_ps"), 1)

            def values(c, dst, dden):
                for h in range(HEADS):
                    pe.matmul(dst[:, h * P:(h + 1) * P], decayed[:, c, h, :], vtok[:, c, h, :], start=True, stop=True)
                for h in range(HEADS):
                    last = pe.matmul(dden[:, h:h + 1], decayed[:, c, h, :], ones[:, 0:1], start=True, stop=True)
                return last

            def memory(c, dst, dn):
                for h in range(HEADS):
                    pe.matmul(dst[:, h * P:(h + 1) * P], ktok[:, c, h, :], vweighted[:, h, :], start=True, stop=True)
                for h in range(HEADS):
                    w0 = 4 * (ROW_WK + c) + h
                    last = pe.matmul(dn[:, h:h + 1], ktok[:, c, h, :], gcol[:, w0:w0 + 1], start=True, stop=True)
                return last

            def turn_heads(c):
                pe.wait_ge(sem("hn_ready"), c + 1)
                if c:
                    pe.wait_ge(sem("hT_done"), c)
                for h in range(HEADS):
                    last = pe.transpose(bank[6][:, h * P:(h + 1) * P], hout[:, c, h, :], ident)
                last.then_inc(sem("hT_ps"), 1)

            project(0)
            pe.wait_ge(sem("gates_done"), 1)
            pe.matmul(bank[5][0:HEADS, 0:SEQ], ident[0:2 * HEADS, HEADS:2 * HEADS], gates[:, 0:SEQ],
                      start=True, stop=True)
            pe.wait_ge(sem("spread_ready"), 1)
            pe.matmul(bank[5][0:STATES, SEQ:SEQ + 2], s_spread, cst[0:2 * HEADS, C_KIND:C_KIND + 2],
                      start=True, stop=True).then_inc(sem("gates_ps"), 1)
            for t in range(1, 6):
                project(t)
            pe.wait_ge(sem("hist_done"), 1)
            pe.wait_ge(sem("rows_ready"), 1)
            for q in range(7):
                pe.transpose(bank[7][:, 4 * q:4 * q + 4], rows[:, q, :], ident[0:HEADS, 0:HEADS])
            pe.matmul(bank[7][:, 28:32], ones[0:HEADS, :], ddiag, start=True, stop=True).then_inc(sem("gcol_ps"), 1)
            for c in range(2):
                pe.matmul(bank[2 + c][:, :], ones[0:HEADS, :], maxdiag[c].rearrange("p h t -> p (h t)"),
                          start=True, stop=True).then_inc(sem("scores_ps"), 1)
            def sample_rows(i):
                pe.wait_ge(sem("scol_ready"), i + 1)
                if i == 0:
                    pe.wait_ge(sem("gates_done"), 1)
                else:
                    pe.wait_ge(sem("srow_ready"), i)
                pe.transpose(bank[6][0:STATES, i * HD:(i + 1) * HD], scol[:, i, :], ident).then_inc(sem("srow_ps"), 1)

            for t in range(6, 9):
                project(t)
            sample_rows(0)
            for t in range(9, 13):
                project(t)
            pe.wait_ge(sem("tile_dve"), 6)
            pe.wait_ge(sem("tile_act"), 6)
            turn_tokens(bank[4], T_K, 0).then_inc(sem("tok_ps"), 1)
            turn_tokens(bank[5], T_K, 1).then_inc(sem("tok_ps"), 1)
            sample_rows(1)
            project(13)
            pe.wait_ge(sem("ktok_done"), 2)
            for c in range(2):
                for h in range(HEADS):
                    last = pe.matmul(bank[4 + c][:, h * P:(h + 1) * P], proj[:, T_K + h, c * P:(c + 1) * P],
                                     proj[:, T_Q + h, c * P:(c + 1) * P], start=True, stop=True)
                last.then_inc(sem("scores_ps"), 1)
            pool_mix(0)
            project(14)
            pe.wait_ge(sem("sdiag_ready"), 1)
            pe.wait_ge(sem("srow_ready"), 2)
            pe.matmul(bank[6][:, 0:STATES], ones[0:STATES, :], sdiag, start=True, stop=True).then_inc(sem("sbc_ps"), 1)
            pool_mix(1)
            project(15)
            pool_mix(2)
            project(16)
            pe.wait_ge(sem("lag_ready"), 8)
            pe.wait_ge(sem("tile_dve"), 8)
            pe.wait_ge(sem("tile_act"), 8)
            turn_tokens(bank[2], T_V, 0).then_inc(sem("tok_ps"), 1)
            turn_tokens(bank[3], T_V, 1).then_inc(sem("tok_ps"), 1)
            pe.wait_ge(sem("sbc_done"), 1)
            sample_rows(2)
            pool_mix(3)
            project(17)
            pe.wait_ge(sem("decayed_ready"), 1)
            pe.wait_ge(sem("vtok_done"), 2)
            values(0, bank[2], bank[3][:, 0:4]).then_inc(sem("num_ps"), 1)
            pe.wait_ge(sem("vw_ready"), 1)
            memory(0, bank[4], bank[3][:, 4:8]).then_inc(sem("mem_ps"), 1)
            project(18)
            pe.wait_ge(sem("sdiag_ready"), 2)
            pe.transpose(bank[6][:, STATES:2 * STATES], srow[:, SV, :], ident[0:STATES, 0:STATES])\
              .then_inc(sem("sbc_ps"), 1)
            pe.wait_ge(sem("decayed_ready"), 2)
            pe.wait_ge(sem("num_done"), 1)
            values(1, bank[5], bank[3][:, 8:12])
            for h in range(HEADS):
                pe.matmul(bank[2][:, h * P:(h + 1) * P], proj[:, T_Q + h, P:2 * P], CT[:, h, :], start=True, stop=True)
            for h in range(HEADS):
                last = pe.matmul(bank[3][:, 12 + h:13 + h], proj[:, T_Q + h, P:2 * P], nstate[:, h:h + 1],
                                 start=True, stop=True)
            last.then_inc(sem("num_ps"), 1)
            pe.wait_ge(sem("vw_ready"), 2)
            memory(1, bank[4], bank[3][:, 16:20]).then_inc(sem("mem_ps"), 1)
            project(19)
            pe.wait_ge(sem("pool_done"), 4)
            for g in range(4):
                last = pe.transpose(bank[7][0:HIST + SAMPLES, g * P:(g + 1) * P], ukeep[:, g, :], ident)
            last.then_inc(sem("cfin_ps"), 1)

            def mix(c, banks, ks):
                t0, n = CHUNKS[c]
                for half in range(2):
                    for k in ks:
                        w = ring[:, k // 2, :].rearrange("p (k n) -> p k n", k=2)
                        last = pe.matmul(banks[half][0:n, :], mixT[:, k, t0:t0 + n],
                                         w[:, k % 2, half * 512:half * 512 + 512], start=(k == 0), stop=(k == KD - 1))
                    if ks[-1] == KD - 1:
                        last.then_inc(sem("mix_ps"), 1)

            def router(i):
                c = ORDER[i]
                t0, n = CHUNKS[c]
                for half in range(2):
                    g = 2 * i + half
                    pe.wait_ge(sem("ln1_ready"), g + 1)
                    if g >= 2:
                        pe.wait_ge(sem("x1T_done"), g - 1)
                    for k in range(4):
                        kk = 4 * half + k
                        last = pe.transpose(bank[6 + half][:, k * P:k * P + n],
                                            xtok[0:n, c, kk * P:(kk + 1) * P], ident[0:n, 0:n])
                    last.then_inc(sem("x1T_ps"), 1)
                if i == 0:
                    pe.wait_ge(sem("wrout_in"), 32)
                pe.wait_ge(sem("x1T_done"), 2 * i + 2)
                pe.matmul(logits_bank[i][0:n, 0:EXPERTS], ones[0:1, 0:n], brout[:, :], start=True, stop=False)
                for k in range(KD):
                    last = pe.matmul(logits_bank[i][0:n, 0:EXPERTS], x1T[:, k, t0:t0 + n], wrout[:, k, :],
                                     start=False, stop=(k == KD - 1))
                last.then_inc(sem("logits_ps"), 1)

            for s in range(4):
                pe.wait_ge(sem(f"slot{s}"), 32)
            pe.wait_ge(sem("tile_act"), 12)
            first, second = (bank[0], bank[1]), (bank[2], bank[5])
            mix(0, first, range(4))
            pe.wait_ge(sem("sbc_done"), 2)
            turn_heads(0)
            pe.wait_ge(sem("num_done"), 2)
            mix(1, second, range(4))
            pe.wait_ge(sem("cfin_done"), 1)
            pe.wait_ge(sem("scq_ready"), 1)
            pe.transpose(bank[7][0:STATES, 0:P], scq, ident).then_inc(sem("scq_ps"), 1)
            pe.wait_ge(sem("hT_done"), 1)
            mix(0, first, range(4, KD))
            turn_heads(1)
            pe.wait_ge(sem("ct_ready"), 2)
            for h in range(HEADS):
                pe.transpose(bank[4][:, h * P:(h + 1) * P], CT[:, h, :], ident)
            pe.transpose(bank[3][0:HEADS, 0:P], nstate, ident).then_inc(sem("cfin_ps"), 1)
            pe.wait_ge(sem("sh_ready"), 1)
            pe.transpose(bank[7][:, P:P + STATES], srow[:, SY, :], ident[0:STATES, 0:STATES])\
              .then_inc(sem("scq_ps"), 1)
            pe.wait_ge(sem("shT_done"), 1)
            pe.wait_ge(sem("cfin_done"), 3)
            for k in range(KD):
                w = ring[:, k // 2, :].rearrange("p (k n) -> p k n", k=2)
                for q in range(4):
                    last = pe.matmul(bank[3][32 * q:32 * q + SAMPLES, 0:256], mixT[:, k, SEQ:TOK],
                                     w[:, k % 2, 256 * q:256 * q + 256], start=(k == 0), stop=(k == KD - 1))
            last.then_inc(sem("mix_ps"), 1)
            pe.wait_ge(sem("hT_done"), 2)
            mix(1, second, range(4, KD))
            router(0)
            router(1)
            router(2)
            def count_places(chunks):
                for a in chunks:
                    m = CHUNKS[a][1]
                    for c in range(a, 3):
                        left = cst[0:m, C_BEFORE:C_BEFORE + P] if a == c else ones[0:m, :]
                        pe.matmul(bank[3][:, c * EXPERTS:(c + 1) * EXPERTS], left, mask[0:m, a, :],
                                  start=(a == 0 and c == 0), stop=False)
                    last = pe.matmul(bank[3][:, 3 * EXPERTS:4 * EXPERTS], ones[0:m, :], mask[0:m, a, :],
                                     start=False, stop=(a == 1))
                return last

            pe.wait_ge(sem("mask_ready"), 2)
            pe.wait_ge(sem("mix2_done"), 4)
            count_places((0, 2))
            pe.wait_ge(sem("mask_ready"), 3)
            count_places((1,)).then_inc(sem("pos_ps"), 1)

            def gather():
                for c, (_, n) in enumerate(CHUNKS):
                    pe.matmul(bank[5][:, 0:2], onehot[0:n, c, :], info[0:n, c, :], start=(c == 0), stop=(c == 2))
                for c, (_, n) in enumerate(CHUNKS):
                    for h in range(2):
                        last = pe.matmul(bank[2][BLOCK * h:BLOCK * (h + 1), :], onehot[0:n, c, 0:BLOCK],
                                         xtok[0:n, c, 512 * h:512 * h + 512], start=(c == 0), stop=(c == 2))
                last.then_inc(sem("gathered"), 1)

            def turn_gathered():
                for q in range(4):
                    last = pe.transpose(bank[6][:, q * P:(q + 1) * P], xg[:, q, :], ident)
                last.then_inc(sem("xgT_ps"), 1)

            def expert(n, j):
                i4 = n - j
                pe.wait_ge(sem("xg_done"), n * 3 + 3)
                pe.wait_ge(sem("h_read"), n + 1)
                for t in range(2):
                    for q in range(2):
                        col = FF * t + 512 * q
                        pe.matmul(bank[q][BLOCK * t:BLOCK * (t + 1), :], sel[:, j % 2, :],
                                  bias_parts[:, col:col + 512], start=True, stop=False)
                for k in range(KD):
                    u = UNITS * j + k
                    s = slot_of(u)
                    pe.wait_ge(sem(f"slot{s}"), i4 * 12 + 16 * (before[s] + landings(u)))
                    for q in range(2):
                        for t in range(2):
                            col = FF * t + 512 * q
                            last = pe.matmul(bank[q][BLOCK * t:BLOCK * (t + 1), :], xgT[:, k % 4, k // 4, :],
                                             ring[:, s, col:col + 512], start=False, stop=(k == KD - 1))
                    last.then_inc(sem("units_used"), 1)
                pe.wait_ge(sem("onehot_ready"), n * 3 + 6)
                gather()
                pe.wait_ge(sem("act_ready"), n + 1)
                for m in range(4):
                    last = pe.transpose(bank[3][:, m * P:(m + 1) * P], act_out[:, m * P:(m + 1) * P], ident)
                last.then_inc(sem("aT_ps"), 1)
                pe.wait_ge(sem("xg_copied"), n + 2)
                turn_gathered()
                pe.wait_ge(sem("aT_done"), n + 1)
                pe.wait_ge(sem("out_done"), n + 1)
                for h in range(2):
                    pe.matmul(bank[4][BLOCK * h:BLOCK * (h + 1), :], sel[:, j % 2, :],
                              bias_parts[:, 2 * FF + 512 * h:2 * FF + 512 * h + 512], start=True, stop=False)
                for k in range(8):
                    u = UNITS * j + 8 + k // 2
                    s = slot_of(u)
                    if k % 2 == 0:
                        pe.wait_ge(sem(f"slot{s}"), i4 * 12 + 16 * (before[s] + landings(u)))
                    w = ring[:, s, :].rearrange("p (a f) -> p a f", a=2)
                    t, m = k // 4, k % 4
                    for h in range(2):
                        last = pe.matmul(bank[4][BLOCK * h:BLOCK * (h + 1), :], aT[:, m, BLOCK * t:BLOCK * (t + 1)],
                                         w[:, k % 2, 512 * h:512 * h + 512], start=False, stop=(k == 7))
                    if k % 2 == 1:
                        last.then_inc(sem("units_used"), 1)

            pe.wait_ge(sem("onehot_ready"), 3)
            gather()
            pe.wait_ge(sem("xg_copied"), 1)
            turn_gathered()
            pe.wait_ge(sem("passes_ready"), 1)
            npass = pe.value_load(extra[0:1, 0:1], min_val=0, max_val=PASSES - 1) + 1
            with pe.Fori(0, npass * EXPERTS, STEP) as n:
                for j in range(STEP):
                    expert(n + j, j)

            pe.wait_ge(sem("out_done"), npass * EXPERTS + 1)
            pe.wait_ge(sem("xg_done"), npass * (3 * EXPERTS) + 3)
            pe.wait_ge(sem("ple_in"), 64)
            for c, (t0, n) in enumerate(CHUNKS):
                for k in range(2):
                    last = pe.transpose(bank[c][:, k * P:k * P + n],
                                        ring[0:n, 9, c * PLE + k * P:c * PLE + (k + 1) * P], ident[0:n, 0:n])
                last.then_inc(sem("pT_ps"), 1)
            pT = ring[:, 9, 768:768 + 2 * TOK].rearrange("p (k n) -> p k n", k=2)
            wple_sb = ring[:, 8, :].rearrange("p (k n) -> p k n", k=2)

            def gate_weights(k):
                return ring[:, 4 + k // 2, :].rearrange("p (k n) -> p k n", k=2)[:, k % 2, :]

            weights_in = npass * (16 * EXPERTS * UNITS // SLOTS) + 16 * (before[4] + 1)
            assert all(before[4 + i] == before[4] for i in range(4))
            gate_banks = {0: (bank[0], bank[1]), 1: (bank[2], bank[3])}

            def embedding(i):
                c = LAST_ORDER[i]
                t0, n = CHUNKS[c]
                for half in range(2):
                    g = 2 * i + half
                    if g >= 2:
                        pe.wait_ge(sem("ple_done"), g - 1)
                    for k in range(2):
                        last = pe.matmul(bank[4 + half][0:n, :], pT[:, k, t0:t0 + n],
                                         wple_sb[:, k, half * 512:half * 512 + 512], start=(k == 0), stop=(k == 1))
                    last.then_inc(sem("ple_ps"), 1)

            def turn_x2(i):
                c = LAST_ORDER[i]
                n = CHUNKS[c][1]
                for half in range(2):
                    g = 2 * i + half
                    pe.wait_ge(sem("ln2_ready"), g + 1)
                    if g >= 2:
                        pe.wait_ge(sem("x2T_done"), g - 1)
                    for k in range(4):
                        kk = 4 * half + k
                        last = pe.transpose(bank[6 + half][:, k * P:k * P + n],
                                            xtok[0:n, c, kk * P:(kk + 1) * P], ident[0:n, 0:n])
                    last.then_inc(sem("x2T_ps"), 1)

            def gates_half(i, half):
                c = LAST_ORDER[i]
                t0, n = CHUNKS[c]
                pe.wait_ge(sem("x2T_done"), 2 * i + 2)
                for k in range(KD):
                    if i == 0 and half == 0 and k % 2 == 0:
                        pe.wait_ge(sem(f"slot{4 + k // 2}"), weights_in)
                    last = pe.matmul(gate_banks[c][half][0:n, :], x1T[:, k, t0:t0 + n],
                                     gate_weights(k)[:, half * 512:half * 512 + 512],
                                     start=(k == 0), stop=(k == KD - 1))
                last.then_inc(sem("gate_ps"), 1)

            pe.wait_ge(sem("pT_done"), 3)
            embedding(0)
            embedding(1)
            embedding(2)
            turn_x2(0)
            gates_half(0, 0)
            turn_x2(1)
            gates_half(0, 1)
            pe.wait_ge(sem("x2T_done"), 4)
            pe.wait_ge(sem("ple_done"), 6)
            for k in range(KD):
                for q in range(4):
                    last = pe.matmul(bank[4][32 * q:32 * q + SAMPLES, 0:256], x1T[:, k, SEQ:TOK],
                                     gate_weights(k)[:, 256 * q:256 * q + 256], start=(k == 0), stop=(k == KD - 1))
            last.then_inc(sem("gate_ps"), 2)
            turn_x2(2)
            gates_half(2, 0)
            gates_half(2, 1)

        @block.vector
        def _(dve):
            counts = {}

            def step(ins, name="dve_chain"):
                counts[name] = counts.get(name, 0) + 1
                ins.then_inc(sem(name), 1)
                dve.wait_ge(sem(name), counts[name])

            TT = dve.tensor_tensor
            TS = dve.tensor_scalar
            STT = dve.scalar_tensor_tensor

            def over(col, shape):
                return col.to_broadcast(shape)

            for g in (0, 2, 4):
                c = g // 2
                t0, n = CHUNKS[c]
                dve.wait_ge(sem("xT_ps"), g + 1)
                dve.tensor_copy(xT[:, 0:4, t0:t0 + n], bank[g][:, :].rearrange("p (k t) -> p k t", k=4)[:, :, 0:n])\
                   .then_inc(sem("xT_dve"), 1)
            dve.wait_ge(sem("hist_ps"), 1)
            dve.tensor_copy(histsum, bank[7][:, 0:32]).then_inc(sem("hist_done"), 1)

            def empty_tile(t):
                dve.wait_ge(sem("tile_ps"), t + 1)
                if T_K <= t < T_V:
                    ins = TS(proj[:, t, :], bank[t % 2][:, 0:TOK], K_SCALE, None, ALU.mult)
                else:
                    ins = dve.tensor_copy(proj[:, t, :], bank[t % 2][:, 0:TOK])
                ins.then_inc(sem("tile_dve"), 1)

            def more(ins, name="dve_chain"):
                counts[name] = counts.get(name, 0) + 1
                ins.then_inc(sem(name), 1)

            empty_tile(0)
            dve.wait_ge(sem("gates_done"), 1)
            step(TT(s_spread.rearrange("g (b h) -> g b h", h=HEADS),
                    gates[:, SEQ:TOK].unsqueeze(2).to_broadcast([2 * HEADS, SAMPLES, HEADS]),
                    cst[0:2 * HEADS, C_HEAD:C_HEAD + STATES].rearrange("g (b h) -> g b h", h=HEADS), ALU.mult),
                 "spread_ready")
            dve.wait_ge(sem("gates_ps"), 2)
            step(dve.tensor_copy(fgate[:, :], bank[5][0:HEADS, 0:SEQ]))
            step(STT(softp, fgate[:, :], -1.0, fgate[:, :], ALU.mult, ALU.min), "soft_ready")
            empty_tile(2)
            dve.wait_ge(sem("soft_done"), 1)
            step(STT(logf, fgate[:, :], 0.0, softp, ALU.min, ALU.subtract))
            for c in range(2):
                s = slice(c * P, (c + 1) * P)
                step(dve.tensor_tensor_scan(cumf[:, s], ones[0:HEADS, :], logf[:, s], 0.0, ALU.mult, ALU.add))
                step(TT(rows[:, ROW_G + c, :], gates[0:HEADS, s], cumf[:, s], ALU.subtract))
                step(dve.tensor_tensor_scan(runmax[:, s], rows[:, ROW_G + c, :], rows[:, ROW_G + c, :],
                                            m1 if c else 0.0, ALU.max, ALU.max))
                e = (c + 1) * P - 1
                step(TT(m2 if c else m1, cumf[:, e:e + 1], runmax[:, e:e + 1], ALU.add))
                step(TS(nlast[:, c:c + 1], runmax[:, e:e + 1], -1.0, None, ALU.mult))
                step(TT(rows[:, ROW_EMT + c, :], cumf[:, s], runmax[:, s], ALU.add))
                step(TT(maxdiag[c], runmax[:, s].unsqueeze(1).to_broadcast([HEADS, HEADS, P]),
                        ident[0:HEADS, 0:HEADS].unsqueeze(2).to_broadcast([HEADS, HEADS, P]), ALU.mult),
                     "runmax_ready")
            empty_tile(4)
            dve.wait_ge(sem("rows_parts"), 4)
            step(TS(ddiag, ident[0:HEADS, 0:HEADS], rows[:, ROW_SC, P - 1:P], None, ALU.mult), "rows_ready")
            step(dve.tensor_copy(s_gate, bank[5][0:STATES, SEQ:SEQ + 2]))
            dve.wait_ge(sem("states_in"), 32)
            f_, i_ = s_gate[:, 1:2], s_gate[:, 0:1]
            step(STT(s_col[S_T], f_, -1.0, f_, ALU.mult, ALU.min), "soft_ready")
            dve.wait_ge(sem("gcol_ps"), 1)
            step(dve.tensor_copy(small[:, 0:32], bank[7][:, 0:32]), "gcol_done")
            for c in range(2):
                dve.wait_ge(sem("scores_ps"), c + 1)
                for h in range(HEADS):
                    g0 = 4 * (ROW_G + c) + h
                    more(TS(decayed[:, c, h, :], bank[2 + c][:, h * P:(h + 1) * P], gcol[:, g0:g0 + 1], 0.0,
                            ALU.subtract, ALU.max), "lag_ready")
            def sample_columns(i):
                more(dve.tensor_copy(scol[:, i, :].rearrange("p (b h) -> p b h", h=HEADS),
                                     proj[:, T_Q + 4 * i:T_Q + 4 * i + 4, SEQ:TOK].rearrange("p h b -> p b h")),
                     "scol_ready")

            empty_tile(6)
            dve.wait_ge(sem("bias_cast"), 1)
            step(TT(bsrc[0:2 * EXPERTS, :], bsrc[0:2 * EXPERTS, :], bias_parts[0:2 * EXPERTS, :], ALU.subtract),
                 "bias_rest")
            dve.wait_ge(sem("tile_act"), 4)
            dve.wait_ge(sem("tile_dve"), 4)
            sample_columns(0)
            empty_tile(8)
            dve.wait_ge(sem("srow_ps"), 1)
            step(dve.tensor_copy(srow[:, SQ, :], bank[6][0:STATES, 0:HD]), "srow_ready")
            dve.wait_ge(sem("soft_done"), 2)
            step(STT(s_col[S_LF], f_, 0.0, s_col[S_T], ALU.min, ALU.subtract))
            step(TT(s_col[S_INTER], s_col[S_M0], s_col[S_LF], ALU.add))
            step(TT(s_col[S_M], s_col[S_INTER], i_, ALU.max))
            step(TS(s_col[S_NM], s_col[S_M], -1.0, None, ALU.mult), "s_m_ready")
            dve.wait_ge(sem("bias_cast"), 2)
            step(TT(bsrc[0:EXPERTS, :], bsrc[0:EXPERTS, :], bias_parts[0:EXPERTS, :], ALU.subtract), "bias_rest")
            empty_tile(10)

            dve.wait_ge(sem("tile_act"), 6)
            dve.wait_ge(sem("tile_dve"), 6)
            sample_columns(1)
            for c in range(2):
                dve.wait_ge(sem("decay_act"), c + 1)
                more(TT(decayed[:, c], decayed[:, c], cst[:, C_CAUSAL:C_CAUSAL + P].unsqueeze(1)
                        .to_broadcast([P, HEADS, P]), ALU.mult))
            empty_tile(12)
            dve.wait_ge(sem("tok_ps"), 1)
            dve.tensor_copy(ktok[:, 0], bank[4][:, :].rearrange("p (h d) -> p h d", h=HEADS)).then_inc(sem("ktok_done"), 1)
            dve.wait_ge(sem("srow_ps"), 2)
            step(dve.tensor_copy(srow[:, SK, :], bank[6][0:STATES, HD:2 * HD]), "srow_ready")
            step(dve.tensor_tensor_reduce(srow[:, SPROD, :], srow[:, SQ, :], srow[:, SK, :], 1.0, 0.0, ALU.mult, ALU.add,
                                          s_col[S_QK]))
            step(dve.tensor_tensor_reduce(srow[:, SPROD, :], srow[:, SQ, :], srow[:, SN, :], 1.0, 0.0, ALU.mult, ALU.add,
                                          s_col[S_NQ]))
            dve.wait_ge(sem("s_exp_done"), 3)
            step(TT(s_col[S_T], s_col[S_QK], s_col[S_DW], ALU.mult))
            step(STT(s_col[S_DEN], s_col[S_NQ], s_col[S_SC], s_col[S_T], ALU.mult, ALU.add))
            step(TS(srow[:, SPROD, :], srow[:, SK, :], s_col[S_DW], None, ALU.mult))
            step(STT(srow[:, SN, :], srow[:, SN, :], s_col[S_SC], srow[:, SPROD, :], ALU.mult, ALU.add), "sn_ready")
            step(TS(sdiag, ident[0:STATES, 0:STATES], s_col[S_SC], None, ALU.mult), "sdiag_ready")
            for c in range(2):
                dve.wait_ge(sem("scores_ps"), c + 3)
                more(TT(decayed[:, c], decayed[:, c], bank[4 + c][:, :].rearrange("p (h t) -> p h t", h=HEADS),
                        ALU.mult), "decayed_ready")
            empty_tile(14)
            dve.wait_ge(sem("tile_act"), 8)
            dve.wait_ge(sem("tile_dve"), 8)
            sample_columns(2)
            dve.wait_ge(sem("sbc_ps"), 1)
            step(dve.tensor_copy(scol[:, 0, :], bank[6][:, 0:STATES]), "sbc_done")
            dve.wait_ge(sem("scq_parts"), 1)
            step(dve.tensor_reduce(scq, qb, AX.X, ALU.add), "scq_ready")
            dve.wait_ge(sem("tok_ps"), 3)
            step(dve.tensor_copy(vtok[:, 0], bank[2][:, :].rearrange("p (h d) -> p h d", h=HEADS)))
            dve.engine_nop().then_inc(sem("vtok_done"), 1)
            step(TT(vweighted, vtok[:, 0], gcol[:, 4 * ROW_WK:4 * ROW_WK + 4].unsqueeze(2)
                    .to_broadcast([P, HEADS, P]), ALU.mult), "vw_ready")
            dve.wait_ge(sem("srow_ps"), 3)
            step(TS(srow[:, SV, :], bank[6][0:STATES, 2 * HD:3 * HD], s_col[S_DW], None, ALU.mult), "sdiag_ready")

            dve.wait_ge(sem("mem_ps"), 1)
            step(dve.tensor_copy(nstate, bank[3][:, 4:8]))
            step(dve.tensor_copy(den, bank[3][:, 0:4]))
            step(dve.tensor_copy(CT, bank[4][:, :].rearrange("p (h d) -> p h d", h=HEADS)), "ct_ready")
            step(dve.tensor_copy(hout[:, 0], bank[2][:, :].rearrange("p (h t) -> p h t", h=HEADS)), "num_done")
            dve.wait_ge(sem("vtok_done"), 2)
            step(TT(vweighted, vtok[:, 1], gcol[:, 4 * ROW_WK + 4:4 * ROW_WK + 8].unsqueeze(2)
                    .to_broadcast([P, HEADS, P]), ALU.mult), "vw_ready")

            def head(c, num, dsum):
                e0 = 4 * (ROW_EMT + c)
                step(STT(den2, dsum, -1.0, dsum, ALU.mult, ALU.max))
                step(TT(den2, den2, gcol[:, e0:e0 + 4], ALU.max))
                step(dve.reciprocal(den2, den2))
                step(TT(hout[:, c], num, den2.unsqueeze(2).to_broadcast([P, HEADS, P]), ALU.mult))
                for h in range(HEADS):
                    more(dve.bn_stats(h_bn[:, h, :], hout[:, c, h, :]))
                dve.wait_ge(sem("dve_chain"), counts["dve_chain"])
                for h in range(HEADS):
                    more(dve.bn_aggr(h_mv[:, h, :], h_bn[:, h, :]), "h_mv_ready")
                dve.wait_ge(sem("h_mv_ready"), counts["h_mv_ready"])
                step(TT(hout[:, c], hout[:, c], h_mv[:, :, 0:1].to_broadcast([P, HEADS, P]), ALU.subtract))
                dve.wait_ge(sem("h_rstd"), c + 1)
                step(dve.reciprocal(h_rstd, h_rstd))
                step(TT(hout[:, c], hout[:, c], h_rstd.unsqueeze(2).to_broadcast([P, HEADS, P]), ALU.mult),
                     "hn_ready")

            def mix_heads(c):
                dve.wait_ge(sem("hT_ps"), c + 1)
                dve.wait_ge(sem("tile_act"), 12)
                for h in range(HEADS):
                    ins = STT(mixT[:, 4 + h, c * P:(c + 1) * P], bank[6][:, h * P:(h + 1) * P], mhg[:, h:h + 1],
                              proj[:, T_O + h, c * P:(c + 1) * P], ALU.mult, ALU.mult)
                ins.then_inc(sem("hT_done"), 1)

            head(0, hout[:, 0], den)
            dve.wait_ge(sem("sbc_ps"), 2)
            step(dve.tensor_copy(scol[:, 1, :], bank[6][:, STATES:2 * STATES]), "sbc_done")
            dve.wait_ge(sem("mem_ps"), 2)
            sc1 = gcol[:, 4 * ROW_SC:4 * ROW_SC + 4]
            step(TT(hout[:, 1], bank[2][:, :].rearrange("p (h t) -> p h t", h=HEADS),
                    sc1.unsqueeze(2).to_broadcast([P, HEADS, P]), ALU.mult))
            step(TT(hout[:, 1], hout[:, 1], bank[5][:, :].rearrange("p (h t) -> p h t", h=HEADS), ALU.add))
            step(TT(den, bank[3][:, 12:16], sc1, ALU.mult))
            step(TT(den, den, bank[3][:, 8:12], ALU.add), "num_done")
            head(1, hout[:, 1], den)
            mix_heads(0)
            step(TT(CT, CT, dec_b.unsqueeze(2).to_broadcast([P, HEADS, P]), ALU.mult))
            step(TT(CT, CT, bank[4][:, :].rearrange("p (h d) -> p h d", h=HEADS), ALU.add))
            step(TT(nstate, nstate, dec_b, ALU.mult))
            step(TT(nstate, nstate, bank[3][:, 16:20], ALU.add), "ct_ready")
            dve.wait_ge(sem("scq_ps"), 1)
            step(TS(srow[:, SCQ, :], bank[7][0:STATES, 0:P], s_col[S_SC], None, ALU.mult))
            step(STT(srow[:, SY, :], srow[:, SV, :], s_col[S_QK], srow[:, SCQ, :], ALU.mult, ALU.add))
            step(STT(s_col[S_T], s_col[S_DEN], -1.0, s_col[S_DEN], ALU.mult, ALU.max))
            step(TT(s_col[S_T], s_col[S_T], s_col[S_EMT], ALU.max))
            step(dve.reciprocal(s_col[S_R], s_col[S_T]))
            step(TS(srow[:, SY, :], srow[:, SY, :], s_col[S_R], None, ALU.mult))
            step(dve.bn_stats(s_bn, srow[:, SY, :]))
            step(dve.bn_aggr(s_mv, s_bn), "s_mv_ready")
            dve.wait_ge(sem("h_rstd"), 3)
            step(dve.reciprocal(s_col[S_RSTD], s_col[S_RSTD]))
            step(TS(srow[:, SY, :], srow[:, SY, :], s_mv[:, 0:1], s_col[S_RSTD], ALU.subtract, ALU.mult), "sh_ready")
            mix_heads(1)
            dve.wait_ge(sem("scq_ps"), 2)
            for h in range(HEADS):
                ins = STT(mixT[:, 4 + h, SEQ:TOK],
                          bank[7][:, P:P + STATES].rearrange("p (b h) -> p h b", h=HEADS)[:, h, :], mhg[:, h:h + 1],
                          proj[:, T_O + h, SEQ:TOK], ALU.mult, ALU.mult)
            ins.then_inc(sem("shT_done"), 1)

            def layer_norm(i, c, n, name):
                x = xtok[0:n, c, :]
                halves = [slice(0, 512), slice(512, 1024)]
                dve.wait_ge(sem("dve_chain"), counts["dve_chain"])
                step(dve.bn_aggr(ln_mv[0:n, :], ln_bn[0:n, :]), name + "_mv")
                if i == 0:
                    dve.wait_ge(sem(name + "_in"), 32)
                for s in halves:
                    more(STT(x[:, s], x[:, s], ln_mv[0:n, 0:1], lnreg[0:n, s], ALU.subtract, ALU.mult))
                dve.wait_ge(sem(name + "_rstd"), i + 1)
                step(dve.reciprocal(ln_rstd[0:n, :], ln_rstd[0:n, :]))
                for h, s in enumerate(halves):
                    more(STT(x[:, s], x[:, s], ln_rstd[0:n, :], lnreg[0:n, D + 512 * h:D + 512 * h + 512],
                             ALU.mult, ALU.add), name + "_ready")

            def half_stats(n, half, x):
                more(dve.bn_stats(ln_bn[0:n, 6 * half:6 * half + 6], x))

            def route(i):
                c = ORDER[i]
                t0, n = CHUNKS[c]
                dve.wait_ge(sem("logits_ps"), i + 1)
                step(dve.tensor_copy(logits[0:n, :], logits_bank[i][0:n, 0:EXPERTS]))
                step(dve.max(top[0:n, :], logits[0:n, :]))
                more(TS(gsum[0:n, 0:1], top[0:n, 0:1], -1.0, None, ALU.mult), "top_ready")
                step(dve.max_index(idx8[0:n, :], top[0:n, :], logits[0:n, :]))
                step(dve.tensor_copy(idx4[0:n, :], idx8[0:n, 0:TOPK]))
                step(TT(oh4[0:n, c], cst[0:n, C_EXP:C_EXP + EXPERTS].unsqueeze(1).to_broadcast([n, TOPK, EXPERTS]),
                        idx4[0:n, :].unsqueeze(2).to_broadcast([n, TOPK, EXPERTS]), ALU.is_equal))
                step(dve.tensor_reduce(mask[0:n, c, :], oh4[0:n, c].rearrange("p k e -> p e k"), AX.X, ALU.add),
                     "mask_ready")
                dve.wait_ge(sem("top_exp"), i + 1)
                step(dve.tensor_reduce(gsum[0:n, 1:2], gate4[0:n, c, :], AX.X, ALU.add))
                step(dve.reciprocal(gsum[0:n, 2:3], gsum[0:n, 1:2]))
                step(TS(gate4[0:n, c, :], gate4[0:n, c, :], gsum[0:n, 2:3], None, ALU.mult), "gate4_ready")

            dve.wait_ge(sem("x_again"), 48)
            for i, c in enumerate(ORDER):
                n = CHUNKS[c][1]
                if c == 2:
                    dve.wait_ge(sem("mix2_done"), 4)
                    x = xtok[0:n, c, :]
                    step(STT(x, x, ALPHA, mix2, ALU.mult, ALU.add))
                    for half in range(2):
                        half_stats(n, half, x[:, 512 * half:512 * half + 512])
                else:
                    for half in range(2):
                        dve.wait_ge(sem("mix_ps"), (4 if c else 1) + half)
                        b = ((bank[0], bank[1]), (bank[2], bank[5]))[c][half]
                        x = xtok[0:n, c, 512 * half:512 * half + 512]
                        step(STT(x, x, ALPHA, b[0:n, :], ALU.mult, ALU.add))
                        half_stats(n, half, x)
                layer_norm(i, c, n, "ln1")
                if i == 0:
                    step(dve.memset(mask, 0.0))
            route(0)
            route(1)
            step(dve.memset(pos_table, FAR))
            route(2)
            c = ORDER[2]
            step(TT(oh4_last, oh4[:, c], cst[:, C_RANK + TOPK * c:C_RANK + TOPK * c + TOPK].unsqueeze(2)
                    .to_broadcast([P, TOPK, EXPERTS]), ALU.mult))
            step(dve.tensor_reduce(logits, oh4_last.rearrange("p k e -> p e k"), AX.X, ALU.add))
            dve.wait_ge(sem("table_clear"), 1)
            step(dve.tensor_copy(val_table[:, c, 0:PASSES * EXPERTS, 0].rearrange("p (b e) -> p b e", b=PASSES),
                                 logits.unsqueeze(1).to_broadcast([P, PASSES, EXPERTS])))
            dve.wait_ge(sem("pos_ps"), 1)
            step(STT(posm, mask, -FAR, bank[3][:, 0:3 * EXPERTS].rearrange("p (c e) -> p c e", c=3), ALU.mult, ALU.add))
            for c in range(3):
                more(TT(pos_table[:, c, 0:PASSES * EXPERTS].rearrange("p (b e) -> p b e", b=PASSES),
                        posm[:, c, :].unsqueeze(1).to_broadcast([P, PASSES, EXPERTS]),
                        cst[:, C_BLK:C_BLK + PASSES].unsqueeze(2).to_broadcast([P, PASSES, EXPERTS]), ALU.add))

            def one_hot(n, parity):
                TT(onehot, cst[:, C_SLOT:C_SLOT + P].unsqueeze(1).to_broadcast([P, 3, P]),
                   pos_table[:, :, bass.ds(n, 1)].to_broadcast([P, 3, P]), ALU.is_equal).then_inc(sem("onehot_ready"), 1)
                dve.tensor_copy(info, val_table[:, :, bass.ds(n, 1), :].rearrange("p c o v -> p c (o v)"))\
                   .then_inc(sem("onehot_ready"), 1)
                dve.tensor_copy(sel[:, parity, :], cst[0:3 * EXPERTS, bass.ds(n + C_SEL, 1)]
                                .to_broadcast([3 * EXPERTS, BLOCK])).then_inc(sem("onehot_ready"), 1)

            def gathered(n, buffer):
                dve.wait_ge(sem("gathered"), n + 1)
                TS(erow[:, buffer:buffer + 1], bank[5][:, 0:1], 2.0, cst[:, C_HALF:C_HALF + 1], ALU.mult, ALU.add)\
                    .then_inc(sem("xg_done"), 1)
                dve.tensor_copy(egate[:, buffer:buffer + 1], bank[5][:, 1:2]).then_inc(sem("xg_done"), 1)

            def turned(n):
                dve.wait_ge(sem("xgT_ps"), n + 1)
                dve.tensor_copy(xgT, bank[6][:, :].rearrange("p (q h s) -> p q h s", q=4, h=2)).then_inc(sem("xg_done"), 1)

            def expert(n, j):
                dve.wait_ge(sem("gathered"), n + 1)
                dve.wait_ge(sem("out_done"), n + 1)
                one_hot(n + 1, (j + 1) % 2)
                dve.wait_ge(sem("units_used"), n * UNITS + 8)
                hb = [bank[q][:, :].rearrange("p (f two) -> p two f", two=2) for q in range(2)]
                for q in range(2):
                    TS(glu[:, q, :], hb[q][:, 0, :], LIMIT, None, ALU.min).then_inc(sem("glu_ready"), 1)
                for q in range(2):
                    TS(lin[:, q, :], hb[q][:, 1, :], LIMIT, -LIMIT, ALU.min, ALU.max).then_inc(sem("lin_ready"), 1)
                dve.wait_ge(sem("lin_ready"), (n + 1) * 2)
                dve.wait_ge(sem("glu_ready"), (n + 1) * 2)
                STT(lin, lin, 1.0, glu, ALU.add, ALU.mult).then_inc(sem("h_read"), 1)
                dve.wait_ge(sem("h_read"), n + 2)
                dve.wait_ge(sem("sig_ready"), n + 1)
                TT(act_out.rearrange("p (q f) -> p q f", q=2), lin, sig, ALU.mult).then_inc(sem("act_ready"), 1)
                dve.wait_ge(sem("rows_left"), n + 2)
                gathered(n + 1, (j + 1) % BUFFERS)
                turned(n + 1)

            dve.wait_ge(sem("dve_chain"), counts["dve_chain"])
            dve.engine_nop().then_inc(sem("h_read"), 1)
            dve.wait_ge(sem("values_ready"), 1)
            one_hot(0, 0)
            step(dve.tensor_reduce(gsum[:, 0:1], bank[3][:, 3 * EXPERTS:4 * EXPERTS], AX.X, ALU.max))
            step(TS(idx4, cst[:, C_LIM:C_LIM + 4], gsum[:, 0:1], None, ALU.is_lt))
            step(dve.tensor_reduce(gsum[:, 1:2], idx4, AX.X, ALU.add))
            step(dve.tensor_copy(extra[:, :], gsum[:, 1:2]), "passes_ready")
            gathered(0, 0)
            turned(0)
            dve.wait_ge(sem("passes_ready"), 1)
            npass = dve.value_load(extra[0:1, 0:1], min_val=0, max_val=PASSES - 1) + 1
            with dve.Fori(0, npass * EXPERTS, STEP) as n:
                for j in range(STEP):
                    expert(n + j, j)

            pT = ring[:, 9, 768:768 + 2 * TOK].rearrange("p (k n) -> p k n", k=2)
            for c, (t0, n) in enumerate(CHUNKS):
                dve.wait_ge(sem("pT_ps"), c + 1)
                dve.tensor_copy(pT[:, :, t0:t0 + n], bank[c][:, 0:2 * P].rearrange("p (k t) -> p k t", k=2)[:, :, 0:n])\
                   .then_inc(sem("pT_done"), 1)
            for i, c in enumerate(LAST_ORDER):
                n = CHUNKS[c][1]
                f = ff_sum(c)[0:n]
                dve.wait_ge(sem(f"ff_in0{c}"), 16)
                step(STT(xtok[0:n, c, :], xtok[0:n, c, :], ALPHA, f[:, 0, :], ALU.mult, ALU.add))
                step(TT(xtok[0:n, c, :], xtok[0:n, c, :], f[:, 1, :], ALU.add))
                dve.wait_ge(sem(f"ff_in1{c}"), 16)
                step(TT(xtok[0:n, c, :], xtok[0:n, c, :], f[:, 2, :], ALU.add))
                for half in range(2):
                    x = xtok[0:n, c, 512 * half:512 * half + 512]
                    step(TT(x, x, f[:, 3, 512 * half:512 * half + 512], ALU.add))
                    half_stats(n, half, x)
                layer_norm(i, c, n, "ln2")
            for i, c in enumerate(LAST_ORDER):
                n = CHUNKS[c][1]
                for half in range(2):
                    s = slice(512 * half, 512 * half + 512)
                    gate = ff_sum(c)[0:n, 0, s]
                    dve.wait_ge(sem("sig_done"), (half + 1, 6, half + 7)[i])
                    dve.wait_ge(sem("ple_done"), 2 * i + 2)
                    dve.wait_ge(sem("x2T_ps"), 2 * i + 2)
                    step(TT(gate, gate, ring[0:n, c, s], ALU.mult))
                    step(TT(xtok[0:n, c, s], xtok[0:n, c, s], gate, ALU.add), "y_done")

        @block.scalar
        def _(act):
            act.dma_start(cst[:, :], consts).then_inc(sem("cst_in"), 16)
            act.dma_start(wgate[:, :, :], w_in[0, :, 2560:2568].rearrange("(k p) n -> p k n", p=P))\
               .then_inc(sem("gate_in"), 16)
            act.dma_start(gbias[0:HEADS, :], b_i.rearrange("o h -> h o")).then_inc(sem("gate_in"), 16)
            act.dma_start(gbias[HEADS:2 * HEADS, :], b_f.rearrange("o h -> h o")).then_inc(sem("gate_in"), 16)

            act.dma_start(hist[0:SAMPLES * HIST, :], state_pool[0].rearrange("b r d -> (b r) d"))\
               .then_inc(sem("hist_in"), 16)

            for g in (1, 3, 5):
                c = g // 2
                t0, n = CHUNKS[c]
                act.wait_ge(sem("xT_ps"), g + 1)
                act.copy(xT[:, 4:8, t0:t0 + n], bank[g][:, :].rearrange("p (k t) -> p k t", k=4)[:, :, 0:n])\
                   .then_inc(sem("xT_act"), 1)
            act.wait_ge(sem("gates_ps"), 1)
            act.wait_ge(sem("gate_in"), 48)
            act.activation(gates[:, :], bank[6][0:2 * HEADS, 0:TOK], ACT.Identity, bias=gbias).then_inc(sem("gates_done"), 1)
            act.dma_start(srow[:, SN, :], state_n[0].rearrange("b h k -> (b h) k")).then_inc(sem("states_in"), 16)
            act.dma_start(s_col[S_M0], state_m.rearrange("o b h -> (b h) o")).then_inc(sem("states_in"), 16)
            act.dma_start(wpool[:, :, :], w_pool[0].rearrange("g c d -> c g d")).then_inc(sem("pool_in"), 16)
            act.dma_start(pscale, pool_scale[0].rearrange("(g d) -> d g", d=P)).then_inc(sem("pool_in"), 16)
            act.dma_start(mhg, mh_g[0].rearrange("(g d) -> d g", d=P)).then_inc(sem("pool_in"), 16)
            act.dma_start(wrout[:, :, :], w_router[0].rearrange("(k p) e -> p k e", p=P)).then_inc(sem("wrout_in"), 16)
            act.dma_start(brout[:, :], b_router).then_inc(sem("wrout_in"), 16)

            def empty_tile(t):
                act.wait_ge(sem("tile_ps"), t + 1)
                if t >= 16:
                    ins = act.activation(proj[:, t, :], bank[t % 2][:, 0:TOK], ACT.Sigmoid)
                elif T_K <= t < T_V:
                    ins = act.activation(proj[:, t, :], bank[t % 2][:, 0:TOK], ACT.Copy, scale=K_SCALE)
                else:
                    ins = act.copy(proj[:, t, :], bank[t % 2][:, 0:TOK])
                ins.then_inc(sem("tile_act"), 1)

            one = ones[0:HEADS, 0:1]
            act.wait_ge(sem("soft_ready"), 1)
            act.activation(softp, softp, ACT.Exp).then_inc(sem("soft_exp"), 1)
            empty_tile(1)
            act.wait_ge(sem("soft_exp"), 1)
            act.activation(softp, softp, ACT.Ln, bias=one).then_inc(sem("soft_done"), 1)
            empty_tile(3)
            act.wait_ge(sem("runmax_ready"), 2)
            act.activation(rows[:, ROW_EMT:ROW_EMT + 2, :], rows[:, ROW_EMT:ROW_EMT + 2, :], ACT.Exp, scale=-1.0)\
               .then_inc(sem("rows_parts"), 1)
            for c in range(2):
                act.activation(rows[:, ROW_WK + c, :], rows[:, ROW_G + c, :], ACT.Exp, bias=nlast[:, c:c + 1])\
                   .then_inc(sem("rows_parts"), 1)
            act.activation(rows[:, ROW_SC, :], runmax[:, P:2 * P], ACT.Exp, bias=m1, scale=-1.0).then_inc(sem("rows_parts"), 1)
            empty_tile(5)

            def bias_part(part_):
                r = slice(0, (3 - part_) * EXPERTS)
                act.copy(bias_parts[r, :], bsrc[r, :]).then_inc(sem("bias_cast"), 1)

            act.wait_ge(sem("bias_in"), 96)
            bias_part(0)
            act.wait_ge(sem("soft_ready"), 2)
            act.activation(s_col[S_T], s_col[S_T], ACT.Exp).then_inc(sem("soft_exp"), 1)
            for c in range(2):
                act.wait_ge(sem("lag_ready"), 4 * (c + 1))
                act.activation(decayed[:, c], decayed[:, c], ACT.Exp, scale=-1.0).then_inc(sem("decay_act"), 1)
            empty_tile(7)
            act.wait_ge(sem("soft_exp"), 2)
            act.activation(s_col[S_T], s_col[S_T], ACT.Ln, bias=ones[0:STATES, 0:1]).then_inc(sem("soft_done"), 1)
            act.wait_ge(sem("bias_rest"), 1)
            bias_part(1)
            empty_tile(9)
            act.wait_ge(sem("s_m_ready"), 1)
            for src, dst in ((s_gate[:, 0:1], S_DW), (s_col[S_INTER], S_SC)):
                act.activation(s_col[dst], src, ACT.Exp, bias=s_col[S_NM]).then_inc(sem("s_exp_done"), 1)
            act.activation(s_col[S_EMT], s_col[S_M], ACT.Exp, scale=-1.0).then_inc(sem("s_exp_done"), 1)
            act.wait_ge(sem("bias_rest"), 2)
            bias_part(2)
            empty_tile(11)
            act.wait_ge(sem("tok_ps"), 2)
            act.copy(ktok[:, 1], bank[5][:, :].rearrange("p (h d) -> p h d", h=HEADS)).then_inc(sem("ktok_done"), 1)

            def pool_group(g):
                act.wait_ge(sem("pool_ps"), g + 1)
                if g == 0:
                    act.wait_ge(sem("pool_in"), 48)
                act.activation(mixT[:, g, :], bank[7][:, 0:TOK], ACT.Copy, scale=pscale[:, g:g + 1])\
                   .then_inc(sem("pool_done"), 1)

            def root(out_, in_, name):
                act.activation(out_, in_, ACT.Sqrt, bias=eps[0:in_.shape[0], :]).then_inc(sem(name), 1)

            empty_tile(13)
            pool_group(0)
            pool_group(1)
            empty_tile(15)
            pool_group(2)
            empty_tile(16)
            act.wait_ge(sem("tok_ps"), 4)
            act.copy(vtok[:, 1], bank[3][:, :].rearrange("p (h d) -> p h d", h=HEADS)).then_inc(sem("vtok_done"), 1)
            pool_group(3)
            empty_tile(17)
            empty_tile(18)
            act.wait_ge(sem("h_mv_ready"), 4)
            root(h_rstd, h_mv[:, :, 1], "h_rstd")
            empty_tile(19)
            act.wait_ge(sem("cfin_ps"), 1)
            act.copy(urow[:, :], bank[7][0:HIST + SAMPLES, :]).then_inc(sem("cfin_done"), 1)
            act.wait_ge(sem("h_mv_ready"), 8)
            act.wait_ge(sem("hn_ready"), 1)
            root(h_rstd, h_mv[:, :, 1], "h_rstd")
            act.wait_ge(sem("s_mv_ready"), 1)
            root(s_col[S_RSTD], s_mv[:, 1:2], "h_rstd")
            act.wait_ge(sem("cfin_ps"), 2)
            act.copy(ncol_out[:, :], bank[3][0:HEADS, 0:P]).then_inc(sem("cfin_done"), 1)
            act.copy(Cfin, bank[4][:, :].rearrange("p (h d) -> p h d", h=HEADS)).then_inc(sem("cfin_done"), 1)

            def ln_root(i, c, name):
                n = CHUNKS[c][1]
                act.wait_ge(sem(name + "_mv"), i + 1)
                if i:
                    act.wait_ge(sem(name + "_ready"), 2 * i)
                root(ln_rstd[0:n, :], ln_mv[0:n, 1:2], name + "_rstd")

            def turned(i, c, name):
                t0, n = CHUNKS[c]
                for half in range(2):
                    act.wait_ge(sem(name + "_ps"), 2 * i + half + 1)
                    act.copy(x1T[:, 4 * half:4 * half + 4, t0:t0 + n],
                             bank[6 + half][:, :].rearrange("p (k t) -> p k t", k=4)[:, :, 0:n])\
                       .then_inc(sem(name + "_done"), 1)

            def top_exp(i):
                n = CHUNKS[ORDER[i]][1]
                act.wait_ge(sem("top_ready"), i + 1)
                act.activation(gate4[0:n, ORDER[i], :], top[0:n, 0:TOPK], ACT.Exp, bias=gsum[0:n, 0:1]).then_inc(sem("top_exp"), 1)

            ln_root(0, 0, "ln1")
            act.wait_ge(sem("mix_ps"), 3)
            for q in range(4):
                act.copy(mix2[:, 256 * q:256 * q + 256], bank[3][32 * q:32 * q + SAMPLES, 0:256])\
                   .then_inc(sem("mix2_done"), 1)
            ln_root(1, 2, "ln1")
            turned(0, ORDER[0], "x1T")
            ln_root(2, 1, "ln1")
            turned(1, ORDER[1], "x1T")
            top_exp(0)
            turned(2, ORDER[2], "x1T")
            top_exp(1)
            top_exp(2)

            def expert(n, j):
                act.wait_ge(sem("glu_ready"), n * 2 + 2)
                act.activation(sig, glu, ACT.Sigmoid, scale=SIG).then_inc(sem("sig_ready"), 1)
                act.wait_ge(sem("gathered"), n + 2)
                act.copy(hist_mix[:, 0:512], bank[2][:, :]).then_inc(sem("xg_copied"), 1)
                act.wait_ge(sem("aT_ps"), n + 1)
                act.copy(aT, bank[3][:, :].rearrange("p (m s) -> p m s", m=4)).then_inc(sem("aT_done"), 1)
                act.wait_ge(sem("units_used"), n * UNITS + UNITS)
                act.wait_ge(sem("rows_left"), n + 1)
                act.activation(eout[:, j, :], bank[4][:, :], ACT.Copy, scale=egate[:, j:j + 1])\
                   .then_inc(sem("out_done"), 1)

            act.wait_ge(sem("gathered"), 1)
            act.copy(hist_mix[:, 0:512], bank[2][:, :]).then_inc(sem("xg_copied"), 1)
            act.nop().then_inc(sem("out_done"), 1)
            act.wait_ge(sem("passes_ready"), 1)
            npass = act.value_load(extra[0:1, 0:1], min_val=0, max_val=PASSES - 1) + 1
            with act.Fori(0, npass * EXPERTS, STEP) as n:
                for j in range(STEP):
                    expert(n + j, j)

            def embedded(i):
                c = LAST_ORDER[i]
                n = CHUNKS[c][1]
                for half in range(2):
                    act.wait_ge(sem("ple_ps"), 2 * i + half + 1)
                    act.copy(ring[0:n, c, 512 * half:512 * half + 512], bank[4 + half][0:n, :])\
                       .then_inc(sem("ple_done"), 1)

            embedded(0)
            embedded(1)
            embedded(2)
            for i, c in enumerate(LAST_ORDER):
                ln_root(i, c, "ln2")
                turned(i, c, "x2T")

            def opened(i, half):
                c = LAST_ORDER[i]
                act.wait_ge(sem("gate_ps"), 2 * i + half + 1)
                act.activation(ff_sum(c)[:, 0, 512 * half:512 * half + 512], bank[2 * c + half][:, :], ACT.Sigmoid)\
                   .then_inc(sem("sig_done"), 1)

            opened(0, 0)
            opened(0, 1)
            act.wait_ge(sem("gate_ps"), 4)
            for q in range(4):
                act.activation(ff_sum(2)[0:SAMPLES, 0, 256 * q:256 * q + 256], bank[4][32 * q:32 * q + SAMPLES, 0:256],
                               ACT.Sigmoid).then_inc(sem("sig_done"), 1)
            opened(2, 0)
            opened(2, 1)

        @block.gpsimd
        def _(pool):
            chain = [0]

            def step(ins):
                chain[0] += 1
                ins.then_inc(sem("pool_chain"), 1)
                pool.wait_ge(sem("pool_chain"), chain[0])

            step(pool.memset(window[:, :, 0:16], 0.0))
            for g, w in enumerate(WINDOWS):
                u = proj[:, T_U + g, :]
                name, count = tile_done(T_U + g)
                pool.wait_ge(sem(name), count)
                step(pool.tensor_copy(window[:, 0, 16:], u[:, 0:SEQ]))
                src, shift = 0, 1
                while shift < w:
                    step(pool.tensor_tensor(window[:, 1 - src, 16:], window[:, src, 16:],
                                            window[:, src, 16 - shift:16 + SEQ - shift], ALU.add))
                    src, shift = 1 - src, 2 * shift
                first = window[:, src, 16:32]
                step(pool.tensor_tensor(first, first, cst[:, C_CNT + 16 * g:C_CNT + 16 * g + 16], ALU.mult))
                if g == 0:
                    pool.wait_ge(sem("hist_done"), 1)
                hs = histsum[:, g * SAMPLES:(g + 1) * SAMPLES]
                step(pool.tensor_tensor(hs, hs, u[:, SEQ:TOK], ALU.add))
                step(pool.tensor_scalar(hs, hs, 1.0 / w, None, ALU.mult))
                step(pool.tensor_scalar(window[:, src, 16:], window[:, src, 16:], 1.0 / w, None, ALU.mult))
                step(pool.tensor_copy(ukeep[:, g, 0:HIST], u[:, SEQ - HIST:SEQ]))
                step(pool.tensor_copy(ukeep[:, g, HIST:HIST + SAMPLES], u[:, SEQ:TOK]))
                step(pool.tensor_tensor(u[:, SEQ:TOK], hs, u[:, SEQ:TOK], ALU.subtract))
                step(pool.tensor_tensor(u[:, 0:SEQ], window[:, src, 16:], u[:, 0:SEQ], ALU.subtract))
                pool.engine_nop().then_inc(sem("z_ready"), 1)

            pool.wait_ge(sem("cq_in"), 32)
            step(pool.tensor_tensor(qb, qb, Cst, ALU.mult))
            pool.engine_nop().then_inc(sem("scq_parts"), 1)
            pool.wait_ge(sem("sbc_done"), 1)
            step(pool.tensor_tensor(Cst, Cst, scol[:, 0, :].unsqueeze(2).to_broadcast([P, STATES, HD]), ALU.mult))
            pool.wait_ge(sem("sbc_done"), 2)
            pool.wait_ge(sem("kb_in"), 16)
            step(pool.tensor_tensor(kb, kb, scol[:, 1, :].unsqueeze(2).to_broadcast([P, STATES, HD]), ALU.mult))
            step(pool.tensor_tensor(Cst, Cst, kb, ALU.add))
            pool.engine_nop().then_inc(sem("Cnew_done"), 1)
            pool.dma_start(C_sample[0].rearrange("b h v k -> v (b h) k"), Cst).then_inc(sem("C_out"), 16)
            pool.wait_ge(sem("cfin_done"), 3)
            pool.dma_start(pool_sample[0, :, HIST - 1, :], urow[HIST:HIST + SAMPLES, :]).then_inc(sem("small_out"), 16)
            pool.dma_start(C_prompt[0, 0].rearrange("h v k -> v h k"), Cfin).then_inc(sem("small_out"), 16)
            pool.dma_start(n_prompt[0, 0], ncol_out[:, :]).then_inc(sem("small_out"), 16)
            pool.dma_start(m_prompt[0].rearrange("b h -> h b"), m2).then_inc(sem("small_out"), 16)
            pool.wait_ge(sem("sn_ready"), 1)
            pool.dma_start(n_sample[0].rearrange("b h k -> (b h) k"), srow[:, SN, :]).then_inc(sem("rows_out0"), 16)
            pool.dma_start(m_sample.rearrange("o b h -> (b h) o"), s_col[S_M]).then_inc(sem("rows_out1"), 16)
            pool.dma_start(pool_sample[0, :, 0:HIST - 1, :], state_pool[0, :, 1:HIST, :]).then_inc(sem("rows_out2"), 16)
            pool.dma_start(pool_prompt[0, 0], urow[0:HIST, :]).then_inc(sem("rows_out3"), 16)
            step(pool.memset(val_table, 0.0))
            pool.engine_nop().then_inc(sem("table_clear"), 1)
            for i, c in enumerate(ORDER):
                n = CHUNKS[c][1]
                table = val_table[0:n, c, 0:PASSES * EXPERTS, :].rearrange("p (b e) v -> p v b e", b=PASSES)
                for v in range(1 if i == 2 else 0, 2):
                    pool.wait_ge(sem("gate4_ready" if v else "mask_ready"), i + 1)
                    factor = gate4[0:n, c, :] if v else cst[0:n, C_RANK + TOPK * c:C_RANK + TOPK * c + TOPK]
                    step(pool.tensor_tensor(oh4v[0:n], oh4[0:n, c], factor.unsqueeze(2).to_broadcast([n, TOPK, EXPERTS]),
                                            ALU.mult))
                    step(pool.tensor_tensor(oh4v[0:n, 0:2], oh4v[0:n, 0:2], oh4v[0:n, 2:4], ALU.add))
                    step(pool.tensor_tensor(vrow[0:n, v, :], oh4v[0:n, 0], oh4v[0:n, 1], ALU.add))
                    step(pool.tensor_copy(table[:, v], vrow[0:n, v, :].unsqueeze(1).to_broadcast([n, PASSES, EXPERTS])))
            pool.engine_nop().then_inc(sem("values_ready"), 1)
            pool.wait_ge(sem("ln1_ready"), 6)
            pool.dma_start(lnreg[:, 0:D], ln2_g.partition_broadcast(P).rearrange("p o d -> p (o d)"))\
                .then_inc(sem("ln2_in"), 16)
            pool.dma_start(lnreg[:, D:2 * D], ln2_b.partition_broadcast(P).rearrange("p o d -> p (o d)"))\
                .then_inc(sem("ln2_in"), 16)

            def expert(n, j):
                pool.wait_ge(sem("out_done"), n + 2)
                pool.wait_ge(sem("xg_done"), n * 3 + 6)
                pool.sem_inc(sem("scatters"), 1)
                pool.indirect_dma_start(out=ff_rows, out_offset=bass.IndirectOffsetOnAxis(
                    ap=erow[:, j:j + 1], axis=0), in_=eout[:, j, :], in_offset=None,
                    bounds_check=last_row, oob_is_err=False).then_inc(sem(f"rows_out{j}"), 16)
                k = (j - 2) % BUFFERS
                pool.wait_ge(sem(f"rows_out{k}"), (n - j) * (16 // STEP) + (32 if j >= 2 else 16))
                pool.sem_inc(sem("rows_left"), 1)

            for _ in range(2):
                pool.engine_nop().then_inc(sem("rows_left"), 1)
            pool.wait_ge(sem("passes_ready"), 1)
            last_row = pool.alloc_register("last_row")
            pool.reg_mov(last_row, TOK * TOPK * 2 - 1)
            npass = pool.value_load(extra[0:1, 0:1], min_val=0, max_val=PASSES - 1) + 1
            with pool.Fori(0, npass * EXPERTS, STEP) as n:
                for j in range(STEP):
                    expert(n + j, j)


INPUTS = ["x_prompt", "x_sample", "state_pool", "state_mlstm_C", "state_mlstm_n", "state_mlstm_m", "p_prompt",
          "p_sample", "w_in", "b_i", "b_f", "w_pool", "pool_scale", "mh_g", "w_out", "ln1_g", "ln1_b", "w_router",
          "b_router", "w_mlp1", "b_mlp1", "w_mlp2", "b_mlp2", "ln2_g", "ln2_b", "w_ple", "w_ple_gate"]
OUTPUTS = [(1, SEQ, D), (SAMPLES, 1, D), (1, 1, HIST, 4 * P), (1, 1, HEADS, HD, HD), (1, 1, HEADS, HD), (1, 1, HEADS),
           (1, SAMPLES, HIST, 4 * P), (1, SAMPLES, HEADS, HD, HD), (1, SAMPLES, HEADS, HD), (1, SAMPLES, HEADS)]


def kernel(**inputs):
    import concourse.bacc as bacc
    from concourse.bass_utils import run_bass_kernel_spmd

    nc = bacc.Bacc("TRN2", target_bir_lowering=False, num_devices=1, dynamic_dma_scratch_size=8192)
    arrays = {"in_consts": constants()}
    for name in INPUTS:
        arrays[f"in_{name}"] = np.ascontiguousarray(inputs[name])
    args = [nc.dram_tensor(name, a.shape, mybir.dt.from_np(a.dtype), kind="ExternalInput").ap()
            for name, a in arrays.items()]
    args += [nc.dram_tensor(f"out_{i}", shape, F32, kind="ExternalOutput").ap() for i, shape in enumerate(OUTPUTS)]
    build(nc, *args)
    r = run_bass_kernel_spmd(nc, [arrays], core_ids=[0])
    return tuple(r.results[0][f"out_{i}"] for i in range(len(OUTPUTS)))
```
